# Optimizing a Trainium2 kernel written in Bass

```python
import math
import jax, jax.numpy as jnp
from jax import lax
import numpy as np

D_MODEL = 1024
BATCH = 1
SEQ = 1024
DEPTH = 1

N_MEM = 256
XATTN_HEADS = 4
XATTN_HEAD_DIM = D_MODEL // XATTN_HEADS

D_MIX = D_MODEL
D_GLA = D_MIX // 2
D_LRU = D_MIX - D_GLA

GLA_HEADS = 4
GLA_DK_TOTAL = D_GLA // 2
GLA_DK = GLA_DK_TOTAL // GLA_HEADS
GLA_DV = D_GLA // GLA_HEADS
GLA_LOWRANK = 16
GLA_GATE_NORMALIZER = 16.0
GLA_CHUNK = 64

LRU_HEADS = 8
LRU_BLOCK = D_LRU // LRU_HEADS
LRU_CONV_W = 4
LRU_C = 8.0

D_FF = 2816
FFN_CONV_W = 3

EPS = 1e-6

IN_SPLITS = (GLA_DK_TOTAL, GLA_DK_TOTAL, D_GLA, D_GLA, GLA_LOWRANK, D_LRU, D_LRU)
D_IN = sum(IN_SPLITS)

kernel_name = "hybrid_gla_rglru_xattn_convffn"

def _rmsnorm(x, g):
    xf = x.astype(jnp.float32)
    y = xf * lax.rsqrt(jnp.mean(xf * xf, axis=-1, keepdims=True) + EPS)
    return (y * g.astype(jnp.float32)).astype(x.dtype)

def _causal_dwconv(x, w, b):
    width, ch = w.shape
    y = lax.conv_general_dilated(
        x, w[:, None, :].astype(x.dtype), window_strides=(1,), padding=[(width - 1, 0)],
        dimension_numbers=("NWC", "WIO", "NWC"), feature_group_count=ch)
    return y + b.astype(x.dtype)

def _gla_chunk_step(state, inp):
    q, k, v, g = inp
    c = q.shape[2]
    b = jnp.cumsum(g, axis=2)
    inter = jnp.einsum('bhcd,bhde->bhce', q * jnp.exp(b), state)
    diff = b[:, :, :, None, :] - b[:, :, None, :, :]
    causal = jnp.tril(jnp.ones((c, c), dtype=bool))[:, :, None]
    decay = jnp.exp(jnp.where(causal, diff, -jnp.inf))
    scores = jnp.einsum('bhid,bhjd,bhijd->bhij', q, k, decay)
    intra = jnp.einsum('bhij,bhje->bhie', scores, v)
    b_last = b[:, :, -1, :]
    k_dec = k * jnp.exp(b_last[:, :, None, :] - b)
    state = jnp.exp(b_last)[..., None] * state + jnp.einsum('bhjd,bhje->bhde', k_dec, v)
    return state, inter + intra

def _gla(q, k, v, glog):
    bsz, s, h, dk = q.shape
    dv = v.shape[-1]
    n = s // GLA_CHUNK

    def to_chunks(t):
        return t.astype(jnp.float32).reshape(bsz, n, GLA_CHUNK, h, t.shape[-1]).transpose(1, 0, 3, 2, 4)

    state0 = jnp.zeros((bsz, h, dk, dv), jnp.float32)
    _, ys = lax.scan(_gla_chunk_step, state0,
                     (to_chunks(q), to_chunks(k), to_chunks(v), to_chunks(glog)))
    return ys.transpose(1, 0, 3, 2, 4).reshape(bsz, s, h, dv)

def _rglru(xc, w_a, b_a, w_x, b_x, lam):
    bsz, s, _ = xc.shape
    xf = xc.astype(jnp.float32)
    xb = xf.reshape(bsz, s, LRU_HEADS, LRU_BLOCK)
    r = jax.nn.sigmoid(jnp.einsum('bshi,hij->bshj', xb, w_a.astype(jnp.float32)).reshape(bsz, s, D_LRU) + b_a)
    i = jax.nn.sigmoid(jnp.einsum('bshi,hij->bshj', xb, w_x.astype(jnp.float32)).reshape(bsz, s, D_LRU) + b_x)
    log_a = -LRU_C * r * jax.nn.softplus(-lam.astype(jnp.float32))
    a = jnp.exp(log_a)
    mult = jnp.sqrt(-jnp.expm1(2.0 * log_a))
    mult = jnp.where(jnp.arange(s)[None, :, None] == 0, 1.0, mult)
    bterm = mult * (i * xf)

    def combine(lhs, rhs):
        a1, b1 = lhs
        a2, b2 = rhs
        return a1 * a2, a2 * b1 + b2

    _, hseq = lax.associative_scan(combine, (a, bterm), axis=1)
    return hseq

def setup_inputs(seed: int = 0) -> dict:
    key = jax.random.key(seed)
    ks = jax.random.split(key, 32)
    L = DEPTH

    def nrm(k, shape, fan_in):
        return jax.random.normal(k, shape, jnp.float32) * (fan_in ** -0.5)

    def gain(k, shape):
        return 1.0 + 0.02 * jax.random.normal(k, shape, jnp.float32)

    def small(k, shape):
        return 0.01 * jax.random.normal(k, shape, jnp.float32)

    a0 = jax.random.uniform(ks[10], (L, D_LRU), jnp.float32, 0.9, 0.999)
    lru_lambda = jnp.log(a0) - jnp.log1p(-a0)

    return {
        "x": jax.random.normal(ks[0], (BATCH, SEQ, D_MODEL), jnp.float32),
        "mem": jax.random.normal(ks[1], (BATCH, N_MEM, D_MODEL), jnp.float32),
        "g_mix": gain(ks[2], (L, D_MODEL)),
        "w_in": nrm(ks[3], (L, D_MODEL, D_IN), D_MODEL),
        "w_gk": nrm(ks[4], (L, GLA_LOWRANK, GLA_DK_TOTAL), GLA_LOWRANK),
        "b_gk": small(ks[5], (L, GLA_DK_TOTAL)),
        "g_gla_head": gain(ks[6], (L, GLA_DV)),
        "conv_lru_w": nrm(ks[7], (L, LRU_CONV_W, D_LRU), LRU_CONV_W),
        "conv_lru_b": small(ks[8], (L, D_LRU)),
        "w_rg_a": nrm(ks[9], (L, LRU_HEADS, LRU_BLOCK, LRU_BLOCK), LRU_BLOCK),
        "b_rg_a": small(ks[11], (L, D_LRU)),
        "w_rg_x": nrm(ks[12], (L, LRU_HEADS, LRU_BLOCK, LRU_BLOCK), LRU_BLOCK),
        "b_rg_x": small(ks[13], (L, D_LRU)),
        "lru_lambda": lru_lambda,
        "w_mix_out": nrm(ks[14], (L, D_MIX, D_MODEL), D_MIX),
        "g_xattn": gain(ks[15], (L, D_MODEL)),
        "g_mem": gain(ks[16], (L, D_MODEL)),
        "w_xq": nrm(ks[17], (L, D_MODEL, D_MODEL), D_MODEL),
        "w_xkv": nrm(ks[18], (L, D_MODEL, 2 * D_MODEL), D_MODEL),
        "w_xo": nrm(ks[19], (L, D_MODEL, D_MODEL), D_MODEL),
        "g_ffn": gain(ks[20], (L, D_MODEL)),
        "w_ffn_in": nrm(ks[21], (L, D_MODEL, 2 * D_FF), D_MODEL),
        "conv_ffn_w": nrm(ks[22], (L, FFN_CONV_W, D_FF), FFN_CONV_W),
        "conv_ffn_b": small(ks[23], (L, D_FF)),
        "w_ffn_out": nrm(ks[24], (L, D_FF, D_MODEL), D_FF),
        "g_final": gain(ks[25], (D_MODEL,)),
    }

def reference(x, mem, g_mix, w_in, w_gk, b_gk, g_gla_head, conv_lru_w, conv_lru_b,
              w_rg_a, b_rg_a, w_rg_x, b_rg_x, lru_lambda, w_mix_out,
              g_xattn, g_mem, w_xq, w_xkv, w_xo,
              g_ffn, w_ffn_in, conv_ffn_w, conv_ffn_b, w_ffn_out, g_final):
    bsz, s, d = x.shape
    offsets = np.cumsum(IN_SPLITS)[:-1].tolist()

    for l in range(DEPTH):
        h = _rmsnorm(x, g_mix[l])
        u = h @ w_in[l]
        q, k, v, og, gk_lr, xr, xg = jnp.split(u, offsets, axis=-1)

        glog = jax.nn.log_sigmoid((gk_lr.astype(jnp.float32) @ w_gk[l].astype(jnp.float32)) + b_gk[l]) / GLA_GATE_NORMALIZER
        qh = q.reshape(bsz, s, GLA_HEADS, GLA_DK) * (GLA_DK ** -0.5)
        kh = k.reshape(bsz, s, GLA_HEADS, GLA_DK)
        vh = v.reshape(bsz, s, GLA_HEADS, GLA_DV)
        gh = glog.reshape(bsz, s, GLA_HEADS, GLA_DK)
        o = _gla(qh, kh, vh, gh)
        o = o * lax.rsqrt(jnp.mean(o * o, axis=-1, keepdims=True) + EPS) * g_gla_head[l].astype(jnp.float32)
        y_gla = o.reshape(bsz, s, D_GLA) * jax.nn.silu(og.astype(jnp.float32))

        xc = _causal_dwconv(xr, conv_lru_w[l], conv_lru_b[l])
        hr = _rglru(xc, w_rg_a[l], b_rg_a[l], w_rg_x[l], b_rg_x[l], lru_lambda[l])
        y_lru = hr * jax.nn.gelu(xg.astype(jnp.float32), approximate=True)

        y_mix = jnp.concatenate([y_gla, y_lru], axis=-1).astype(x.dtype)
        x = x + y_mix @ w_mix_out[l]

        hq = _rmsnorm(x, g_xattn[l])
        hm = _rmsnorm(mem, g_mem[l])
        xq = (hq @ w_xq[l]).reshape(bsz, s, XATTN_HEADS, XATTN_HEAD_DIM)
        xk, xv = jnp.split(hm @ w_xkv[l], 2, axis=-1)
        xk = xk.reshape(bsz, N_MEM, XATTN_HEADS, XATTN_HEAD_DIM)
        xv = xv.reshape(bsz, N_MEM, XATTN_HEADS, XATTN_HEAD_DIM)
        sc = jnp.einsum('bshd,bmhd->bhsm', xq.astype(jnp.float32), xk.astype(jnp.float32)) * (XATTN_HEAD_DIM ** -0.5)
        p = jax.nn.softmax(sc, axis=-1)
        att = jnp.einsum('bhsm,bmhd->bshd', p, xv.astype(jnp.float32)).reshape(bsz, s, D_MODEL)
        x = x + att.astype(x.dtype) @ w_xo[l]

        hf = _rmsnorm(x, g_ffn[l])
        gate, up = jnp.split(hf @ w_ffn_in[l], 2, axis=-1)
        gate = _causal_dwconv(gate, conv_ffn_w[l], conv_ffn_b[l])
        f = (jax.nn.silu(gate.astype(jnp.float32)) * up.astype(jnp.float32)).astype(x.dtype)
        x = x + f @ w_ffn_out[l]

    return _rmsnorm(x, g_final)


_drawn_inputs = setup_inputs


def setup_inputs(seed=0):
    import zlib

    import numpy as np

    out = dict(_drawn_inputs(seed))
    spreads = {}
    factors = {'g_mix': 2.91,
     'b_gk': 8.0,
     'g_gla_head': 6.389,
     'conv_lru_b': 5.381,
     'b_rg_a': 8.0,
     'b_rg_x': 8.0,
     'g_xattn': 8.0,
     'g_mem': 8.0,
     'g_ffn': 12.292,
     'conv_ffn_b': 34.136,
     'g_final': 7.862}
    for name, (base, spread) in spreads.items():
        noise = np.random.default_rng([zlib.crc32(name.encode()), seed]).standard_normal(out[name].shape)
        drawn = base * np.exp(spread * noise) if base else spread * noise
        out[name] = __import__('jax').numpy.asarray(drawn.astype(out[name].dtype))
    for name, factor in factors.items():
        out[name] = (out[name] * factor).astype(out[name].dtype)
    return out
```

```python
from contextlib import ExitStack

import concourse.bass as bass
import concourse.mybir as mybir

P = 128
D = 1024
S = 1024
N_MEM = 256
KT = D // P
HALF = 512
EPS = 1e-6

GLA_HEADS = 4
DK = 64
GLA_LOWRANK = 16
GATE_NORM = 16.0
CH = 128
NC = S // CH

LRU_TILES = 4
LRU_BLOCK = 64
XHEADS = 4
XHEAD_DIM = D // XHEADS

D_FF = 2816
FF_TILES = D_FF // P
GROUP = 2
GROUPS = FF_TILES // GROUP

F32 = mybir.dt.float32
F32R = mybir.dt.float32r
U32 = mybir.dt.uint32
ACT = mybir.ActivationFunctionType
ALU = mybir.AluOpType
AX = mybir.AxisListType

KIB = 1024
RING = 2

SLOT_LRU = 0
SLOT_GK = 2 * LRU_TILES
SLOT_KQ = SLOT_GK + 1
SLOT_VO = SLOT_KQ + 4
SLOT_MEM = SLOT_VO + 8
SLOT_MIX = SLOT_MEM + 16
SLOT_XQ = SLOT_MIX + KT
SLOT_XO = SLOT_XQ + KT
SLOT_FFN = SLOT_XO + KT
N_SLOTS = SLOT_FFN + 6 * GROUPS

MAIN_ATT = SLOT_XO
MAIN_XO = MAIN_ATT + KT
MAIN_END = MAIN_XO + KT

PARAMS = {}
_col = 0
for _name, _n in (("g_mix", KT), ("g_xattn", KT), ("g_mem", KT), ("g_ffn", KT), ("g_final", KT),
                  ("b_gk", 2), ("g_head", 1), ("conv_lru_w", 4 * LRU_TILES), ("conv_lru_b", LRU_TILES),
                  ("b_rg_a", LRU_TILES), ("b_rg_x", LRU_TILES), ("lru_lambda", LRU_TILES),
                  ("conv_ffn_w", 3 * FF_TILES), ("conv_ffn_b", FF_TILES)):
    PARAMS[_name] = _col
    _col += _n
N_PARAMS = _col

LEVELS = [64, 32, 16, 8, 4, 2, 1]


class Steps:

    def __init__(self, engine, sem):
        self.engine, self.sem, self.n = engine, sem, 0

    def __call__(self, instruction):
        instruction.then_inc(self.sem, 1)
        self.n = self.n + 1
        return self.n

    def settle(self):
        self.engine.wait_ge(self.sem, self.n)


def build(nc, xT, memT, wstream, params, w_gk, w_rg_a, w_rg_x, yT):
    ctx = ExitStack()
    with ctx:
        base = (nc.sbuf_base + 31) // 32 * 32

        RAW, WHI, WLO = base, base + RING * 4 * KIB, base + 2 * RING * 4 * KIB
        A_HI = WLO + RING * 4 * KIB
        A_LO = A_HI + 32 * KIB
        B_HI = A_LO + 32 * KIB
        B_LO = B_HI + 32 * KIB
        X = B_LO + 32 * KIB
        KV = X + 32 * KIB
        RS = KV + 16 * KIB
        TMP = RS + 4 * KIB
        CONST = TMP + 4 * KIB
        top = [CONST]

        def at(name, shape, dt, offset):
            return nc.alloc_sbuf_tensor_at(name, shape, dt, offset=offset)

        def const(name, shape, dt=F32):
            n = 4
            for s in shape[1:]:
                n *= s
            t = at(name, shape, dt, top[0])
            top[0] += (n + 31) // 32 * 32
            assert top[0] <= nc.sbuf_usable_end, (name, top[0])
            return t

        raw = at("raw", [P, RING, 1024], F32, RAW)
        w_hi = at("w_hi", [P, RING, 1024], F32R, WHI)
        w_lo = at("w_lo", [P, RING, 1024], F32R, WLO)
        a_hi = at("a_hi", [P, KT, S], F32R, A_HI)
        a_lo = at("a_lo", [P, KT, S], F32R, A_LO)
        b_hi = at("b_hi", [P, KT, S], F32R, B_HI)
        b_lo = at("b_lo", [P, KT, S], F32R, B_LO)
        x = at("x", [P, KT, S], F32, X)
        rstd = at("rstd", [P, S], F32, RS)
        acc = at("acc", [P, S], F32, RS)
        diag = at("diag", [P, NC, P], F32, RS)
        tmp = at("tmp", [P, S], F32, TMP)
        masks = at("masks", [P, len(LEVELS), CH // 2], F32, TMP)

        names = ["xr", "xc", "ra", "ts", "ix", "gg"]
        places = [[B_HI + 4 * KIB * n for n in range(4)] + [KV, KV + 4 * KIB],
                  [B_LO + 4 * KIB * n for n in range(4)] + [KV + 8 * KIB, KV + 12 * KIB]]
        lru = [{n: at(f"lru_{n}{s}", [P, S], F32, places[s][i]) for i, n in enumerate(names)}
               for s in range(2)]
        og = at("og", [P, GLA_HEADS, S], F32, B_HI)
        kk = at("kk", [P, 2, S], F32, B_LO)
        qq = at("qq", [P, 2, S], F32, B_LO + 8 * KIB)
        v_tok = at("v_tok", [P, NC, 512], F32, X)
        bsum = at("bsum", [P, 2, S], F32, X + 16 * KIB)
        states = at("states", [P, NC, 2, P], F32, X + 24 * KIB)
        mem_raw = at("mem_raw", [P, KT, N_MEM], F32, X + 24 * KIB)
        gk_a = at("gk_a", [P, 2, S], F32, X)
        gk_b = at("gk_b", [P, 2, S], F32, X + 8 * KIB)
        gk_lr = at("gk_lr", [GLA_LOWRANK, S], F32, X + 24 * KIB)
        v_feat = at("v_feat", [P, 4, S], F32, B_HI)
        m_hi = at("m_hi", [P, KT, N_MEM], F32R, KV)
        m_lo = at("m_lo", [P, KT, N_MEM], F32R, KV + 8 * KIB)
        xk_new = at("xk_new", [P, KT, N_MEM], F32, A_HI)
        xk_tok = at("xk_tok", [P, 2, D], F32, A_LO + 24 * KIB)
        xv_new = at("xv_new", [P, 2, D], F32, A_HI + 8 * KIB)
        lev = [at(f"lev{n}", [P, 2, S], F32, place)
               for n, place in enumerate((A_HI + 16 * KIB, A_HI + 24 * KIB, X + 24 * KIB))]
        sT = at("sT", [P, 2, NC, 2, P], F32, A_LO)
        m_acc = at("m_acc", [P, N_MEM], F32, TMP + 2 * KIB)
        qe = at("qe", [P, 2, S], F32, A_LO + 16 * KIB)
        kd_tok = at("kd_tok", [P, NC, 2 * P], F32, A_LO + 24 * KIB)
        o_sb = [at(f"o_sb{n}", [P, 512], F32, A_HI + (16 + 2 * n) * KIB) for n in range(4)]
        o_sq = [at(f"o_sq{n}", [P, 512], F32, A_HI + (24 + 2 * n) * KIB) for n in range(2)]
        o_dg = [at(f"o_dg{n}", [P, GLA_HEADS, P], F32, A_HI + (28 + 2 * n) * KIB) for n in range(2)]
        xk = at("xk", [P, KT, N_MEM], F32, KV)
        xv = at("xv", [P, 2, D], F32, KV + 8 * KIB)
        xk_hi = at("xk_hi", [P, KT, N_MEM], F32R, A_HI)
        xk_lo = at("xk_lo", [P, KT, N_MEM], F32R, A_HI + 8 * KIB)
        xv_hi = at("xv_hi", [P, 2, D], F32R, A_HI + 16 * KIB)
        xv_lo = at("xv_lo", [P, 2, D], F32R, A_HI + 24 * KIB)
        pr = [at(f"pr{n}", [P, 2, N_MEM], F32, A_LO + 2 * n * KIB) for n in range(4)]
        pT_hi = [at(f"pT_hi{n}", [P, 2, S], F32R, (A_LO + 8 * KIB, KV)[n]) for n in range(2)]
        pT_lo = [at(f"pT_lo{n}", [P, 2, S], F32R, (A_LO + 16 * KIB, KV + 8 * KIB)[n]) for n in range(2)]
        f_hi = [at(f"f_hi{n}", [P, GROUP, S], F32R, B_HI + 8 * n * KIB) for n in range(2)]
        f_lo = [at(f"f_lo{n}", [P, GROUP, S], F32R, B_HI + (16 + 8 * n) * KIB) for n in range(2)]
        gate = at("gate", [P, S], F32, B_LO)
        conv = at("conv", [P, S], F32, B_LO + 4 * KIB)
        up = at("up", [P, S], F32, B_LO + 8 * KIB)
        facc = at("facc", [P, S], F32, B_LO + 12 * KIB)
        frs = at("frs", [P, S], F32, B_LO + 16 * KIB)
        fdiag = at("fdiag", [P, NC, P], F32, B_LO + 16 * KIB)

        ident = const("ident", [P, P])
        ones = const("ones", [P, P])
        par = const("par", [P, N_PARAMS])
        wgk = const("wgk", [GLA_LOWRANK, 2 * P])
        bd = const("bd", [P, 2, LRU_TILES, P])
        eps = const("eps", [P, 1])
        small = const("small", [P, 12, LRU_TILES])
        dec = const("dec", [P, 2, NC])
        ssum = const("ssum", [P, NC])
        srec = const("srec", [P, NC])
        m_std = const("m_std", [P, 2])
        m_rec = const("m_rec", [P, 2])
        sel = const("sel", [P, 2])
        o_std = const("o_std", [P, NC, GLA_HEADS])
        o_rec = const("o_rec", [P, NC, GLA_HEADS])
        nmax = const("nmax", [P, 16, 2])
        psum_p = const("psum_p", [P, 16, 2])
        prec = const("prec", [P, 16, 2])

        def col(name, i=0):
            return par[:, PARAMS[name] + i:PARAMS[name] + i + 1]

        ps = ctx.enter_context(nc.psum_tensor("ps", [P, 8, HALF], F32))
        main = [ps[:, 0:2, :], ps[:, 2:4, :]]
        aux = [ps[:, 4:6, :], ps[:, 6:8, :]]

        def flat(pair):
            return pair.rearrange("p b n -> p (b n)")

        def sem(name):
            return ctx.enter_context(nc.semaphore(name))

        s_raw = [sem(f"raw_loaded{n}") for n in range(RING)]
        s_taken = sem("slot_taken")
        s_whi = sem("w_hi_done")
        s_split = sem("w_split")
        s_par = sem("params_loaded")
        s_x = [sem(f"x_loaded{n}") for n in range(KT)]
        s_xr = [sem(f"x_reloaded{n}") for n in range(KT)]
        s_mem = sem("mem_loaded")
        s_bd = sem("gate_weights_loaded")
        s_cst = sem("constants_made")
        s_bd0 = sem("gate_weights_zeroed")
        s_ones = sem("ones_made")
        s_full = sem("main_full")
        s_evac = sem("main_evacuated")
        s_dve = sem("dve_steps")
        s_act = sem("act_steps")
        s_hhi = sem("h_hi_done")
        s_sq = sem("squares_done")
        s_h = sem("h_ready")
        s_acc = sem("squares_summed")
        s_ssq = sem("ssq_ready")
        s_std = sem("std_ready")
        s_rstd = sem("rstd_ready")
        s_dg = sem("diag_ready")
        s_bc = sem("rstd_broadcast")
        s_xc = sem("xc_ready")
        s_gate = sem("gates_ready")
        s_sig = sem("sigmoids_done")
        s_rec = sem("lru_factors_ready")
        s_gelu = sem("gelu_done")
        s_y = sem("y_lru_ready")
        s_yhi = sem("y_lru_hi_done")
        s_ylo = sem("y_mix_lru_ready")
        s_sp = sem("softplus_exp")
        s_spd = sem("softplus_ready")
        s_z = sem("gate_logits_ready")
        s_lse = sem("log1p_exp_ready")
        s_b = sem("log_gates_summed")
        s_silu = sem("silu_done")
        s_vt = sem("v_turned")
        s_vtok = sem("v_token_ready")
        s_mhi = sem("mem_hi_done")
        s_mh = sem("mem_ready")
        s_wgk = sem("w_gk_loaded")
        s_mq = sem("mem_squares")
        s_msq = sem("mem_squares_summed")
        s_mssq = sem("mem_ssq")
        s_mstd = sem("mem_std")
        s_ld = sem("level_exponents")
        s_le = sem("level_exps")
        s_lt = sem("level_ready")
        s_lp = sem("level_scores")
        s_lc = sem("level_scores_kept")
        s_qk = sem("q_times_k")
        s_qks = sem("q_dot_k")
        s_qe = sem("q_decayed")
        s_xkt = sem("memory_keys_turned")
        s_xkc = sem("memory_keys_copied")
        s_kvc = sem("memory_moved")
        s_ke = sem("k_exps")
        s_kd = sem("k_decayed")
        s_kt = sem("k_turned")
        s_ktok = sem("k_token_ready")
        s_dec = sem("chunk_decay")
        s_delta = sem("state_products")
        s_st = sem("states_ready")
        s_o = sem("o_ready")
        s_oc = sem("o_copied")
        s_ossq = sem("o_ssq")
        s_ostd = sem("o_std")
        s_odg = sem("o_diag")
        s_obc = sem("o_broadcast")
        s_oy = sem("y_gla_ready")
        s_oyhi = sem("y_gla_hi")
        s_oylo = sem("y_mix_gla_ready")
        s_xqh = sem("xq_hi")
        s_xq = sem("xq_ready")
        s_kvh = sem("kv_hi")
        s_kv = sem("kv_ready")
        s_sc = sem("scores_ready")
        s_mx = sem("max_ready")
        s_ex = sem("exps_ready")
        s_pn = sem("p_normalised")
        s_pt = sem("p_turned")
        s_pth = sem("p_turned_hi")
        s_ptl = sem("p_turned_ready")
        s_ath = sem("att_hi")
        s_gu = sem("gate_up_full")
        s_gue = sem("gate_up_evacuated")
        s_cv = sem("conv_ready")
        s_sl = sem("ffn_silu_done")
        s_f = sem("f_product")
        s_fh = sem("f_hi")
        s_fr = sem("f_ready")
        s_out = sem("out_full")
        s_oute = sem("out_added")
        s_fsq = sem("final_squares")
        s_facc = sem("final_summed")
        s_yf = sem("y_final_ready")
        s_store = sem("y_stored")

        block = ctx.enter_context(nc.Block())

        @block.sync
        def _(sp):
            sp.dma_start(par[:, :], params).then_inc(s_par, 16)
            sp.dma_start(x[:, 0, :], xT[0, :, :]).then_inc(s_x[0], 16)
            sp.dma_start(raw[:, 0, :], wstream[0, :, :]).then_inc(s_raw[0], 16)
            for t in range(2, KT, 2):
                sp.dma_start(x[:, t, :], xT[t, :, :]).then_inc(s_x[t], 16)
            sp.dma_start(raw[:, 1, :], wstream[1, :, :]).then_inc(s_raw[1], 16)
            assert N_SLOTS % 2 == 1
            with sp.Fori(1, N_SLOTS // 2) as i:
                for j in range(RING):
                    sp.wait_ge(s_split, i * 2 + (j - 1))
                    sp.dma_start(raw[:, j, :], wstream[i * 2 + j, :, :]).then_inc(s_raw[j], 16)
            sp.wait_ge(s_split, N_SLOTS - 2)
            sp.dma_start(raw[:, 0, :], wstream[N_SLOTS - 1, :, :]).then_inc(s_raw[0], 16)
            for t in range(KT):
                sp.wait_ge(s_yf, t + 1)
                sp.dma_start(yT[t, :, :], x[:, t, :]).then_inc(s_store, 16)
            sp.wait_ge(s_store, 16 * KT)

        @block.gpsimd
        def _(pool):
            made = 0
            pool.memset(bd[:, :, :, :], 0.0).then_inc(s_bd0, 1)
            pool.memset(ones[:, :], 1.0).then_inc(s_ones, 1)
            pool.memset(eps[:, :], EPS).then_inc(s_ones, 1)
            pool.memset(ident[:, :], 0.0).then_inc(s_cst, 1)
            pool.wait_ge(s_cst, 1)
            pool.affine_select(out=ident[:, :], in_=ident[:, :], compare_op=ALU.not_equal, fill=1.0,
                               base=0, pattern=[[-1, P]], channel_multiplier=1).then_inc(s_cst, 1)
            made = 2

            def split(n, slot_of, freed=None):
                pool.wait_ge(s_raw[slot_of], (n // 2 if isinstance(n, int) else n) * 16 + 16)
                if freed is not None:
                    pool.wait_ge(*freed)
                pool.sem_inc(s_taken, 1)
                pool.tensor_scalar(w_hi[:, slot_of, :], raw[:, slot_of, :], 1.0, 1.0, ALU.mult,
                                   ALU.mult).then_inc(s_whi, 1)

            def rest(slot_of, count):
                pool.wait_ge(s_whi, count)
                pool.tensor_tensor(w_lo[:, slot_of, :], raw[:, slot_of, :],
                                   w_hi[:, slot_of, :].bitcast(F32), ALU.subtract).then_inc(s_split, 1)

            def slot(n, freed=None):
                split(n, n % RING, freed)
                rest(n % RING, n + 1)

            slot(0)
            slot(1)
            pool.memset(masks[:, :, :], 1.0).then_inc(s_cst, 1)
            pool.memset(sel[:, :], 0.0).then_inc(s_cst, 1)
            pool.wait_ge(s_cst, made + 2)
            pool.memset(sel[0:DK, 0:1], 1.0).then_inc(s_cst, 1)
            pool.memset(sel[DK:P, 1:2], 1.0).then_inc(s_cst, 1)
            made += 4
            pool.wait_ge(s_cst, made)
            for i, m in enumerate(LEVELS):
                mask = masks[:, i, :].rearrange("p (n m) -> p n m", m=m)
                pool.affine_select(out=mask, in_=mask, compare_op=ALU.is_ge, fill=0.0, base=0,
                                   pattern=[[-2 * m, CH // (2 * m)], [0, m]], channel_multiplier=1)\
                    .then_inc(s_cst, 1)
                pool.wait_ge(s_cst, made + 1)
                pool.affine_select(out=mask, in_=mask, compare_op=ALU.is_ge, fill=0.0, base=m - 1,
                                   pattern=[[2 * m, CH // (2 * m)], [0, m]], channel_multiplier=-1)\
                    .then_inc(s_cst, 1)
                made += 2
                pool.wait_ge(s_cst, made)
            last_xq = SLOT_XO - 1
            with pool.Fori(1, (last_xq + 1) // 2) as i:
                for j in range(RING):
                    split(i, j, (s_full, i * 2 + (j - 1)))
                    rest(j, i * 2 + (j + 1))
            for n in range((last_xq + 1) // 2 * 2, SLOT_FFN + 2):
                used = n - 2 + 1
                if n - 2 >= SLOT_XO:
                    used += KT
                slot(n, (s_full, used))
            slot(SLOT_FFN + 2, (s_gu, 1))
            slot(SLOT_FFN + 3, (s_gu, 2))
            first = SLOT_FFN + 4
            for n, freed in enumerate(((s_gu, 3), (s_gu, 4), (s_gu, 5), (s_gu, 6), (s_out, 4), (s_gu, 7))):
                slot(first + n, freed)
            with pool.Fori(2, GROUPS) as g:
                for n in range(6):
                    freed = ((s_gu, g * 4), (s_out, g * 8 - 8), (s_gu, g * 4 + 1), (s_gu, g * 4 + 2),
                             (s_out, g * 8 - 4), (s_gu, g * 4 + 3))[n]
                    start = first - 6 + n
                    place = start % RING
                    split(g * 3 + start // 2, place, freed)
                    rest(place, g * 6 + (start + 1))
            slot(N_SLOTS - 2, (s_gu, 4 * GROUPS))
            slot(N_SLOTS - 1, (s_out, 8 * (GROUPS - 1)))

        @block.tensor
        def _(pe):
            def project(ring, out, hi, lo, order=range(KT), width=S, before=None, cols=P):
                halves = [(c, min(HALF, width)) for c in range(0, width, HALF)]
                first = True
                for n, k in enumerate(order):
                    if before:
                        before(k)
                    wh, wl = (w[:, ring, k * P:k * P + cols] for w in (w_hi, w_lo))
                    for m, (w, h) in enumerate(((wh, hi), (wh, lo), (wl, hi))):
                        for b, (c, size) in enumerate(halves):
                            mm = pe.matmul(out[0:cols, b, 0:size], w, h[:, k, c:c + size],
                                           start=first, stop=(n == len(order) - 1 and m == 2))
                        first = False
                return mm

            def ssq(src, out, n):
                for c in range(n):
                    mm = pe.matmul(out[:, c:c + 1], src[:, c * P:(c + 1) * P], ones[:, 0:1],
                                   start=True, stop=True)
                return mm

            def spread(dg, out, n):
                for c in range(0, n, 4):
                    w = min(4, n - c)
                    mm = pe.matmul(out[:, c // 4, 0:w * P], ones[:, :],
                                   dg[:, c:c + w, :].rearrange("p c n -> p (c n)"), start=True, stop=True)
                return mm

            def ready(n):
                pe.wait_ge(s_split, n + 1)
                if n >= 2:
                    u = n if n < SLOT_XO else n + KT
                    pe.wait_ge(s_evac, u - 1)

            def norm_matmuls(k):
                pe.wait_ge(s_acc, KT * (k + 1))
                ssq(acc, aux[0][:, 0, :], NC).then_inc(s_ssq, 1)

            def norm_spread(k):
                pe.wait_ge(s_dg, k + 1)
                spread(diag, aux[1], NC).then_inc(s_bc, 1)

            def gates(t):
                pe.wait_ge(s_xc, t + 1)
                if t:
                    pe.wait_ge(s_sig, 2 * t)
                for g in range(2):
                    for h in range(2):
                        mm = pe.matmul(aux[g][:, h, :], bd[:, g, t, :],
                                       lru[t % 2]["xc"][:, h * HALF:(h + 1) * HALF], start=True, stop=True)
                mm.then_inc(s_gate, 1)

            pe.wait_ge(s_ones, 2)
            for n in range(2 * LRU_TILES):
                ready(n)
                before = (lambda k: pe.wait_ge(s_h, k + 1)) if n == 0 else None
                project(n % RING, main[n % 2], a_hi, a_lo, before=before).then_inc(s_full, 1)
                if n == 0:
                    norm_matmuls(0)
                if n == 1:
                    pe.wait_ge(s_cst, 2)
                    norm_spread(0)
                if n >= 2 and n % 2 == 0:
                    if n == 2:
                        pe.wait_ge(s_bd, 64)
                    if n == 2:
                        pe.wait_ge(s_rstd, 1)
                    gates(n // 2 - 1)
            n = SLOT_GK
            ready(n)
            project(n % RING, main[n % 2], a_hi, a_lo, cols=GLA_LOWRANK).then_inc(s_full, 1)
            gates(LRU_TILES - 1)
            for n in range(SLOT_KQ, SLOT_KQ + 4):
                ready(n)
                project(n % RING, main[n % 2], a_hi, a_lo).then_inc(s_full, 1)
                if n == SLOT_KQ:
                    pe.wait_ge(s_evac, SLOT_GK + 1)
                    pe.wait_ge(s_wgk, 16)
                    pe.wait_ge(s_sig, 2 * LRU_TILES)
                    for j in range(2):
                        for h in range(2):
                            mm = pe.matmul(aux[j][:, h, :], wgk[:, j * P:(j + 1) * P],
                                           gk_lr[:, h * HALF:(h + 1) * HALF], start=True, stop=True)
                    mm.then_inc(s_z, 1)
            assert SLOT_VO % 2 == 1
            with pe.Fori(0, 2) as i:
                for j in range(2):
                    n = SLOT_VO + j
                    pe.wait_ge(s_split, i * 2 + (n + 1))
                    pe.wait_ge(s_evac, i * 2 + (n - 1))
                    project(n % RING, main[n % 2], a_hi, a_lo).then_inc(s_full, 1)
            for n in range(SLOT_VO + 4, SLOT_VO + 8):
                ready(n)
                project(n % RING, main[n % 2], a_hi, a_lo).then_inc(s_full, 1)
                if n == SLOT_VO + 4:
                    pe.wait_ge(s_b, 2 * NC)
                    pe.wait_ge(s_evac, SLOT_VO + 4)
                    for c in range(NC):
                        if c >= 4:
                            pe.wait_ge(s_vtok, c - 3)
                        for h in range(4):
                            mm = pe.transpose(ps[:, 4 + c % 4, h * P:(h + 1) * P],
                                              v_feat[:, h, c * P:(c + 1) * P], ident[:, :])
                        mm.then_inc(s_vt, 1)
                if n == SLOT_VO + 6:
                    pe.wait_ge(s_msq, 1)
                    ssq(m_acc, ps[:, 4, :], 2).then_inc(s_mssq, 1)
                    pe.wait_ge(s_qk, 1)

            def memory(i):
                n = SLOT_MEM + i
                half, part = divmod(i, 4)
                out = main[(half + 1) % 2]
                pe.wait_ge(s_split, n + 1)
                if i == 0:
                    pe.wait_ge(s_mh, 1)
                if part == 0:
                    pe.wait_ge(s_evac, SLOT_MEM - 1 + half if half < 2 else SLOT_MEM + 4 * (half - 1))
                if i == 12:
                    pe.wait_ge(s_xkc, 2)
                for mt in range(2):
                    for k in range(2):
                        ms = slice(mt * P, (mt + 1) * P)
                        ws = slice(k * HALF, (k + 1) * HALF)
                        for p, (m, w) in enumerate(((m_hi, w_hi), (m_hi, w_lo), (m_lo, w_hi))):
                            mm = pe.matmul(out[:, mt, :], m[:, 2 * part + k, ms], w[:, n % RING, ws],
                                           start=(part == 0 and k == 0 and p == 0),
                                           stop=(part == 3 and k == 1 and p == 2))
                mm.then_inc(s_full, 1)

            def turn_keys(part):
                if part == 0:
                    pe.wait_ge(s_evac, SLOT_MEM + 8)
                else:
                    pe.wait_ge(s_xkc, part)
                for t in range(4):
                    for mt in range(2):
                        at_ = (t % 2) * 2 + mt
                        mm = pe.transpose(main[0][:, t // 2, at_ * P:(at_ + 1) * P],
                                          xk_tok[:, mt, (4 * part + t) * P:(4 * part + t + 1) * P], ident[:, :])
                mm.then_inc(s_xkt, 1)

            for c in range(NC):
                for j in range(2):
                    at_ = (c * 2 + j) * 2
                    mm = pe.matmul(ps[:, 7, at_:at_ + 2], lev[2][:, j, c * CH:(c + 1) * CH], sel[:, :],
                                   start=True, stop=True)
            mm.then_inc(s_qks, 1)
            memory(0)
            memory(1)
            kd = lev[len(LEVELS) % 3]
            unit = 0
            for L in range(len(LEVELS)):
                if L < len(LEVELS) - 1:
                    memory(2 * L + 2)
                    memory(2 * L + 3)
                else:
                    memory(14)
                    memory(15)
                    pe.wait_ge(s_kd, 1)
                    pe.wait_ge(s_evac, SLOT_MIX)
                    for b in range(4):
                        for c in range(2 * b, 2 * b + 2):
                            for j in range(2):
                                mm = pe.transpose(ps[:, b, ((c % 2) * 2 + j) * P:((c % 2) * 2 + j + 1) * P],
                                                  kd[:, j, c * CH:(c + 1) * CH], ident[:, :])
                        mm.then_inc(s_kt, 1)
                if L in (3, 4):
                    turn_keys(L - 3)
                pe.wait_ge(s_lt, L + 1)
                if L == 0:
                    pe.wait_ge(s_lc, 1)
                    pe.wait_ge(s_mstd, 1)
                src = lev[L % 3]
                for c in range(0, NC, 2):
                    for odd in range(2):
                        if unit + odd >= 4:
                            pe.wait_ge(s_lc, unit + odd - 2)
                    for i in range(4):
                        cs = slice((c + i // 2) * CH, (c + i // 2 + 1) * CH)
                        for odd in range(2):
                            rows = slice(DK * odd, DK * odd + DK)
                            mm = pe.matmul(ps[:, 4 + (unit + odd) % 4, i * P:(i + 1) * P],
                                           src[rows, i % 2, cs], src[rows, i % 2, cs], start=True, stop=True)
                            if i == 3:
                                mm.then_inc(s_lp, 1)
                    unit += 2
            for c in range(NC - 1):
                if c % 2 == 0:
                    pe.wait_ge(s_ktok, 4)
                for h in range(GLA_HEADS):
                    rows = slice(DK * (h % 2), DK * (h % 2) + DK)
                    at_ = (c % 2) * 2 + h // 2
                    mm = pe.matmul(ps[rows, c // 2, at_ * P:(at_ + 1) * P],
                                   kd_tok[:, c, h * DK:(h + 1) * DK], v_tok[:, c, h * P:(h + 1) * P],
                                   start=True, stop=True)
                if c % 2 or c == NC - 2:
                    mm.then_inc(s_delta, 1)
            pe.wait_ge(s_lc, 1 + unit)
            pe.wait_ge(s_qe, 1)
            for c in range(NC + 2):
                if c < NC:
                    if c >= 1:
                        pe.wait_ge(s_st, c)
                    if c >= 2:
                        pe.wait_ge(s_oc, 2 * (c - 1))
                    out = ps[:, 4 + c % 2 * 2:6 + c % 2 * 2, :]
                    for h in range(GLA_HEADS):
                        rows, j = slice(DK * (h % 2), DK * (h % 2) + DK), h // 2
                        hs, js = slice(h * P, (h + 1) * P), slice(j * P, (j + 1) * P)
                        if c:
                            pe.matmul(out[:, h % 2, js], states[rows, c, j, :], qe[rows, j, c * CH:(c + 1) * CH],
                                      start=True, stop=False)
                        mm = pe.matmul(out[:, h % 2, js], v_tok[:, c, hs], sT[:, h % 2, c, h // 2, :], start=(c == 0), stop=True)
                    mm.then_inc(s_o, 1)
                if 1 <= c <= NC:
                    pe.wait_ge(s_oc, 2 * c)
                    if c == 1:
                        pe.wait_ge(s_st, NC - 1)
                    else:
                        pe.wait_ge(s_ostd, c - 1)
                    for h in range(GLA_HEADS):
                        at_ = (c - 1) * GLA_HEADS + h
                        mm = pe.matmul(ps[:, 3, at_:at_ + 1], o_sq[(c - 1) % 2][:, h * P:(h + 1) * P],
                                       ones[:, 0:1], start=True, stop=True)
                    mm.then_inc(s_ossq, 1)
                if c >= 2:
                    pe.wait_ge(s_odg, c - 1)
                    if c >= 4:
                        pe.wait_ge(s_oy, c - 3)
                    pe.matmul(ps[:, c % 2, :], ones[:, :],
                              o_dg[c % 2][:, :, :].rearrange("p c n -> p (c n)"),
                              start=True, stop=True).then_inc(s_obc, 1)

            order = list(range(4, 8)) + list(range(4))
            pe.wait_ge(s_ostd, NC)

            def y_tiles(k):
                if k == 4:
                    pe.wait_ge(s_ylo, LRU_TILES)
                if k == 0:
                    pe.wait_ge(s_oylo, NC)

            ready(SLOT_MIX)
            n = SLOT_MIX
            project(n % RING, main[n % 2], b_hi, b_lo, order=order, before=y_tiles).then_inc(s_full, 1)
            ready(n + 1)
            project((n + 1) % RING, main[(n + 1) % 2], b_hi, b_lo, order=order).then_inc(s_full, 1)
            with pe.Fori(1, KT // 2) as i:
                for j in range(2):
                    pe.wait_ge(s_split, i * 2 + (n + j + 1))
                    pe.wait_ge(s_evac, i * 2 + (n + j - 1))
                    project((n + j) % RING, main[(n + j) % 2], b_hi, b_lo, order=order).then_inc(s_full, 1)

            def after_norm(first, k, tiles):
                for n in range(first, first + 2):
                    ready(n)
                    before = (lambda q: pe.wait_ge(s_h, KT * k + q + 1)) if n == first else None
                    project(n % RING, main[n % 2], a_hi, a_lo, before=before).then_inc(s_full, 1)
                    (norm_matmuls if n == first else norm_spread)(k)
                with pe.Fori(1, tiles // 2) as i:
                    for j in range(2):
                        pe.wait_ge(s_split, i * 2 + (first + j + 1))
                        pe.wait_ge(s_evac, i * 2 + (first + j - 1))
                        project((first + j) % RING, main[(first + j) % 2], a_hi, a_lo).then_inc(s_full, 1)

            after_norm(SLOT_XQ, 1, KT)

            pe.wait_ge(s_kv, 2)
            pe.wait_ge(s_xq, KT)
            UNITS = XHEADS * 4

            def scores(u):
                h, b = divmod(u, 4)
                if u >= 2:
                    pe.wait_ge(s_ex, 2 * (u - 1))
                for i in range(2):
                    ts = slice((2 * b + i) * P, (2 * b + i + 1) * P)
                    for d in range(2):
                        t = 2 * h + d
                        for p, (q, k) in enumerate(((b_hi, xk_hi), (b_hi, xk_lo), (b_lo, xk_hi))):
                            mm = pe.matmul(ps[:, 4 + u % 2, i * N_MEM:(i + 1) * N_MEM], q[:, t, ts],
                                           k[:, t, :], start=(d == 0 and p == 0), stop=(d == 1 and p == 2))
                mm.then_inc(s_sc, 1)

            def turn(u):
                pe.wait_ge(s_pn, u + 1)
                if u >= 2:
                    pe.wait_ge(s_ptl, u - 1)
                for m in range(2):
                    for i in range(2):
                        mm = pe.transpose(ps[:, 6 + u % 2, (2 * m + i) * P:(2 * m + i + 1) * P],
                                          pr[u % 4][:, i, m * P:(m + 1) * P], ident[:, :])
                mm.then_inc(s_pt, 1)

            def values(h):
                pe.wait_ge(s_ptl, 4 * h + 4)
                for d in range(2):
                    t = 2 * h + d
                    u = MAIN_ATT + t
                    pe.wait_ge(s_evac, u - 1)
                    for m in range(2):
                        ws = slice(t * P, (t + 1) * P)
                        for p, (w, q) in enumerate(((xv_hi, pT_hi[h % 2]), (xv_hi, pT_lo[h % 2]),
                                                    (xv_lo, pT_hi[h % 2]))):
                            for b in range(2):
                                mm = pe.matmul(main[u % 2][:, b, :], w[:, m, ws],
                                               q[:, m, b * HALF:(b + 1) * HALF],
                                               start=(m == 0 and p == 0), stop=(m == 1 and p == 2))
                    mm.then_inc(s_full, 1)

            scores(0)
            scores(1)
            for u in range(UNITS):
                turn(u)
                if u + 2 < UNITS:
                    scores(u + 2)
                if u % 4 == 0 and u:
                    values(u // 4 - 1)
            values(XHEADS - 1)

            n = SLOT_XO
            ready(n)
            project(n % RING, main[(n + KT) % 2], b_hi, b_lo,
                    before=lambda k: pe.wait_ge(s_evac, MAIN_ATT + k + 1)).then_inc(s_full, 1)
            ready(n + 1)
            project((n + 1) % RING, main[(n + 1) % 2], b_hi, b_lo).then_inc(s_full, 1)
            with pe.Fori(1, KT // 2) as i:
                for j in range(2):
                    pe.wait_ge(s_split, i * 2 + (n + j + 1))
                    pe.wait_ge(s_evac, i * 2 + (n + KT + j - 1))
                    project((n + j) % RING, main[(n + j) % 2], b_hi, b_lo).then_inc(s_full, 1)

            def out_part(ring, f, waits):
                for m in range(4):
                    if waits[m] is not None:
                        pe.wait_ge(s_oute, waits[m])
                    for k in range(GROUP):
                        ws = slice(k * HALF + m * P, k * HALF + (m + 1) * P)
                        for p, (w, q) in enumerate(((w_hi, f_hi[f]), (w_hi, f_lo[f]), (w_lo, f_hi[f]))):
                            for b in range(2):
                                mm = pe.matmul(aux[m % 2][:, b, :], w[:, ring, ws],
                                               q[:, k, b * HALF:(b + 1) * HALF],
                                               start=(k == 0 and p == 0), stop=(k == GROUP - 1 and p == 2))
                    mm.then_inc(s_out, 1)

            for q in range(4):
                n = SLOT_FFN + q
                pe.wait_ge(s_split, n + 1)
                pe.wait_ge(*((s_evac, MAIN_END - 1 + q) if q < 2 else (s_gue, q - 1)))
                before = (lambda k: pe.wait_ge(s_h, KT * 2 + k + 1)) if q == 0 else None
                project(n % RING, main[(q + 1) % 2], a_hi, a_lo, before=before).then_inc(s_gu, 1)
                if q == 0:
                    norm_matmuls(2)
                if q == 1:
                    norm_spread(2)

            def group(g, f, first):
                start = SLOT_FFN - 2
                for part in range(2):
                    for q in range(2):
                        n = start + 3 * part + q
                        pe.wait_ge(s_split, g * 6 + (n + 1))
                        pe.wait_ge(s_gue, g * 4 + (2 * part + q - 1))
                        project(n % RING, main[1 - q], a_hi, a_lo).then_inc(s_gu, 1)
                    n = start + 3 * part + 2
                    pe.wait_ge(s_split, g * 6 + (n + 1))
                    if part == 0:
                        pe.wait_ge(s_fr, g * 2)
                    waits = [g * 8 + (4 * part + m - 9) for m in range(4)]
                    if first and part == 0:
                        waits[0:2] = [None, None]
                    out_part(n % RING, f, waits)

            pe.wait_ge(s_rstd, 3)
            group(1, 0, True)
            assert GROUPS % 2 == 1
            group(2, 1, False)
            with pe.Fori(1, GROUPS // 2) as i:
                for j in range(2):
                    group(i * 2 + (1 + j), j, False)
            n = N_SLOTS - 2
            for part in range(2):
                pe.wait_ge(s_split, n + part + 1)
                if part == 0:
                    pe.wait_ge(s_fr, 2 * GROUPS)
                out_part((n + part) % RING, (GROUPS - 1) % 2,
                         [8 * (GROUPS - 1) + 4 * part + m - 1 for m in range(4)])
            pe.wait_ge(s_facc, KT)
            pe.wait_ge(s_oute, 8 * GROUPS)
            ssq(facc, aux[0][:, 0, :], NC).then_inc(s_ssq, 1)
            pe.wait_ge(s_dg, 4)
            spread(fdiag, aux[1], NC).then_inc(s_bc, 1)

        @block.scalar
        def _(act):
            for t in range(1, KT, 2):
                act.dma_start(x[:, t, :], xT[t, :, :]).then_inc(s_x[t], 16)
            act.wait_ge(s_bd0, 1)
            for g, w in enumerate((w_rg_a, w_rg_x)):
                for h in range(2):
                    rows = slice(h * LRU_BLOCK, (h + 1) * LRU_BLOCK)
                    act.dma_start(bd[rows, g, :, rows], w[h, :, :, :]).then_inc(s_bd, 16)
            act.dma_start(wgk[:, :], w_gk).then_inc(s_wgk, 16)
            step = Steps(act, s_act)

            act.wait_ge(s_par, 16)
            act.wait_ge(s_ones, 2)
            step(act.activation(small[:, 0, :], par[:, PARAMS["lru_lambda"]:PARAMS["lru_lambda"] + 4], ACT.Abs))
            step.settle()
            act.activation(small[:, 1, :], small[:, 0, :], ACT.Exp, scale=-1.0).then_inc(s_sp, 1)

            def h_tile(gain, xs, hi, count, acc_done, where):
                act.activation(hi, xs, ACT.Identity, scale=gain).then_inc(s_hhi, 1)
                if acc_done is not None:
                    act.wait_ge(s_acc, acc_done)
                act.activation(where, xs, ACT.Square).then_inc(s_sq, 1)

            for t in range(KT):
                act.wait_ge(s_x[t], 16)
                h_tile(col("g_mix", t), x[:, t, :], a_hi[:, t, :], t, t - 1 if t >= 2 else None,
                       flat(aux[t % 2]))

            def root(k):
                act.wait_ge(s_ssq, k + 1)
                act.activation(ssum[:, :], aux[0][:, 0, 0:NC], ACT.Sqrt, scale=1.0 / D,
                               bias=eps[:, 0:1]).then_inc(s_std, 1)

            root(0)

            def lru_tile(t):
                b = lru[t % 2]
                act.wait_ge(s_gate, t + 1)
                if t == 0:
                    act.wait_ge(s_spd, 1)
                if t >= 2:
                    act.wait_ge(s_ylo, t - 1)
                act.activation(b["ra"][:, :], flat(aux[0]), ACT.Sigmoid, bias=col("b_rg_a", t)).then_inc(s_sig, 1)
                act.activation(b["ix"][:, :], flat(aux[1]), ACT.Sigmoid, bias=col("b_rg_x", t)).then_inc(s_sig, 1)
                act.wait_ge(s_sig, 2 * t + 1)
                step(act.activation(b["ts"][:, :], b["ra"][:, :], ACT.Tanh, scale=small[:, 10, t:t + 1]))
                step(act.activation(b["ra"][:, :], b["ra"][:, :], ACT.Exp, scale=small[:, 11, t:t + 1]))
                step.settle()
                act.activation(b["ts"][:, :], b["ts"][:, :], ACT.Sqrt).then_inc(s_rec, 1)
                act.wait_ge(s_evac, 2 * t + 2)
                act.activation(b["gg"][:, :], b["gg"][:, :], ACT.Gelu_apprx_tanh).then_inc(s_gelu, 1)
                act.wait_ge(s_y, t + 1)
                act.activation(b_hi[:, 4 + t, :], b["gg"][:, :], ACT.Identity).then_inc(s_yhi, 1)

            for t in range(LRU_TILES):
                lru_tile(t)
            act.wait_ge(s_z, 1)
            act.dma_start(mem_raw[:, :, :], memT).then_inc(s_mem, 16)
            for j in range(2):
                step(act.activation(gk_a[:, j, :], flat(aux[j]), ACT.Abs, bias=col("b_gk", j)))
            step.settle()
            step(act.activation(gk_a[:, :, :], gk_a[:, :, :], ACT.Exp, scale=-1.0))
            step.settle()
            act.activation(gk_a[:, :, :], gk_a[:, :, :], ACT.Ln, bias=1.0).then_inc(s_lse, 1)
            for c in range(NC):
                act.wait_ge(s_vt, c + 1)
                act.activation(v_tok[:, c, :], ps[:, 4 + c % 4, :], ACT.Identity).then_inc(s_vtok, 1)
            act.wait_ge(s_mem, 16)
            act.wait_ge(s_vtok, NC)
            act.activation(ps[:, 4:8, :].rearrange("p b n -> p (b n)"),
                           mem_raw[:, :, :].rearrange("p k m -> p (k m)"), ACT.Square).then_inc(s_mq, 1)
            for k in range(KT):
                act.activation(m_hi[:, k, :], mem_raw[:, k, :], ACT.Identity,
                               scale=col("g_mem", k)).then_inc(s_mhi, 1)
            act.wait_ge(s_mssq, 1)
            act.activation(m_std[:, :], ps[:, 4, 0:2], ACT.Sqrt, scale=1.0 / D, bias=eps[:, 0:1])\
                .then_inc(s_mstd, 1)
            for h in range(4):
                act.wait_ge(s_evac, SLOT_VO + 4 + h + 1)
                act.activation(og[:, h, :], og[:, h, :], ACT.Silu).then_inc(s_silu, 1)
            ends = bsum[:, :, :].rearrange("p j (c i) -> p j c i", i=CH)[:, :, :, CH - 1]
            act.activation(dec[:, :, :], ends, ACT.Exp, scale=1.0 / GATE_NORM).then_inc(s_dec, 1)
            for L in range(len(LEVELS) + 1):
                act.wait_ge(s_ld, L + 1)
                act.activation(lev[L % 3][:, :, :], lev[L % 3][:, :, :], ACT.Exp,
                               scale=1.0 / GATE_NORM).then_inc(s_le, 1)
                if L in (4, 5):
                    act.wait_ge(s_xkt, L - 3)
                    act.activation(xk_new[:, 4 * (L - 4):4 * (L - 3), :].rearrange("p t m -> p (t m)"),
                                   flat(main[0]), ACT.Identity).then_inc(s_xkc, 1)
                if L == 1:
                    act.activation(qe[:, :, :], bsum[:, :, :], ACT.Exp, scale=1.0 / GATE_NORM).then_inc(s_ke, 1)
            for b in range(4):
                act.wait_ge(s_kt, b + 1)
                act.activation(kd_tok[:, 2 * b:2 * b + 2, :],
                               ps[:, b, :].rearrange("p (c n) -> p c n", c=2), ACT.Identity)\
                    .then_inc(s_ktok, 1)
            act.wait_ge(s_evac, SLOT_MIX)
            act.activation(xk[:, :, :], xk_new[:, :, :], ACT.Identity).then_inc(s_kvc, 1)
            act.activation(xv[:, :, :], xv_new[:, :, :], ACT.Identity).then_inc(s_kvc, 1)
            for c in range(NC + 3):
                if c < NC:
                    act.wait_ge(s_o, c + 1)
                    if c >= 4:
                        act.wait_ge(s_oylo, c - 3)
                    out = ps[:, 4 + c % 2 * 2:6 + c % 2 * 2, 0:256].rearrange("p o (j n) -> p o j n", j=2)
                    copy, squares = (t[:, :].rearrange("p (j o n) -> p o j n", j=2, o=2)
                                     for t in (o_sb[c % 4], o_sq[c % 2]))
                    act.activation(copy, out, ACT.Identity).then_inc(s_oc, 1)
                    if c >= 2:
                        act.wait_ge(s_ossq, c - 1)
                    act.activation(squares, out, ACT.Square).then_inc(s_oc, 1)
                if 1 <= c <= NC:
                    act.wait_ge(s_ossq, c)
                    act.activation(o_std[:, c - 1, :], ps[:, 3, (c - 1) * 4:c * 4], ACT.Sqrt, scale=1.0 / P,
                                   bias=eps[:, 0:1]).then_inc(s_ostd, 1)
                if c >= 3:
                    act.wait_ge(s_oy, c - 2)
                    d = c - 3
                    act.activation(b_hi[:, 0:4, d * CH:(d + 1) * CH],
                                   o_sb[d % 4][:, :].rearrange("p (h n) -> p h n", h=4), ACT.Identity)\
                        .then_inc(s_oyhi, 1)
            act.wait_ge(s_o, NC)
            act.wait_ge(s_oylo, NC)
            for t in range(KT):
                act.dma_start(x[:, t, :], xT[t, :, :]).then_inc(s_xr[t], 16)
            for t in range(KT):
                act.wait_ge(s_evac, SLOT_MIX + t + 1)
                h_tile(col("g_xattn", t), x[:, t, :], a_hi[:, t, :], t, KT + t - 1 if t >= 2 else None,
                       flat(aux[t % 2]))
            root(1)
            with act.Fori(0, KT) as t:
                act.wait_ge(s_evac, t + (SLOT_XQ + 1))
                act.activation(b_hi[:, bass.ds(t, 1), :].rearrange("p o n -> p (o n)"), tmp[:, :],
                               ACT.Identity).then_inc(s_xqh, 1)
            act.wait_ge(s_full, SLOT_XO)
            act.activation(xk_hi[:, :, :], xk[:, :, :], ACT.Identity).then_inc(s_kvh, 1)
            act.activation(xv_hi[:, :, :], xv[:, :, :], ACT.Identity).then_inc(s_kvh, 1)

            def exps(u):
                act.wait_ge(s_mx, u + 1)
                if u >= 4:
                    act.wait_ge(s_pt, u - 3)
                for i in range(2):
                    act.activation(pr[u % 4][:, i, :], ps[:, 4 + u % 2, i * N_MEM:(i + 1) * N_MEM], ACT.Exp,
                                   bias=nmax[:, u, i:i + 1], accum_out=psum_p[:, u, i:i + 1]).then_inc(s_ex, 1)

            def turned(u):
                act.wait_ge(s_pt, u + 1)
                h, b = divmod(u, 4)
                if h >= 2:
                    act.wait_ge(s_full, MAIN_ATT + 2 * h - 2)
                act.activation(pT_hi[h % 2][:, :, b * 256:(b + 1) * 256],
                               ps[:, 6 + u % 2, :].rearrange("p (m n) -> p m n", m=2), ACT.Identity)\
                    .then_inc(s_pth, 1)

            def att(h):
                for d in range(2):
                    t = 2 * h + d
                    act.wait_ge(s_full, MAIN_ATT + t + 1)
                    act.activation(b_hi[:, t, :], flat(main[(MAIN_ATT + t) % 2]),
                                   ACT.Identity).then_inc(s_ath, 1)

            exps(0)
            exps(1)
            for u in range(4 * XHEADS):
                turned(u)
                if u + 2 < 4 * XHEADS:
                    exps(u + 2)
                if u % 4 == 0 and u:
                    att(u // 4 - 1)
            att(XHEADS - 1)
            for t in range(KT):
                act.wait_ge(s_evac, MAIN_XO + t + 1)
                h_tile(col("g_ffn", t), x[:, t, :], a_hi[:, t, :], t, 2 * KT + t - 1 if t >= 2 else None,
                       flat(aux[t % 2]))
            root(2)

            def ffn_tile(g, j, f):
                act.wait_ge(s_cv, g * 2 + (j + 1))
                act.activation(conv[:, :], conv[:, :], ACT.Silu).then_inc(s_sl, 1)
                act.wait_ge(s_f, g * 2 + (j + 1))
                act.activation(f_hi[f][:, j, :], up[:, :], ACT.Identity).then_inc(s_fh, 1)

            with act.Fori(0, GROUPS // 2) as i:
                for f in range(2):
                    for j in range(GROUP):
                        ffn_tile(i * 2 + f, j, f)
            for j in range(GROUP):
                ffn_tile(GROUPS - 1, j, (GROUPS - 1) % 2)
            for t in range(KT):
                act.wait_ge(s_oute, 8 * (GROUPS - 1) + t + 1)
                if t >= 2:
                    act.wait_ge(s_facc, t - 1)
                if t == 0:
                    act.wait_ge(s_gue, 4 * GROUPS)
                act.activation(flat(main[t % 2]), x[:, t, :], ACT.Square).then_inc(s_fsq, 1)
            root(3)

        @block.vector
        def _(dve):
            step = Steps(dve, s_dve)
            def h_rest(gain, xs, hi, lo, hhi, sq, where, into, first):
                dve.wait_ge(s_hhi, hhi)
                dve.scalar_tensor_tensor(lo, xs, gain, hi.bitcast(F32), ALU.mult, ALU.subtract).then_inc(s_h, 1)
                dve.wait_ge(s_sq, sq)
                if first:
                    dve.tensor_copy(into, where).then_inc(s_acc, 1)
                else:
                    dve.wait_ge(s_acc, sq - 1)
                    dve.tensor_tensor(into, where, into, ALU.add).then_inc(s_acc, 1)

            for t in range(KT):
                dve.wait_ge(s_x[t], 16)
                h_rest(col("g_mix", t), x[:, t, :], a_hi[:, t, :], a_lo[:, t, :], t + 1, t + 1,
                       flat(aux[t % 2]), acc[:, :], t == 0)

            sm = [small[:, n, :] for n in range(12)]
            dve.wait_ge(s_sp, 1)
            step(dve.tensor_scalar(sm[2], sm[1], 2.0, None, ALU.add))
            step.settle()
            step(dve.reciprocal(sm[3], sm[2]))
            step.settle()
            step(dve.tensor_tensor(sm[4], sm[1], sm[3], ALU.mult))
            step.settle()
            step(dve.tensor_tensor(sm[5], sm[4], sm[4], ALU.mult))
            step.settle()
            step(dve.tensor_scalar(sm[6], sm[5], 1.0 / 17, 1.0 / 15, ALU.mult, ALU.add))
            for d in (13, 11, 9, 7, 5, 3, 1):
                step.settle()
                step(dve.tensor_tensor(sm[6], sm[6], sm[5], ALU.mult))
                step.settle()
                step(dve.tensor_scalar(sm[6], sm[6], 1.0 / d, None, ALU.add))
            step(dve.tensor_scalar(sm[7], par[:, PARAMS["lru_lambda"]:PARAMS["lru_lambda"] + 4], -1.0, 0.0,
                                   ALU.mult, ALU.max))
            step.settle()
            step(dve.scalar_tensor_tensor(sm[8], sm[4], 2.0, sm[6], ALU.mult, ALU.mult))
            step.settle()
            step(dve.tensor_tensor(sm[9], sm[8], sm[7], ALU.add))
            step.settle()
            step(dve.tensor_scalar(sm[10], sm[9], 4.0, None, ALU.mult))
            step.settle()
            dve.tensor_scalar(sm[11], sm[9], -8.0, None, ALU.mult).then_inc(s_spd, 1)

            def diagonal(k, out):
                dve.wait_ge(s_std, k + 1)
                step(dve.reciprocal(srec[:, :], ssum[:, :]))
                step.settle()
                dve.wait_ge(s_cst, 2)
                dve.tensor_tensor(out, ident[:, :].unsqueeze(1).to_broadcast([P, NC, P]),
                                  srec[:, :].unsqueeze(2).to_broadcast([P, NC, P]), ALU.mult).then_inc(s_dg, 1)

            def rstd_ready(k):
                dve.wait_ge(s_bc, k + 1)
                dve.tensor_copy(rstd[:, :], flat(aux[1])).then_inc(s_rstd, 1)
                dve.wait_ge(s_rstd, k + 1)

            diagonal(0, diag[:, :, :])
            rstd_ready(0)

            def scaled(out, u):
                dve.wait_ge(s_full, u + 1)
                dve.tensor_tensor(out, flat(main[u % 2]), rstd[:, :], ALU.mult).then_inc(s_evac, 1)

            def branch(t):
                b = lru[t % 2]
                scaled(b["xr"][:, :], 2 * t)
                dve.wait_ge(s_evac, 2 * t + 1)
                tap = [col("conv_lru_w", 4 * t + n) for n in range(4)]
                step(dve.tensor_scalar(b["xc"][:, :], b["xr"][:, :], tap[3], col("conv_lru_b", t),
                                       ALU.mult, ALU.add))
                for back in (1, 2, 3):
                    step.settle()
                    ins = dve.scalar_tensor_tensor(b["xc"][:, back:], b["xr"][:, 0:S - back], tap[3 - back],
                                                   b["xc"][:, back:], ALU.mult, ALU.add)
                    if back < 3:
                        step(ins)
                    else:
                        ins.then_inc(s_xc, 1)

            def recurrence(t):
                b = lru[t % 2]
                dve.wait_ge(s_rec, t + 1)
                step(dve.scalar_tensor_tensor(b["ts"][:, :], b["ra"][:, :], 1.0, b["ts"][:, :],
                                              ALU.add, ALU.mult))
                step(dve.tensor_tensor(b["ix"][:, :], b["ix"][:, :], b["xc"][:, :], ALU.mult))
                step.settle()
                step(dve.memset(b["ts"][:, 0:1], 1.0))
                step.settle()
                step(dve.tensor_tensor(b["ts"][:, :], b["ts"][:, :], b["ix"][:, :], ALU.mult))
                step.settle()
                step(dve.tensor_tensor_scan(b["xr"][:, :], b["ra"][:, :], b["ts"][:, :], 0.0,
                                            ALU.mult, ALU.add))
                step.settle()
                dve.wait_ge(s_gelu, t + 1)
                dve.tensor_tensor(b["gg"][:, :], b["gg"][:, :], b["xr"][:, :], ALU.mult).then_inc(s_y, 1)
                dve.wait_ge(s_yhi, t + 1)
                dve.wait_ge(s_y, t + 1)
                dve.tensor_tensor(b_lo[:, 4 + t, :], b["gg"][:, :], b_hi[:, 4 + t, :].bitcast(F32),
                                  ALU.subtract).then_inc(s_ylo, 1)

            def gelu_in(t):
                scaled(lru[t % 2]["gg"][:, :], 2 * t + 1)

            branch(0)
            gelu_in(0)
            for t in range(LRU_TILES):
                if t + 1 < LRU_TILES:
                    branch(t + 1)
                else:
                    dve.wait_ge(s_full, SLOT_GK + 1)
                    dve.tensor_tensor(gk_lr[:, :], flat(main[SLOT_GK % 2])[0:GLA_LOWRANK, :],
                                      rstd[0:GLA_LOWRANK, :], ALU.mult).then_inc(s_evac, 1)
                recurrence(t)
                if t + 1 < LRU_TILES:
                    gelu_in(t + 1)
            for j in range(2):
                scaled(kk[:, j, :], SLOT_KQ + j)
                if j == 0:
                    dve.wait_ge(s_lse, 1)
                    for i in range(2):
                        step(dve.tensor_scalar(gk_b[:, i, :], flat(aux[i]), col("b_gk", i), 0.0,
                                               ALU.add, ALU.min))
                    step.settle()
                    step(dve.tensor_tensor(gk_b[:, :, :], gk_b[:, :, :], gk_a[:, :, :], ALU.subtract))
                    step.settle()
                    for i in range(2):
                        for c in range(NC):
                            cs = slice(c * CH, (c + 1) * CH)
                            dve.tensor_tensor_scan(bsum[:, i, cs], ones[:, :], gk_b[:, i, cs], 0.0,
                                                   ALU.mult, ALU.add).then_inc(s_b, 1)
            for j in range(2):
                u = SLOT_KQ + 2 + j
                dve.wait_ge(s_full, u + 1)
                dve.scalar_tensor_tensor(qq[:, j, :], flat(main[u % 2]), DK ** -0.5, rstd[:, :],
                                         ALU.mult, ALU.mult).then_inc(s_evac, 1)
            for h in range(4):
                scaled(v_feat[:, h, :], SLOT_VO + h)
            dve.wait_ge(s_mq, 1)
            dve.wait_ge(s_cst, 6 + 2 * len(LEVELS))
            dve.tensor_reduce(m_acc[:, :], ps[:, 4:8, :].rearrange("p b (k m) -> p m (b k)", m=N_MEM),
                              AX.X, ALU.add).then_inc(s_msq, 1)
            scaled(og[:, 0, :], SLOT_VO + 4)
            for k in range(KT):
                dve.wait_ge(s_mhi, k + 1)
                ins = dve.scalar_tensor_tensor(m_lo[:, k, :], mem_raw[:, k, :], col("g_mem", k),
                                               m_hi[:, k, :].bitcast(F32), ALU.mult, ALU.subtract)
                if k < KT - 1:
                    step(ins)
            ins.then_inc(s_mh, 1)
            scaled(og[:, 1, :], SLOT_VO + 5)
            step.settle()
            dve.wait_ge(s_mh, 1)
            dve.tensor_tensor(lev[2][:, :, :], qq[:, :, :], kk[:, :, :], ALU.mult).then_inc(s_qk, 1)
            dve.wait_ge(s_mstd, 1)
            step(dve.reciprocal(m_rec[:, :], m_std[:, :]))
            step.settle()
            scaled(og[:, 2, :], SLOT_VO + 6)
            scaled(og[:, 3, :], SLOT_VO + 7)

            def level(L):
                m = LEVELS[L]
                buf = lev[L % 3]
                sv, bv = (t[:, :, :].rearrange("p j (n h m) -> p (j n) h m", h=2, m=m) for t in (buf, bsum))
                n = 2 * S // (2 * m)
                ref = bv[:, :, 0, m - 1:m].to_broadcast([P, n, m])
                step(dve.tensor_tensor(sv[:, :, 0, :], ref, bv[:, :, 0, :], ALU.subtract))
                dve.tensor_tensor(sv[:, :, 1, :], bv[:, :, 1, :], ref, ALU.subtract).then_inc(s_ld, 1)

            def level_product(L):
                m = LEVELS[L]
                sv, kv, qv = (t[:, :, :].rearrange("p j (n h m) -> p (j n) h m", h=2, m=m)
                              for t in (lev[L % 3], kk, qq))
                dve.wait_ge(s_le, L + 1)
                step(dve.tensor_tensor(sv[:, :, 0, :], sv[:, :, 0, :], kv[:, :, 0, :], ALU.mult))
                step.settle()
                dve.tensor_tensor(sv[:, :, 1, :], sv[:, :, 1, :], qv[:, :, 1, :], ALU.mult).then_inc(s_lt, 1)

            dve.wait_ge(s_b, 2 * NC)
            level(0)

            def memory(half):
                dve.wait_ge(s_full, SLOT_MEM + 4 * half + 4)
                out = (xk_tok, xv_new)[half // 2][:, :, (half % 2) * HALF:(half % 2 + 1) * HALF]
                dve.tensor_tensor(out, main[(half + 1) % 2], m_rec[:, :].unsqueeze(2).to_broadcast([P, 2, HALF]),
                                  ALU.mult).then_inc(s_evac, 4)

            dve.wait_ge(s_qks, 1)
            level(1)
            got = ps[:, 7, 0:4 * NC].rearrange("p (n o) -> p o n", o=2)
            for odd in range(2):
                ins = dve.tensor_tensor(sT[:, odd, :, :, :].rearrange("p c j n -> p (c j) n"),
                                        ident[:, :].unsqueeze(1).to_broadcast([P, 2 * NC, P]),
                                        got[:, odd, :].unsqueeze(2).to_broadcast([P, 2 * NC, P]), ALU.mult)
                if odd == 0:
                    step(ins)
            ins.then_inc(s_lc, 1)
            step.settle()
            level_product(0)
            kd = lev[len(LEVELS) % 3]
            unit = 0
            for L in range(len(LEVELS)):
                m = LEVELS[L]
                if L >= 1:
                    dve.wait_ge(s_lp, 8 * L)
                    if L + 1 < len(LEVELS):
                        level(L + 1)
                    else:
                        bv, kdv = (t[:, :, :].rearrange("p j (c i) -> p (j c) i", i=CH) for t in (bsum, kd))
                        dve.tensor_tensor(kdv, bv[:, :, CH - 1:CH].to_broadcast([P, 2 * NC, CH]), bv,
                                          ALU.subtract).then_inc(s_ld, 1)
                if L + 1 < len(LEVELS):
                    level_product(L + 1)
                else:
                    dve.wait_ge(s_le, L + 2)
                    dve.wait_ge(s_ld, L + 2)
                    dve.tensor_tensor(kd[:, :, :], kd[:, :, :], kk[:, :, :], ALU.mult).then_inc(s_kd, 1)
                if L == 2:
                    dve.wait_ge(s_ke, 1)
                    dve.tensor_tensor(qe[:, :, :], qe[:, :, :], qq[:, :, :], ALU.mult).then_inc(s_qe, 1)
                if L % 2 == 0:
                    memory(L // 2)
                for c in range(0, NC, 2):
                    for odd in range(2):
                        dve.wait_ge(s_lp, unit + 1)
                        dve.wait_ge(s_lc, max(1, unit - 6))
                        got = ps[:, 4 + unit % 4, :].rearrange("p (i n h m) -> p i n h m", i=4, h=2, m=m)
                        kept = sT[:, odd, c:c + 2, :, :].rearrange("p c j (n h m) -> p (c j) n h m", h=2, m=m)
                        mask = masks[:, L, :].bitcast(U32).rearrange("p (n m) -> p n m", m=m)
                        mask = mask.unsqueeze(1).to_broadcast([P, 4, CH // (2 * m), m])
                        dve.copy_predicated(kept[:, :, :, 1, :], mask, got[:, :, :, 1, :]).then_inc(s_lc, 1)
                        unit += 1
            dve.wait_ge(s_dec, 1)
            for c in range(NC - 1):
                dve.wait_ge(s_delta, c // 2 + 1)
                got = ps[:, c // 2, (c % 2) * 256:(c % 2) * 256 + 256].rearrange("p (j n) -> p j n", j=2)
                if c == 0:
                    dve.tensor_copy(states[:, 1, :, :], got).then_inc(s_st, 1)
                    continue
                dve.wait_ge(s_st, c)
                step(dve.scalar_tensor_tensor(states[:, c + 1, 0, :], states[:, c, 0, :], dec[:, 0, c:c + 1],
                                              got[:, 0, :], ALU.mult, ALU.add))
                dve.scalar_tensor_tensor(states[:, c + 1, 1, :], states[:, c, 1, :], dec[:, 1, c:c + 1],
                                         got[:, 1, :], ALU.mult, ALU.add).then_inc(s_st, 1)
            for c in range(NC + 2):
                if c < NC:
                    dve.wait_ge(s_ostd, c + 1)
                    step(dve.reciprocal(o_rec[:, c, :], o_std[:, c, :]))
                    step.settle()
                    if c >= 2:
                        dve.wait_ge(s_obc, c - 1)
                    dve.tensor_tensor(o_dg[c % 2][:, :, :], ident[:, :].unsqueeze(1).to_broadcast([P, 4, P]),
                                      o_rec[:, c, :].unsqueeze(2).to_broadcast([P, 4, P]), ALU.mult)\
                        .then_inc(s_odg, 1)
                if c >= 1 and c <= NC:
                    d = c - 1
                    dve.wait_ge(s_obc, d + 1)
                    o = o_sb[d % 4]
                    step(dve.tensor_tensor(o[:, :], ps[:, d % 2, :], o[:, :], ALU.mult))
                    step.settle()
                    ov = o[:, :].rearrange("p (h n) -> p h n", h=4)
                    dve.wait_ge(s_silu, 4)
                    dve.scalar_tensor_tensor(ov, ov, col("g_head"), og[:, :, d * CH:(d + 1) * CH],
                                             ALU.mult, ALU.mult).then_inc(s_oy, 1)
                if c >= 2:
                    d = c - 2
                    dve.wait_ge(s_oyhi, d + 1)
                    cs = slice(d * CH, (d + 1) * CH)
                    dve.tensor_tensor(b_lo[:, 0:4, cs], o_sb[d % 4][:, :].rearrange("p (h n) -> p h n", h=4),
                                      b_hi[:, 0:4, cs].bitcast(F32), ALU.subtract).then_inc(s_oylo, 1)

            def residual(t, u, gain, k):
                dve.wait_ge(s_full, u + 1)
                dve.tensor_tensor(x[:, t, :], flat(main[u % 2]), x[:, t, :], ALU.add).then_inc(s_evac, 1)
                h_rest(col(gain, t), x[:, t, :], a_hi[:, t, :], a_lo[:, t, :], KT * k + t + 1,
                       KT * k + t + 1, flat(aux[t % 2]), acc[:, :], t == 0)

            for t in range(KT):
                dve.wait_ge(s_xr[t], 16)
                residual(t, SLOT_MIX + t, "g_xattn", 1)
            diagonal(1, diag[:, :, :])
            rstd_ready(1)
            def query(i, j):
                u = SLOT_XQ + j
                dve.wait_ge(s_full, i * 2 + (u + 1))
                if not isinstance(i, int) or j:
                    dve.wait_ge(s_xq, i * 2 + j)
                dve.scalar_tensor_tensor(tmp[:, :], flat(main[u % 2]), XHEAD_DIM ** -0.5, rstd[:, :],
                                         ALU.mult, ALU.mult).then_inc(s_evac, 1)
                dve.wait_ge(s_xqh, i * 2 + (j + 1))
                dve.wait_ge(s_evac, i * 2 + (u + 1))
                hi, lo = (z[:, bass.ds(i * 2 + j, 1), :].rearrange("p o n -> p (o n)")
                          for z in (b_hi, b_lo))
                dve.tensor_tensor(lo, tmp[:, :], hi.bitcast(F32), ALU.subtract).then_inc(s_xq, 1)

            query(0, 0)
            query(0, 1)
            with dve.Fori(1, KT // 2) as i:
                query(i, 0)
                query(i, 1)
            dve.wait_ge(s_kvh, 1)
            dve.tensor_tensor(xk_lo[:, :, :], xk[:, :, :], xk_hi[:, :, :].bitcast(F32), ALU.subtract)\
                .then_inc(s_kv, 1)
            dve.wait_ge(s_kvh, 2)
            dve.tensor_tensor(xv_lo[:, :, :], xv[:, :, :], xv_hi[:, :, :].bitcast(F32), ALU.subtract)\
                .then_inc(s_kv, 1)

            def maxima(u):
                dve.wait_ge(s_sc, u + 1)
                dve.tensor_reduce(nmax[:, u, :], ps[:, 4 + u % 2, :].rearrange("p (i m) -> p i m", i=2),
                                  AX.X, ALU.max, negate=True).then_inc(s_mx, 1)

            def normalise(u):
                dve.wait_ge(s_ex, 2 * u + 2)
                step(dve.reciprocal(prec[:, u, :], psum_p[:, u, :]))
                step.settle()
                dve.tensor_tensor(pr[u % 4][:, :, :], pr[u % 4][:, :, :],
                                  prec[:, u, :].unsqueeze(2).to_broadcast([P, 2, N_MEM]), ALU.mult)\
                    .then_inc(s_pn, 1)

            def turned_rest(u):
                dve.wait_ge(s_pth, u + 1)
                h, b = divmod(u, 4)
                ts = slice(b * 256, (b + 1) * 256)
                dve.tensor_tensor(pT_lo[h % 2][:, :, ts], ps[:, 6 + u % 2, :].rearrange("p (m n) -> p m n", m=2),
                                  pT_hi[h % 2][:, :, ts].bitcast(F32), ALU.subtract).then_inc(s_ptl, 1)

            def att_rest(h):
                for t in (2 * h, 2 * h + 1):
                    dve.wait_ge(s_ath, t + 1)
                    dve.tensor_tensor(b_lo[:, t, :], flat(main[(MAIN_ATT + t) % 2]),
                                      b_hi[:, t, :].bitcast(F32), ALU.subtract).then_inc(s_evac, 1)

            units = 4 * XHEADS
            maxima(0)
            maxima(1)
            normalise(0)
            for u in range(units):
                if u + 1 < units:
                    normalise(u + 1)
                turned_rest(u)
                if u + 2 < units:
                    maxima(u + 2)
                if u % 4 == 0 and u:
                    att_rest(u // 4 - 1)
            att_rest(XHEADS - 1)
            for t in range(KT):
                residual(t, MAIN_XO + t, "g_ffn", 2)
            diagonal(2, diag[:, :, :])
            rstd_ready(2)

            def ffn_tile(g, j, f, n):
                t = g * 2 + j
                dve.wait_ge(s_gu, g * 4 + (2 * j + 1))
                dve.tensor_tensor(gate[:, :], flat(main[1]), rstd[:, :], ALU.mult).then_inc(s_gue, 1)
                dve.wait_ge(s_gue, g * 4 + (2 * j + 1))
                tap = [par[:, bass.ds(g * 6 + (3 * j + k + PARAMS["conv_ffn_w"]), 1)] if not isinstance(g, int)
                       else col("conv_ffn_w", 3 * t + k) for k in range(3)]
                bias = (par[:, bass.ds(g * 2 + (j + PARAMS["conv_ffn_b"]), 1)] if not isinstance(g, int)
                        else col("conv_ffn_b", t))
                dve.tensor_scalar(conv[:, :], gate[:, :], tap[2], bias, ALU.mult, ALU.add).then_inc(s_dve, 1)
                dve.wait_ge(s_dve, n + 1)
                dve.scalar_tensor_tensor(conv[:, 1:], gate[:, 0:S - 1], tap[1], conv[:, 1:], ALU.mult,
                                         ALU.add).then_inc(s_dve, 1)
                dve.wait_ge(s_dve, n + 2)
                dve.scalar_tensor_tensor(conv[:, 2:], gate[:, 0:S - 2], tap[0], conv[:, 2:], ALU.mult,
                                         ALU.add).then_inc(s_cv, 1)
                dve.wait_ge(s_gu, g * 4 + (2 * j + 2))
                dve.tensor_tensor(up[:, :], flat(main[0]), rstd[:, :], ALU.mult).then_inc(s_gue, 1)
                dve.wait_ge(s_gue, g * 4 + (2 * j + 2))
                dve.wait_ge(s_sl, g * 2 + (j + 1))
                dve.tensor_tensor(up[:, :], up[:, :], conv[:, :], ALU.mult).then_inc(s_f, 1)

            def ffn_rest(g, j, f):
                dve.wait_ge(s_fh, g * 2 + (j + 1))
                dve.tensor_tensor(f_lo[f][:, j, :], up[:, :], f_hi[f][:, j, :].bitcast(F32),
                                  ALU.subtract).then_inc(s_fr, 1)

            def add_out(g, t):
                dve.wait_ge(s_out, g * 8 + (t - 7))
                dve.tensor_tensor(x[:, t, :], flat(aux[t % 2]), x[:, t, :], ALU.add).then_inc(s_oute, 1)

            per_group = 4

            def group(g, f, n0):
                for j in range(2):
                    ffn_tile(g, j, f, n0 + 2 * j)
                    add_out(g, 4 * j)
                    ffn_rest(g, j, f)
                    for t in range(4 * j + 1, 4 * j + 4):
                        add_out(g, t)

            before = step.n
            for j in range(GROUP):
                ffn_tile(0, j, 0, before + 2 * j)
                ffn_rest(0, j, 0)
            group(1, 1, before + per_group)
            group(2, 0, before + 2 * per_group)
            with dve.Fori(1, GROUPS // 2) as i:
                for j in range(2):
                    group(i * 2 + (1 + j), (1 + j) % 2, i * (2 * per_group) + (before + (1 + j) * per_group))
            step.n = before + GROUPS * per_group
            def add_squares(t):
                dve.wait_ge(s_fsq, t + 1)
                if t:
                    dve.wait_ge(s_facc, t)
                    dve.tensor_tensor(facc[:, :], flat(main[t % 2]), facc[:, :], ALU.add).then_inc(s_facc, 1)
                else:
                    dve.tensor_copy(facc[:, :], flat(main[0])).then_inc(s_facc, 1)

            for t in range(KT):
                add_out(GROUPS, t)
                if t:
                    add_squares(t - 1)
            add_squares(KT - 1)
            diagonal(3, fdiag[:, :, :])
            dve.wait_ge(s_bc, 4)
            dve.tensor_copy(frs[:, :], flat(aux[1])).then_inc(s_rstd, 1)
            dve.wait_ge(s_rstd, 4)
            for t in range(KT):
                dve.scalar_tensor_tensor(x[:, t, :], x[:, t, :], col("g_final", t), frs[:, :], ALU.mult,
                                         ALU.mult).then_inc(s_yf, 1)


def kernel(x, mem, g_mix, w_in, w_gk, b_gk, g_gla_head, conv_lru_w, conv_lru_b, w_rg_a, b_rg_a, w_rg_x,
           b_rg_x, lru_lambda, w_mix_out, g_xattn, g_mem, w_xq, w_xkv, w_xo, g_ffn, w_ffn_in, conv_ffn_w,
           conv_ffn_b, w_ffn_out, g_final):
    import numpy as np
    import concourse.bacc as bacc
    from concourse.bass_utils import run_bass_kernel_spmd as run

    def slots(w):
        w = np.asarray(w)
        n = w.shape[1] // P
        return w.reshape(KT, P, n, P).transpose(2, 1, 0, 3).reshape(n, P, KT * P)

    def cols(v):
        v = np.asarray(v)
        return v.reshape(-1, P).T if v.ndim == 1 else v.reshape(v.shape[0], -1, P).transpose(2, 1, 0).reshape(P, -1)

    w = np.asarray(w_in)[0]
    at = np.cumsum([0, 256, 256, 512, 512, GLA_LOWRANK, 512, 512])
    q, k, v, og, gk, xr, xg = (w[:, at[n]:at[n + 1]] for n in range(7))
    gk_pad = np.zeros((D, P), w.dtype)
    gk_pad[:, :GLA_LOWRANK] = gk
    lru = np.stack([slots(xr), slots(xg)], 1).reshape(2 * LRU_TILES, P, D)
    ffn_in = slots(np.asarray(w_ffn_in)[0])
    out = np.asarray(w_ffn_out)[0].reshape(GROUPS, GROUP, P, 2, HALF).transpose(0, 3, 2, 1, 4)
    out = out.reshape(GROUPS, 2, P, GROUP * HALF)
    ffn = [ffn_in[0], ffn_in[FF_TILES], ffn_in[1], ffn_in[FF_TILES + 1]]
    for g in range(1, GROUPS):
        for half in range(2):
            t = GROUP * g + half
            ffn += [ffn_in[t], ffn_in[FF_TILES + t], out[g - 1, half]]
    ffn += [out[GROUPS - 1, 0], out[GROUPS - 1, 1]]
    xkv = np.asarray(w_xkv)[0].reshape(4, 2, P, 4, HALF).transpose(3, 0, 2, 1, 4).reshape(16, P, D)
    stream = np.concatenate([lru, slots(gk_pad), slots(k), slots(q), slots(v), slots(og),
                             xkv, slots(np.asarray(w_mix_out)[0]),
                             slots(np.asarray(w_xq)[0]), slots(np.asarray(w_xo)[0]), np.stack(ffn)])
    blocks = {"g_mix": g_mix, "g_xattn": g_xattn, "g_mem": g_mem, "g_ffn": g_ffn, "g_final": [g_final],
              "b_gk": b_gk, "g_head": g_gla_head, "conv_lru_w": conv_lru_w, "conv_lru_b": conv_lru_b,
              "b_rg_a": b_rg_a, "b_rg_x": b_rg_x, "lru_lambda": lru_lambda, "conv_ffn_w": conv_ffn_w,
              "conv_ffn_b": conv_ffn_b}
    params = np.concatenate([cols(np.asarray(blocks[n][0])) for n in PARAMS], 1)
    arrays = {
        "xT": np.asarray(x)[0].T.reshape(KT, P, S),
        "memT": np.asarray(mem)[0].T.reshape(KT, P, N_MEM).transpose(1, 0, 2),
        "wstream": stream,
        "params": params,
        "w_gk": np.asarray(w_gk)[0],
        "w_rg_a": np.asarray(w_rg_a)[0].reshape(LRU_TILES, 2, LRU_BLOCK, LRU_BLOCK).transpose(1, 2, 0, 3),
        "w_rg_x": np.asarray(w_rg_x)[0].reshape(LRU_TILES, 2, LRU_BLOCK, LRU_BLOCK).transpose(1, 2, 0, 3),
    }
    arrays = {n: np.ascontiguousarray(a) for n, a in arrays.items()}
    nc = bacc.Bacc("TRN2", target_bir_lowering=False, num_devices=1, dynamic_dma_scratch_size=1024)
    ins = [nc.dram_tensor(n, a.shape, mybir.dt.from_np(a.dtype), kind="ExternalInput").ap()
           for n, a in arrays.items()]
    yT = nc.dram_tensor("yT", (KT, P, S), F32, kind="ExternalOutput").ap()
    build(nc, *ins, yT)
    got = run(nc, [arrays], core_ids=[0]).results[0]["yT"]
    return np.ascontiguousarray(got.reshape(D, S).T)[None]
```

```python
from contextlib import ExitStack

import concourse.bass as bass
import concourse.mybir as mybir

P = 128
D = 1024
S = 1024
N_MEM = 256
KT = D // P
HALF = 512
EPS = 1e-6

GLA_HEADS = 4
DK = 64
GLA_LOWRANK = 16
GATE_NORM = 16.0
CH = 128
NC = S // CH

LRU_TILES = 4
LRU_BLOCK = 64
XHEADS = 4
XHEAD_DIM = D // XHEADS

D_FF = 2816
FF_TILES = D_FF // P
GROUP = 2
GROUPS = FF_TILES // GROUP

F32 = mybir.dt.float32
F32R = mybir.dt.float32r
U32 = mybir.dt.uint32
ACT = mybir.ActivationFunctionType
ALU = mybir.AluOpType
AX = mybir.AxisListType

KIB = 1024
RING = 2

SLOT_LRU = 0
SLOT_GK = 2 * LRU_TILES
SLOT_KQ = SLOT_GK + 1
SLOT_VO = SLOT_KQ + 4
SLOT_MEM = SLOT_VO + 8
SLOT_MIX = SLOT_MEM + 16
SLOT_XQ = SLOT_MIX + KT
SLOT_XO = SLOT_XQ + KT
SLOT_FFN = SLOT_XO + KT
N_SLOTS = SLOT_FFN + 6 * GROUPS

MAIN_ATT = SLOT_XO
MAIN_XO = MAIN_ATT + KT
MAIN_END = MAIN_XO + KT

PARAMS = {}
_col = 0
for _name, _n in (("g_mix", KT), ("g_xattn", KT), ("g_mem", KT), ("g_ffn", KT), ("g_final", KT),
                  ("b_gk", 2), ("g_head", 1), ("conv_lru_w", 4 * LRU_TILES), ("conv_lru_b", LRU_TILES),
                  ("b_rg_a", LRU_TILES), ("b_rg_x", LRU_TILES), ("lru_lambda", LRU_TILES),
                  ("conv_ffn_w", 3 * FF_TILES), ("conv_ffn_b", FF_TILES)):
    PARAMS[_name] = _col
    _col += _n
N_PARAMS = _col

LEVELS = [64, 32, 16, 8, 4, 2, 1]


class Steps:

    def __init__(self, engine, sem):
        self.engine, self.sem, self.n = engine, sem, 0

    def __call__(self, instruction):
        instruction.then_inc(self.sem, 1)
        self.n = self.n + 1
        return self.n

    def settle(self):
        self.engine.wait_ge(self.sem, self.n)


def build(nc, xT, memT, wstream, params, w_gk, w_rg_a, w_rg_x, yT):
    ctx = ExitStack()
    with ctx:
        base = (nc.sbuf_base + 31) // 32 * 32

        RAW, WHI, WLO = base, base + RING * 4 * KIB, base + 2 * RING * 4 * KIB
        A_HI = WLO + RING * 4 * KIB
        A_LO = A_HI + 32 * KIB
        B_HI = A_LO + 32 * KIB
        B_LO = B_HI + 32 * KIB
        X = B_LO + 32 * KIB
        KV = X + 32 * KIB
        RS = KV + 16 * KIB
        TMP = RS + 4 * KIB
        CONST = TMP + 4 * KIB
        top = [CONST]

        def at(name, shape, dt, offset):
            return nc.alloc_sbuf_tensor_at(name, shape, dt, offset=offset)

        def const(name, shape, dt=F32):
            n = 4
            for s in shape[1:]:
                n *= s
            t = at(name, shape, dt, top[0])
            top[0] += (n + 31) // 32 * 32
            assert top[0] <= nc.sbuf_usable_end, (name, top[0])
            return t

        raw = at("raw", [P, RING, 1024], F32, RAW)
        w_hi = at("w_hi", [P, RING, 1024], F32R, WHI)
        w_lo = at("w_lo", [P, RING, 1024], F32R, WLO)
        a_hi = at("a_hi", [P, KT, S], F32R, A_HI)
        a_lo = at("a_lo", [P, KT, S], F32R, A_LO)
        b_hi = at("b_hi", [P, KT, S], F32R, B_HI)
        b_lo = at("b_lo", [P, KT, S], F32R, B_LO)
        x = at("x", [P, KT, S], F32, X)
        rstd = at("rstd", [P, S], F32, RS)
        acc = at("acc", [P, S], F32, RS)
        diag = at("diag", [P, NC, P], F32, RS)
        tmp = at("tmp", [P, S], F32, TMP)
        masks = at("masks", [P, len(LEVELS), CH // 2], F32, TMP)

        names = ["xr", "xc", "ra", "ts", "ix", "gg"]
        places = [[B_HI + 4 * KIB * n for n in range(4)] + [KV, KV + 4 * KIB],
                  [B_LO + 4 * KIB * n for n in range(4)] + [KV + 8 * KIB, KV + 12 * KIB]]
        lru = [{n: at(f"lru_{n}{s}", [P, S], F32, places[s][i]) for i, n in enumerate(names)}
               for s in range(2)]
        og = at("og", [P, GLA_HEADS, S], F32, B_HI)
        kk = at("kk", [P, 2, S], F32, B_LO)
        qq = at("qq", [P, 2, S], F32, B_LO + 8 * KIB)
        v_tok = at("v_tok", [P, NC, 512], F32, X)
        bsum = at("bsum", [P, 2, S], F32, X + 16 * KIB)
        states = at("states", [P, NC, 2, P], F32, X + 24 * KIB)
        mem_raw = at("mem_raw", [P, KT, N_MEM], F32, X + 24 * KIB)
        gk_a = at("gk_a", [P, 2, S], F32, X)
        gk_b = at("gk_b", [P, 2, S], F32, X + 8 * KIB)
        gk_lr = at("gk_lr", [GLA_LOWRANK, S], F32, X + 24 * KIB)
        v_feat = at("v_feat", [P, 4, S], F32, B_HI)
        m_hi = at("m_hi", [P, KT, N_MEM], F32R, KV)
        m_lo = at("m_lo", [P, KT, N_MEM], F32R, KV + 8 * KIB)
        xk_new = at("xk_new", [P, KT, N_MEM], F32, A_HI)
        xk_tok = at("xk_tok", [P, 2, D], F32, A_LO + 24 * KIB)
        xv_new = at("xv_new", [P, 2, D], F32, A_HI + 8 * KIB)
        lev = [at(f"lev{n}", [P, 2, S], F32, place)
               for n, place in enumerate((A_HI + 16 * KIB, A_HI + 24 * KIB, X + 24 * KIB))]
        sT = at("sT", [P, 2, NC, 2, P], F32, A_LO)
        m_acc = at("m_acc", [P, N_MEM], F32, TMP + 2 * KIB)
        qe = at("qe", [P, 2, S], F32, A_LO + 16 * KIB)
        kd_tok = at("kd_tok", [P, NC, 2 * P], F32, A_LO + 24 * KIB)
        o_sb = [at(f"o_sb{n}", [P, 512], F32, A_HI + (16 + 2 * n) * KIB) for n in range(4)]
        o_sq = [at(f"o_sq{n}", [P, 512], F32, A_HI + (24 + 2 * n) * KIB) for n in range(2)]
        o_dg = [at(f"o_dg{n}", [P, GLA_HEADS, P], F32, A_HI + (28 + 2 * n) * KIB) for n in range(2)]
        xk = at("xk", [P, KT, N_MEM], F32, KV)
        xv = at("xv", [P, 2, D], F32, KV + 8 * KIB)
        xk_hi = at("xk_hi", [P, KT, N_MEM], F32R, A_HI)
        xk_lo = at("xk_lo", [P, KT, N_MEM], F32R, A_HI + 8 * KIB)
        xv_hi = at("xv_hi", [P, 2, D], F32R, A_HI + 16 * KIB)
        xv_lo = at("xv_lo", [P, 2, D], F32R, A_HI + 24 * KIB)
        pr = [at(f"pr{n}", [P, 2, N_MEM], F32, A_LO + 2 * n * KIB) for n in range(4)]
        pT_hi = [at(f"pT_hi{n}", [P, 2, S], F32R, (A_LO + 8 * KIB, KV)[n]) for n in range(2)]
        pT_lo = [at(f"pT_lo{n}", [P, 2, S], F32R, (A_LO + 16 * KIB, KV + 8 * KIB)[n]) for n in range(2)]
        f_hi = [at(f"f_hi{n}", [P, GROUP, S], F32R, B_HI + 8 * n * KIB) for n in range(2)]
        f_lo = [at(f"f_lo{n}", [P, GROUP, S], F32R, B_HI + (16 + 8 * n) * KIB) for n in range(2)]
        gate = at("gate", [P, S], F32, B_LO)
        conv = at("conv", [P, S], F32, B_LO + 4 * KIB)
        up = at("up", [P, S], F32, B_LO + 8 * KIB)
        facc = at("facc", [P, S], F32, B_LO + 12 * KIB)
        frs = at("frs", [P, S], F32, B_LO + 16 * KIB)
        fdiag = at("fdiag", [P, NC, P], F32, B_LO + 16 * KIB)
        fsq = at("fsq", [P, 4, HALF], F32, B_LO)

        ident = const("ident", [P, P])
        ones = const("ones", [P, P])
        par = const("par", [P, N_PARAMS])
        wgk = const("wgk", [GLA_LOWRANK, 2 * P])
        bd = const("bd", [P, 2, LRU_TILES, P])
        eps = const("eps", [P, 1])
        small = const("small", [P, 12, LRU_TILES])
        dec = const("dec", [P, 2, NC])
        ssum = const("ssum", [P, NC])
        srec = const("srec", [P, NC])
        m_std = const("m_std", [P, 2])
        m_rec = const("m_rec", [P, 2])
        sel = const("sel", [P, 2])
        o_std = const("o_std", [P, NC, GLA_HEADS])
        o_rec = const("o_rec", [P, NC, GLA_HEADS])
        nmax = const("nmax", [P, 16, 2])
        psum_p = const("psum_p", [P, 16, 2])
        prec = const("prec", [P, 16, 2])

        def col(name, i=0):
            return par[:, PARAMS[name] + i:PARAMS[name] + i + 1]

        ps = ctx.enter_context(nc.psum_tensor("ps", [P, 8, HALF], F32))
        main = [ps[:, 0:2, :], ps[:, 2:4, :]]
        aux = [ps[:, 4:6, :], ps[:, 6:8, :]]

        score_banks = (4, 5, 2)
        turn_banks = (6, 7, 3)
        att_pair = [main[1] if t == KT - 2 else main[0] for t in range(KT)]

        def flat(pair):
            return pair.rearrange("p b n -> p (b n)")

        def sem(name):
            return ctx.enter_context(nc.semaphore(name))

        s_raw = [sem(f"raw_loaded{n}") for n in range(RING)]
        s_taken = sem("slot_taken")
        s_whi = sem("w_hi_done")
        s_split = sem("w_split")
        s_par = sem("params_loaded")
        s_x = [sem(f"x_loaded{n}") for n in range(KT)]
        s_xr = [sem(f"x_reloaded{n}") for n in range(KT)]
        s_mem = sem("mem_loaded")
        s_bd = sem("gate_weights_loaded")
        s_cst = sem("constants_made")
        s_bd0 = sem("gate_weights_zeroed")
        s_ones = sem("ones_made")
        s_full = sem("main_full")
        s_evac = sem("main_evacuated")
        s_dve = sem("dve_steps")
        s_act = sem("act_steps")
        s_hhi = sem("h_hi_done")
        s_sq = sem("squares_done")
        s_h = sem("h_ready")
        s_acc = sem("squares_summed")
        s_ssq = sem("ssq_ready")
        s_std = sem("std_ready")
        s_rstd = sem("rstd_ready")
        s_dg = sem("diag_ready")
        s_bc = sem("rstd_broadcast")
        s_xc = sem("xc_ready")
        s_gate = sem("gates_ready")
        s_sig = sem("sigmoids_done")
        s_rec = sem("lru_factors_ready")
        s_gelu = sem("gelu_done")
        s_y = sem("y_lru_ready")
        s_yhi = sem("y_lru_hi_done")
        s_ylo = sem("y_mix_lru_ready")
        s_sp = sem("softplus_exp")
        s_spd = sem("softplus_ready")
        s_z = sem("gate_logits_ready")
        s_lse = sem("log1p_exp_ready")
        s_b = sem("log_gates_summed")
        s_silu = sem("silu_done")
        s_vt = sem("v_turned")
        s_vtok = sem("v_token_ready")
        s_mhi = sem("mem_hi_done")
        s_mh = sem("mem_ready")
        s_wgk = sem("w_gk_loaded")
        s_mq = sem("mem_squares")
        s_msq = sem("mem_squares_summed")
        s_mssq = sem("mem_ssq")
        s_mstd = sem("mem_std")
        s_ld = sem("level_exponents")
        s_le = sem("level_exps")
        s_lt = sem("level_ready")
        s_lp = sem("level_scores")
        s_lc = sem("level_scores_kept")
        s_qk = sem("q_times_k")
        s_qks = sem("q_dot_k")
        s_qe = sem("q_decayed")
        s_xkt = sem("memory_keys_turned")
        s_xkc = sem("memory_keys_copied")
        s_kvc = sem("memory_moved")
        s_ke = sem("k_exps")
        s_kd = sem("k_decayed")
        s_kt = sem("k_turned")
        s_ktok = sem("k_token_ready")
        s_dec = sem("chunk_decay")
        s_delta = sem("state_products")
        s_st = sem("states_ready")
        s_o = sem("o_ready")
        s_oc = sem("o_copied")
        s_ossq = sem("o_ssq")
        s_ostd = sem("o_std")
        s_odg = sem("o_diag")
        s_obc = sem("o_broadcast")
        s_oy = sem("y_gla_ready")
        s_oyhi = sem("y_gla_hi")
        s_oylo = sem("y_mix_gla_ready")
        s_xqh = sem("xq_hi")
        s_xq = sem("xq_ready")
        s_kvh = sem("kv_hi")
        s_kv = sem("kv_ready")
        s_sc = sem("scores_ready")
        s_mx = sem("max_ready")
        s_ex = sem("exps_ready")
        s_pn = sem("p_normalised")
        s_pt = sem("p_turned")
        s_pth = sem("p_turned_hi")
        s_ptl = sem("p_turned_ready")
        s_ath = sem("att_hi")
        s_gu = sem("gate_up_full")
        s_gue = sem("gate_up_evacuated")
        s_cv = sem("conv_ready")
        s_sl = sem("ffn_silu_done")
        s_f = sem("f_product")
        s_fh = sem("f_hi")
        s_fr = sem("f_ready")
        s_out = sem("out_full")
        s_oute = sem("out_added")
        s_fsq = sem("final_squares")
        s_facc = sem("final_summed")
        s_xg = sem("x_times_gain_final")
        s_yf = sem("y_final_ready")
        s_yfp = sem("y_final_ready_pool")
        s_store = sem("y_stored")

        pieces = [(i, i % KT, slice(i // KT * HALF, (i // KT + 1) * HALF)) for i in range(2 * KT)]
        by_pool = (5, 3)

        def added(i):
            return i - i // KT

        block = ctx.enter_context(nc.Block())

        @block.sync
        def _(sp):
            sp.dma_start(par[:, :], params).then_inc(s_par, 16)
            sp.dma_start(x[:, 0, :], xT[0, :, :]).then_inc(s_x[0], 16)
            sp.dma_start(raw[:, 0, :], wstream[0, :, :]).then_inc(s_raw[0], 16)
            sp.dma_start(raw[:, 1, :], wstream[1, :, :]).then_inc(s_raw[1], 16)
            for t in range(2, KT, 2):
                sp.dma_start(x[:, t, :], xT[t, :, :]).then_inc(s_x[t], 16)
            assert N_SLOTS % 2 == 1
            with sp.Fori(1, N_SLOTS // 2) as i:
                for j in range(RING):
                    sp.wait_ge(s_split, i * 2 + (j - 1))
                    sp.dma_start(raw[:, j, :], wstream[i * 2 + j, :, :]).then_inc(s_raw[j], 16)
            sp.wait_ge(s_split, N_SLOTS - 2)
            sp.dma_start(raw[:, 0, :], wstream[N_SLOTS - 1, :, :]).then_inc(s_raw[0], 16)
            done = 0
            for i, t, hs in pieces:
                if t < by_pool[i // KT]:
                    done += 1
                    sp.wait_ge(s_yfp, done)
                    sp.dma_start(yT[t, :, hs], x[:, t, hs]).then_inc(s_store, 16)
            sp.wait_ge(s_store, 16 * len(pieces))

        @block.gpsimd
        def _(pool):
            made = 0
            pool.memset(bd[:, :, :, :], 0.0).then_inc(s_bd0, 1)
            pool.memset(ones[:, :], 1.0).then_inc(s_ones, 1)
            pool.memset(eps[:, :], EPS).then_inc(s_ones, 1)
            pool.memset(ident[:, :], 0.0).then_inc(s_cst, 1)
            pool.wait_ge(s_cst, 1)
            pool.affine_select(out=ident[:, :], in_=ident[:, :], compare_op=ALU.not_equal, fill=1.0,
                               base=0, pattern=[[-1, P]], channel_multiplier=1).then_inc(s_cst, 1)
            made = 2

            def split(n, slot_of, freed=None):
                pool.wait_ge(s_raw[slot_of], (n // 2 if isinstance(n, int) else n) * 16 + 16)
                if freed is not None:
                    pool.wait_ge(*freed)
                pool.sem_inc(s_taken, 1)
                pool.tensor_scalar(w_hi[:, slot_of, :], raw[:, slot_of, :], 1.0, 1.0, ALU.mult,
                                   ALU.mult).then_inc(s_whi, 1)

            def rest(slot_of, count):
                pool.wait_ge(s_whi, count)
                pool.tensor_tensor(w_lo[:, slot_of, :], raw[:, slot_of, :],
                                   w_hi[:, slot_of, :].bitcast(F32), ALU.subtract).then_inc(s_split, 1)

            def slot(n, freed=None):
                split(n, n % RING, freed)
                rest(n % RING, n + 1)

            slot(0)
            slot(1)
            pool.memset(masks[:, :, :], 1.0).then_inc(s_cst, 1)
            pool.memset(sel[:, :], 0.0).then_inc(s_cst, 1)
            pool.wait_ge(s_cst, made + 2)
            pool.memset(sel[0:DK, 0:1], 1.0).then_inc(s_cst, 1)
            pool.memset(sel[DK:P, 1:2], 1.0).then_inc(s_cst, 1)
            made += 4
            pool.wait_ge(s_cst, made)
            for i, m in enumerate(LEVELS):
                mask = masks[:, i, :].rearrange("p (n m) -> p n m", m=m)
                pool.affine_select(out=mask, in_=mask, compare_op=ALU.is_ge, fill=0.0, base=0,
                                   pattern=[[-2 * m, CH // (2 * m)], [0, m]], channel_multiplier=1)\
                    .then_inc(s_cst, 1)
                pool.wait_ge(s_cst, made + 1)
                pool.affine_select(out=mask, in_=mask, compare_op=ALU.is_ge, fill=0.0, base=m - 1,
                                   pattern=[[2 * m, CH // (2 * m)], [0, m]], channel_multiplier=-1)\
                    .then_inc(s_cst, 1)
                made += 2
                pool.wait_ge(s_cst, made)
            last_xq = SLOT_XO - 1
            with pool.Fori(1, (last_xq + 1) // 2) as i:
                for j in range(RING):
                    split(i, j, (s_full, i * 2 + (j - 1)))
                    rest(j, i * 2 + (j + 1))
            for n in range((last_xq + 1) // 2 * 2, SLOT_FFN + 2):
                used = n - 2 + 1
                if n - 2 >= SLOT_XO:
                    used += KT
                slot(n, (s_full, used))
            slot(SLOT_FFN + 2, (s_gu, 1))
            slot(SLOT_FFN + 3, (s_gu, 2))
            first = SLOT_FFN + 4
            for n, freed in enumerate(((s_gu, 3), (s_gu, 4), (s_gu, 5), (s_gu, 6), (s_out, 4), (s_gu, 7))):
                slot(first + n, freed)
            with pool.Fori(2, GROUPS) as g:
                for n in range(6):
                    freed = ((s_gu, g * 4), (s_out, g * 8 - 8), (s_gu, g * 4 + 1), (s_gu, g * 4 + 2),
                             (s_out, g * 8 - 4), (s_gu, g * 4 + 3))[n]
                    start = first - 6 + n
                    place = start % RING
                    split(g * 3 + start // 2, place, freed)
                    rest(place, g * 6 + (start + 1))
            slot(N_SLOTS - 2, (s_gu, 4 * GROUPS))
            slot(N_SLOTS - 1, (s_out, 8 * (GROUPS - 1)))
            for i, t, hs in pieces:
                if t < by_pool[i // KT]:
                    pool.wait_ge(s_xg, i + 1)
                    pool.wait_ge(s_rstd, 4 + i // KT)
                    pool.tensor_tensor(x[:, t, hs], x[:, t, hs], frs[:, hs], ALU.mult).then_inc(s_yfp, 1)

        @block.tensor
        def _(pe):
            def step_of(ring, out, k, hi, lo, first, last):
                ws = slice(k * P, (k + 1) * P)
                for m, (w, h) in enumerate(((w_hi, hi), (w_hi, lo), (w_lo, hi))):
                    for b in range(2):
                        mm = pe.matmul(out[:, b, :], w[:, ring, ws], h[:, k, b * HALF:(b + 1) * HALF],
                                       start=first and m == 0, stop=last and m == 2)
                return mm

            def project(ring, out, hi, lo, order=range(KT), width=S, before=None, cols=P):
                halves = [(c, min(HALF, width)) for c in range(0, width, HALF)]
                first = True
                for n, k in enumerate(order):
                    if before:
                        before(k)
                    wh, wl = (w[:, ring, k * P:k * P + cols] for w in (w_hi, w_lo))
                    for m, (w, h) in enumerate(((wh, hi), (wh, lo), (wl, hi))):
                        for b, (c, size) in enumerate(halves):
                            mm = pe.matmul(out[0:cols, b, 0:size], w, h[:, k, c:c + size],
                                           start=first, stop=(n == len(order) - 1 and m == 2))
                        first = False
                return mm

            def ssq(src, out, n):
                for c in range(n):
                    mm = pe.matmul(out[:, c:c + 1], src[:, c * P:(c + 1) * P], ones[:, 0:1],
                                   start=True, stop=True)
                return mm

            def spread(dg, out, n):
                for c in range(0, n, 4):
                    w = min(4, n - c)
                    mm = pe.matmul(out[:, c // 4, 0:w * P], ones[:, :],
                                   dg[:, c:c + w, :].rearrange("p c n -> p (c n)"), start=True, stop=True)
                return mm

            def ready(n):
                pe.wait_ge(s_split, n + 1)
                if n >= 2:
                    u = n if n < SLOT_XO else n + KT
                    pe.wait_ge(s_evac, u - 1)

            def norm_matmuls(k):
                pe.wait_ge(s_acc, KT * (k + 1))
                ssq(acc, aux[0][:, 0, :], NC).then_inc(s_ssq, 1)

            def norm_spread(k):
                pe.wait_ge(s_dg, k + 1)
                spread(diag, aux[1], NC).then_inc(s_bc, 1)

            def tile_ready(k):
                return lambda q: pe.wait_ge(s_h, KT * k + q + 1)

            def spread_at(k):
                return lambda q: norm_spread(k) if q == KT // 2 else None

            def gates(t):
                pe.wait_ge(s_xc, t + 1)
                if t:
                    pe.wait_ge(s_sig, 2 * t)
                for g in range(2):
                    for h in range(2):
                        mm = pe.matmul(aux[g][:, h, :], bd[:, g, t, :],
                                       lru[t % 2]["xc"][:, h * HALF:(h + 1) * HALF], start=True, stop=True)
                mm.then_inc(s_gate, 1)

            pe.wait_ge(s_ones, 2)
            for k in range(KT):
                pe.wait_ge(s_h, k + 1)
                for n in range(2):
                    ready(n)
                    if k == KT - 1 and n == 1:
                        norm_matmuls(0)
                    mm = step_of(n, main[n], k, a_hi, a_lo, k == 0, k == KT - 1)
                    if k == KT - 1:
                        mm.then_inc(s_full, 1)
            norm_spread(0)
            for n in range(2, 2 * LRU_TILES):
                ready(n)
                project(n % RING, main[n % 2], a_hi, a_lo).then_inc(s_full, 1)
                if n % 2 == 0:
                    if n == 2:
                        pe.wait_ge(s_bd, 64)
                    if n == 2:
                        pe.wait_ge(s_rstd, 1)
                    gates(n // 2 - 1)
            n = SLOT_GK
            ready(n)
            project(n % RING, main[n % 2], a_hi, a_lo, cols=GLA_LOWRANK).then_inc(s_full, 1)
            gates(LRU_TILES - 1)
            for n in range(SLOT_KQ, SLOT_KQ + 4):
                ready(n)
                project(n % RING, main[n % 2], a_hi, a_lo).then_inc(s_full, 1)
                if n == SLOT_KQ:
                    pe.wait_ge(s_evac, SLOT_GK + 1)
                    pe.wait_ge(s_wgk, 16)
                    pe.wait_ge(s_sig, 2 * LRU_TILES)
                    for j in range(2):
                        for h in range(2):
                            mm = pe.matmul(aux[j][:, h, :], wgk[:, j * P:(j + 1) * P],
                                           gk_lr[:, h * HALF:(h + 1) * HALF], start=True, stop=True)
                    mm.then_inc(s_z, 1)
            assert SLOT_VO % 2 == 1
            with pe.Fori(0, 2) as i:
                for j in range(2):
                    n = SLOT_VO + j
                    pe.wait_ge(s_split, i * 2 + (n + 1))
                    pe.wait_ge(s_evac, i * 2 + (n - 1))
                    project(n % RING, main[n % 2], a_hi, a_lo).then_inc(s_full, 1)
            for n in range(SLOT_VO + 4, SLOT_VO + 8):
                ready(n)
                project(n % RING, main[n % 2], a_hi, a_lo).then_inc(s_full, 1)
                if n == SLOT_VO + 4:
                    pe.wait_ge(s_b, 2 * NC)
                    pe.wait_ge(s_evac, SLOT_VO + 4)
                    for c in range(NC):
                        if c >= 4:
                            pe.wait_ge(s_vtok, c - 3)
                        for h in range(4):
                            mm = pe.transpose(ps[:, 4 + c % 4, h * P:(h + 1) * P],
                                              v_feat[:, h, c * P:(c + 1) * P], ident[:, :])
                        mm.then_inc(s_vt, 1)
                if n == SLOT_VO + 6:
                    pe.wait_ge(s_msq, 1)
                    ssq(m_acc, ps[:, 4, :], 2).then_inc(s_mssq, 1)
                    pe.wait_ge(s_qk, 1)

            def memory(i):
                n = SLOT_MEM + i
                half, part = divmod(i, 4)
                out = main[(half + 1) % 2]
                pe.wait_ge(s_split, n + 1)
                if i == 0:
                    pe.wait_ge(s_mh, 1)
                if part == 0:
                    pe.wait_ge(s_evac, SLOT_MEM - 1 + half if half < 2 else SLOT_MEM + 4 * (half - 1))
                if i == 12:
                    pe.wait_ge(s_xkc, 2)
                for mt in range(2):
                    for k in range(2):
                        ms = slice(mt * P, (mt + 1) * P)
                        ws = slice(k * HALF, (k + 1) * HALF)
                        for p, (m, w) in enumerate(((m_hi, w_hi), (m_hi, w_lo), (m_lo, w_hi))):
                            mm = pe.matmul(out[:, mt, :], m[:, 2 * part + k, ms], w[:, n % RING, ws],
                                           start=(part == 0 and k == 0 and p == 0),
                                           stop=(part == 3 and k == 1 and p == 2))
                mm.then_inc(s_full, 1)

            def turn_keys(part):
                if part == 0:
                    pe.wait_ge(s_evac, SLOT_MEM + 8)
                else:
                    pe.wait_ge(s_xkc, part)
                for t in range(4):
                    for mt in range(2):
                        at_ = (t % 2) * 2 + mt
                        mm = pe.transpose(main[0][:, t // 2, at_ * P:(at_ + 1) * P],
                                          xk_tok[:, mt, (4 * part + t) * P:(4 * part + t + 1) * P], ident[:, :])
                mm.then_inc(s_xkt, 1)

            for c in range(NC):
                for j in range(2):
                    at_ = (c * 2 + j) * 2
                    mm = pe.matmul(ps[:, 7, at_:at_ + 2], lev[2][:, j, c * CH:(c + 1) * CH], sel[:, :],
                                   start=True, stop=True)
            mm.then_inc(s_qks, 1)
            memory(0)
            memory(1)
            kd = lev[len(LEVELS) % 3]
            unit = 0
            for L in range(len(LEVELS)):
                if L < len(LEVELS) - 1:
                    memory(2 * L + 2)
                    memory(2 * L + 3)
                else:
                    memory(14)
                    memory(15)
                    pe.wait_ge(s_kd, 1)
                    pe.wait_ge(s_evac, SLOT_MIX)
                    for b in range(4):
                        for c in range(2 * b, 2 * b + 2):
                            for j in range(2):
                                mm = pe.transpose(ps[:, b, ((c % 2) * 2 + j) * P:((c % 2) * 2 + j + 1) * P],
                                                  kd[:, j, c * CH:(c + 1) * CH], ident[:, :])
                        mm.then_inc(s_kt, 1)
                if L in (3, 4):
                    turn_keys(L - 3)
                pe.wait_ge(s_lt, L + 1)
                if L == 0:
                    pe.wait_ge(s_lc, 1)
                    pe.wait_ge(s_mstd, 1)
                src = lev[L % 3]
                for c in range(0, NC, 2):
                    for odd in range(2):
                        if unit + odd >= 4:
                            pe.wait_ge(s_lc, unit + odd - 2)
                    for i in range(4):
                        cs = slice((c + i // 2) * CH, (c + i // 2 + 1) * CH)
                        for odd in range(2):
                            rows = slice(DK * odd, DK * odd + DK)
                            mm = pe.matmul(ps[:, 4 + (unit + odd) % 4, i * P:(i + 1) * P],
                                           src[rows, i % 2, cs], src[rows, i % 2, cs], start=True, stop=True)
                            if i == 3:
                                mm.then_inc(s_lp, 1)
                    unit += 2
            for c in range(NC - 1):
                if c % 2 == 0:
                    pe.wait_ge(s_ktok, 4)
                for h in range(GLA_HEADS):
                    rows = slice(DK * (h % 2), DK * (h % 2) + DK)
                    at_ = (c % 2) * 2 + h // 2
                    mm = pe.matmul(ps[rows, c // 2, at_ * P:(at_ + 1) * P],
                                   kd_tok[:, c, h * DK:(h + 1) * DK], v_tok[:, c, h * P:(h + 1) * P],
                                   start=True, stop=True)
                if c % 2 or c == NC - 2:
                    mm.then_inc(s_delta, 1)
            pe.wait_ge(s_lc, 1 + unit)
            pe.wait_ge(s_qe, 2)
            for c in range(NC + 2):
                if c < NC:
                    if c >= 1:
                        pe.wait_ge(s_st, c)
                    if c >= 2:
                        pe.wait_ge(s_oc, 2 * (c - 1))
                    out = ps[:, 4 + c % 2 * 2:6 + c % 2 * 2, :]
                    for h in range(GLA_HEADS):
                        rows, j = slice(DK * (h % 2), DK * (h % 2) + DK), h // 2
                        hs, js = slice(h * P, (h + 1) * P), slice(j * P, (j + 1) * P)
                        if c:
                            pe.matmul(out[:, h % 2, js], states[rows, c, j, :], qe[rows, j, c * CH:(c + 1) * CH],
                                      start=True, stop=False)
                        mm = pe.matmul(out[:, h % 2, js], v_tok[:, c, hs], sT[:, h % 2, c, h // 2, :], start=(c == 0), stop=True)
                    mm.then_inc(s_o, 1)
                if 1 <= c <= NC:
                    pe.wait_ge(s_oc, 2 * c)
                    if c == 1:
                        pe.wait_ge(s_st, NC - 1)
                    else:
                        pe.wait_ge(s_ostd, c - 1)
                    for h in range(GLA_HEADS):
                        at_ = (c - 1) * GLA_HEADS + h
                        mm = pe.matmul(ps[:, 3, at_:at_ + 1], o_sq[(c - 1) % 2][:, h * P:(h + 1) * P],
                                       ones[:, 0:1], start=True, stop=True)
                    mm.then_inc(s_ossq, 1)
                if c >= 2:
                    pe.wait_ge(s_odg, c - 1)
                    if c >= 4:
                        pe.wait_ge(s_oy, c - 3)
                    pe.matmul(ps[:, c % 2, :], ones[:, :],
                              o_dg[c % 2][:, :, :].rearrange("p c n -> p (c n)"),
                              start=True, stop=True).then_inc(s_obc, 1)

            order = list(range(4, 8)) + list(range(4))
            pe.wait_ge(s_ostd, NC)

            def y_tiles(k):
                if k == 4:
                    pe.wait_ge(s_ylo, LRU_TILES)
                if k == 0:
                    pe.wait_ge(s_oylo, NC)

            ready(SLOT_MIX)
            n = SLOT_MIX
            project(n % RING, main[n % 2], b_hi, b_lo, order=order, before=y_tiles).then_inc(s_full, 1)
            ready(n + 1)
            project((n + 1) % RING, main[(n + 1) % 2], b_hi, b_lo, order=order).then_inc(s_full, 1)
            with pe.Fori(1, KT // 2) as i:
                for j in range(2):
                    pe.wait_ge(s_split, i * 2 + (n + j + 1))
                    pe.wait_ge(s_evac, i * 2 + (n + j - 1))
                    project((n + j) % RING, main[(n + j) % 2], b_hi, b_lo, order=order).then_inc(s_full, 1)

            def after_norm(first, k, tiles):
                for n in range(first, first + 2):
                    ready(n)
                    before = tile_ready(k) if n == first else spread_at(k)
                    project(n % RING, main[n % 2], a_hi, a_lo, before=before).then_inc(s_full, 1)
                    if n == first:
                        norm_matmuls(k)
                with pe.Fori(1, tiles // 2) as i:
                    for j in range(2):
                        pe.wait_ge(s_split, i * 2 + (first + j + 1))
                        pe.wait_ge(s_evac, i * 2 + (first + j - 1))
                        project((first + j) % RING, main[(first + j) % 2], a_hi, a_lo).then_inc(s_full, 1)

            after_norm(SLOT_XQ, 1, KT)

            UNITS = XHEADS * 4

            def scores(u):
                h, b = divmod(u, 4)
                if b == 0:
                    pe.wait_ge(s_kv, 2 if h else 1)
                    pe.wait_ge(s_xq, 2 * h + 2)
                if u == 2:
                    pe.wait_ge(s_evac, SLOT_XO - 1)
                if u >= 3:
                    pe.wait_ge(s_ex, 2 * (u - 2))
                for i in range(2):
                    ts = slice((2 * b + i) * P, (2 * b + i + 1) * P)
                    for d in range(2):
                        t = 2 * h + d
                        for p, (q, k) in enumerate(((b_hi, xk_hi), (b_hi, xk_lo), (b_lo, xk_hi))):
                            mm = pe.matmul(ps[:, score_banks[u % 3], i * N_MEM:(i + 1) * N_MEM], q[:, t, ts],
                                           k[:, t, :], start=(d == 0 and p == 0), stop=(d == 1 and p == 2))
                mm.then_inc(s_sc, 1)

            def turn(u):
                pe.wait_ge(s_pn, u + 1)
                if u >= 3:
                    pe.wait_ge(s_ptl, u - 2)
                for m in range(2):
                    for i in range(2):
                        mm = pe.transpose(ps[:, turn_banks[u % 3], (2 * m + i) * P:(2 * m + i + 1) * P],
                                          pr[u % 4][:, i, m * P:(m + 1) * P], ident[:, :])
                mm.then_inc(s_pt, 1)

            def values(t):
                h = t // 2
                pe.wait_ge(s_kv, 4)
                pe.wait_ge(s_ptl, 4 * h + 4)
                if t != KT - 2:
                    pe.wait_ge(s_evac, MAIN_ATT + min(t, KT - 2))
                for m in range(2):
                    ws = slice(t * P, (t + 1) * P)
                    for p, (w, q) in enumerate(((xv_hi, pT_hi[h % 2]), (xv_hi, pT_lo[h % 2]),
                                                (xv_lo, pT_hi[h % 2]))):
                        for b in range(2):
                            mm = pe.matmul(att_pair[t][:, b, :], w[:, m, ws],
                                           q[:, m, b * HALF:(b + 1) * HALF],
                                           start=(m == 0 and p == 0), stop=(m == 1 and p == 2))
                mm.then_inc(s_full, 1)

            for u in range(3):
                scores(u)
            for u in range(UNITS):
                turn(u)
                if u + 3 < UNITS:
                    scores(u + 3)
                if u > 4 and u % 2:
                    values((u - 5) // 2)
            values(KT - 2)
            values(KT - 1)

            n = SLOT_XO
            ready(n)
            project(n % RING, main[(n + KT) % 2], b_hi, b_lo,
                    before=lambda k: pe.wait_ge(s_evac, MAIN_ATT + k + 1)).then_inc(s_full, 1)
            ready(n + 1)
            project((n + 1) % RING, main[(n + 1) % 2], b_hi, b_lo).then_inc(s_full, 1)
            with pe.Fori(1, KT // 2) as i:
                for j in range(2):
                    pe.wait_ge(s_split, i * 2 + (n + j + 1))
                    pe.wait_ge(s_evac, i * 2 + (n + KT + j - 1))
                    project((n + j) % RING, main[(n + j) % 2], b_hi, b_lo).then_inc(s_full, 1)

            def out_part(ring, f, waits):
                for m in range(4):
                    if waits[m] is not None:
                        pe.wait_ge(s_oute, waits[m])
                    for k in range(GROUP):
                        ws = slice(k * HALF + m * P, k * HALF + (m + 1) * P)
                        for p, (w, q) in enumerate(((w_hi, f_hi[f]), (w_hi, f_lo[f]), (w_lo, f_hi[f]))):
                            for b in range(2):
                                mm = pe.matmul(aux[m % 2][:, b, :], w[:, ring, ws],
                                               q[:, k, b * HALF:(b + 1) * HALF],
                                               start=(k == 0 and p == 0), stop=(k == GROUP - 1 and p == 2))
                    mm.then_inc(s_out, 1)

            for q in range(4):
                n = SLOT_FFN + q
                pe.wait_ge(s_split, n + 1)
                pe.wait_ge(*((s_evac, MAIN_END - 1 + q) if q < 2 else (s_gue, q - 1)))
                before = (tile_ready(2), spread_at(2), None, None)[q]
                project(n % RING, main[(q + 1) % 2], a_hi, a_lo, before=before).then_inc(s_gu, 1)
                if q == 0:
                    norm_matmuls(2)

            def group(g, f, first):
                start = SLOT_FFN - 2
                for part in range(2):
                    for q in range(2):
                        n = start + 3 * part + q
                        pe.wait_ge(s_split, g * 6 + (n + 1))
                        pe.wait_ge(s_gue, g * 4 + (2 * part + q - 1))
                        project(n % RING, main[1 - q], a_hi, a_lo).then_inc(s_gu, 1)
                    n = start + 3 * part + 2
                    pe.wait_ge(s_split, g * 6 + (n + 1))
                    if part == 0:
                        pe.wait_ge(s_fr, g * 2)
                    waits = [g * 8 + (4 * part + m - 9) for m in range(4)]
                    if first and part == 0:
                        waits[0:2] = [None, None]
                    out_part(n % RING, f, waits)

            def final_sums(half):
                if half == 0:
                    pe.wait_ge(s_gue, 4 * GROUPS)
                pe.wait_ge(s_facc, added((half + 1) * KT - 1))
                ssq(facc[:, half * HALF:(half + 1) * HALF], ps[:, half, :], NC // 2).then_inc(s_ssq, 1)

            def final_spread(half):
                pe.wait_ge(s_dg, 4 + half)
                spread(fdiag[:, half * 4:half * 4 + 4, :], ps[:, 2 + half:3 + half, :], NC // 2).then_inc(s_bc, 1)

            pe.wait_ge(s_rstd, 3)
            group(1, 0, True)
            assert GROUPS % 2 == 1
            group(2, 1, False)
            with pe.Fori(1, GROUPS // 2) as i:
                for j in range(2):
                    group(i * 2 + (1 + j), j, False)
            f = (GROUPS - 1) % 2
            pe.wait_ge(s_fr, 2 * GROUPS)
            for i, t, hs in pieces:
                if i in (0, 4):
                    pe.wait_ge(s_split, N_SLOTS - 1 + i // 4)
                if i < 4:
                    pe.wait_ge(s_oute, 8 * (GROUPS - 1) - 1 + i // 2)
                else:
                    pe.wait_ge(s_oute, 8 * (GROUPS - 1) + i - 3)
                for k in range(GROUP):
                    ring = (N_SLOTS - 2 + t // 4) % RING
                    ws = slice(k * HALF + t % 4 * P, k * HALF + (t % 4 + 1) * P)
                    for p, (w, q) in enumerate(((w_hi, f_hi[f]), (w_hi, f_lo[f]), (w_lo, f_hi[f]))):
                        mm = pe.matmul(ps[:, 4 + i % 4, :], w[:, ring, ws], q[:, k, hs],
                                       start=(k == 0 and p == 0), stop=(k == GROUP - 1 and p == 2))
                mm.then_inc(s_out, 1)
                if i == KT + 1:
                    final_sums(0)
                if i == KT + 5:
                    final_spread(0)
            final_sums(1)
            final_spread(1)

        @block.scalar
        def _(act):
            for t in range(1, KT, 2):
                act.dma_start(x[:, t, :], xT[t, :, :]).then_inc(s_x[t], 16)
            act.wait_ge(s_bd0, 1)
            for g, w in enumerate((w_rg_a, w_rg_x)):
                for h in range(2):
                    rows = slice(h * LRU_BLOCK, (h + 1) * LRU_BLOCK)
                    act.dma_start(bd[rows, g, :, rows], w[h, :, :, :]).then_inc(s_bd, 16)
            act.dma_start(wgk[:, :], w_gk).then_inc(s_wgk, 16)
            step = Steps(act, s_act)

            act.wait_ge(s_ones, 2)
            step(act.activation(small[:, 0, 0:1], eps[:, :], ACT.Square))
            act.wait_ge(s_par, 16)
            def h_tile(gain, xs, hi, count, acc_done, where):
                act.activation(hi, xs, ACT.Identity, scale=gain).then_inc(s_hhi, 1)
                if acc_done is not None:
                    act.wait_ge(s_acc, acc_done)
                act.activation(where, xs, ACT.Square).then_inc(s_sq, 1)

            for t in range(KT):
                act.wait_ge(s_x[t], 16)
                h_tile(col("g_mix", t), x[:, t, :], a_hi[:, t, :], t, t - 1 if t >= 2 else None,
                       flat(aux[t % 2]))

            def root(k):
                act.wait_ge(s_ssq, k + 1)
                act.activation(ssum[:, :], aux[0][:, 0, 0:NC], ACT.Sqrt, scale=1.0 / D,
                               bias=eps[:, 0:1]).then_inc(s_std, 1)

            root(0)
            step(act.activation(small[:, 0, :], par[:, PARAMS["lru_lambda"]:PARAMS["lru_lambda"] + 4], ACT.Abs))
            step.settle()
            act.activation(small[:, 1, :], small[:, 0, :], ACT.Exp, scale=-1.0).then_inc(s_sp, 1)

            def lru_tile(t):
                b = lru[t % 2]
                act.wait_ge(s_gate, t + 1)
                if t == 0:
                    act.wait_ge(s_spd, 1)
                if t >= 2:
                    act.wait_ge(s_ylo, t - 1)
                act.activation(b["ra"][:, :], flat(aux[0]), ACT.Sigmoid, bias=col("b_rg_a", t)).then_inc(s_sig, 1)
                act.activation(b["ix"][:, :], flat(aux[1]), ACT.Sigmoid, bias=col("b_rg_x", t)).then_inc(s_sig, 1)
                act.wait_ge(s_sig, 2 * t + 1)
                step(act.activation(b["ts"][:, :], b["ra"][:, :], ACT.Tanh, scale=small[:, 10, t:t + 1]))
                step(act.activation(b["ra"][:, :], b["ra"][:, :], ACT.Exp, scale=small[:, 11, t:t + 1]))
                step.settle()
                act.activation(b["ts"][:, :], b["ts"][:, :], ACT.Sqrt).then_inc(s_rec, 1)
                act.wait_ge(s_evac, 2 * t + 2)
                act.activation(b["gg"][:, :], b["gg"][:, :], ACT.Gelu_apprx_tanh).then_inc(s_gelu, 1)
                act.wait_ge(s_y, t + 1)
                act.activation(b_hi[:, 4 + t, :], b["gg"][:, :], ACT.Identity).then_inc(s_yhi, 1)

            for t in range(LRU_TILES):
                lru_tile(t)
            act.wait_ge(s_z, 1)
            act.dma_start(mem_raw[:, :, :], memT).then_inc(s_mem, 16)
            for j in range(2):
                step(act.activation(gk_a[:, j, :], flat(aux[j]), ACT.Abs, bias=col("b_gk", j)))
            step.settle()
            step(act.activation(gk_a[:, :, :], gk_a[:, :, :], ACT.Exp, scale=-1.0))
            step.settle()
            act.activation(gk_a[:, :, :], gk_a[:, :, :], ACT.Ln, bias=1.0).then_inc(s_lse, 1)
            for c in range(NC):
                act.wait_ge(s_vt, c + 1)
                act.activation(v_tok[:, c, :], ps[:, 4 + c % 4, :], ACT.Identity).then_inc(s_vtok, 1)
            act.wait_ge(s_mem, 16)
            act.wait_ge(s_vtok, NC)
            act.activation(ps[:, 4:8, :].rearrange("p b n -> p (b n)"),
                           mem_raw[:, :, :].rearrange("p k m -> p (k m)"), ACT.Square).then_inc(s_mq, 1)
            for k in range(KT):
                act.activation(m_hi[:, k, :], mem_raw[:, k, :], ACT.Identity,
                               scale=col("g_mem", k)).then_inc(s_mhi, 1)
            act.wait_ge(s_mssq, 1)
            act.activation(m_std[:, :], ps[:, 4, 0:2], ACT.Sqrt, scale=1.0 / D, bias=eps[:, 0:1])\
                .then_inc(s_mstd, 1)
            for h in range(4):
                act.wait_ge(s_evac, SLOT_VO + 4 + h + 1)
                act.activation(og[:, h, :], og[:, h, :], ACT.Silu).then_inc(s_silu, 1)
            ends = bsum[:, :, :].rearrange("p j (c i) -> p j c i", i=CH)[:, :, :, CH - 1]
            act.activation(dec[:, :, :], ends, ACT.Exp, scale=1.0 / GATE_NORM).then_inc(s_dec, 1)
            for L in range(len(LEVELS) + 1):
                act.wait_ge(s_ld, L + 1)
                act.activation(lev[L % 3][:, :, :], lev[L % 3][:, :, :], ACT.Exp,
                               scale=1.0 / GATE_NORM).then_inc(s_le, 1)
                if L in (4, 5):
                    act.wait_ge(s_xkt, L - 3)
                    act.activation(xk_new[:, 4 * (L - 4):4 * (L - 3), :].rearrange("p t m -> p (t m)"),
                                   flat(main[0]), ACT.Identity).then_inc(s_xkc, 1)
                if L == 1:
                    act.activation(qe[:, :, :], bsum[:, :, :], ACT.Exp, scale=1.0 / GATE_NORM).then_inc(s_ke, 1)
            for b in range(4):
                act.wait_ge(s_kt, b + 1)
                act.activation(kd_tok[:, 2 * b:2 * b + 2, :],
                               ps[:, b, :].rearrange("p (c n) -> p c n", c=2), ACT.Identity)\
                    .then_inc(s_ktok, 1)
            act.wait_ge(s_evac, SLOT_MIX)
            act.activation(xk[:, :, :], xk_new[:, :, :], ACT.Identity).then_inc(s_kvc, 1)
            act.activation(xv[:, :, :], xv_new[:, :, :], ACT.Identity).then_inc(s_kvc, 1)
            for c in range(NC + 3):
                if c < NC:
                    act.wait_ge(s_o, c + 1)
                    if c >= 4:
                        act.wait_ge(s_oylo, c - 3)
                    out = ps[:, 4 + c % 2 * 2:6 + c % 2 * 2, 0:256].rearrange("p o (j n) -> p o j n", j=2)
                    copy, squares = (t[:, :].rearrange("p (j o n) -> p o j n", j=2, o=2)
                                     for t in (o_sb[c % 4], o_sq[c % 2]))
                    act.activation(copy, out, ACT.Identity).then_inc(s_oc, 1)
                    if c >= 2:
                        act.wait_ge(s_ossq, c - 1)
                    act.activation(squares, out, ACT.Square).then_inc(s_oc, 1)
                if 1 <= c <= NC:
                    act.wait_ge(s_ossq, c)
                    act.activation(o_std[:, c - 1, :], ps[:, 3, (c - 1) * 4:c * 4], ACT.Sqrt, scale=1.0 / P,
                                   bias=eps[:, 0:1]).then_inc(s_ostd, 1)
                if c >= 3:
                    act.wait_ge(s_oy, c - 2)
                    d = c - 3
                    act.activation(b_hi[:, 0:4, d * CH:(d + 1) * CH],
                                   o_sb[d % 4][:, :].rearrange("p (h n) -> p h n", h=4), ACT.Identity)\
                        .then_inc(s_oyhi, 1)
            act.wait_ge(s_o, NC)
            act.wait_ge(s_oylo, NC)
            for t in range(KT):
                act.dma_start(x[:, t, :], xT[t, :, :]).then_inc(s_xr[t], 16)
            for t in range(KT):
                act.wait_ge(s_evac, SLOT_MIX + t + 1)
                h_tile(col("g_xattn", t), x[:, t, :], a_hi[:, t, :], t, KT + t - 1 if t >= 2 else None,
                       flat(aux[t % 2]))
            root(1)
            with act.Fori(0, KT - 1) as t:
                act.wait_ge(s_evac, t + (SLOT_XQ + 1))
                act.activation(b_hi[:, bass.ds(t, 1), :].rearrange("p o n -> p (o n)"), tmp[:, :],
                               ACT.Identity).then_inc(s_xqh, 1)
            act.wait_ge(s_full, SLOT_XO)
            act.activation(xk_hi[:, 0:2, :], xk[:, 0:2, :], ACT.Identity).then_inc(s_kvh, 1)
            act.activation(xk_hi[:, 2:, :], xk[:, 2:, :], ACT.Identity).then_inc(s_kvh, 1)
            act.wait_ge(s_evac, SLOT_XO)
            act.activation(b_hi[:, KT - 1, :], tmp[:, :], ACT.Identity).then_inc(s_xqh, 1)

            def exps(u):
                act.wait_ge(s_mx, u + 1)
                if u >= 4:
                    act.wait_ge(s_pt, u - 3)
                for i in range(2):
                    act.activation(pr[u % 4][:, i, :], ps[:, score_banks[u % 3], i * N_MEM:(i + 1) * N_MEM], ACT.Exp,
                                   bias=nmax[:, u, i:i + 1], accum_out=psum_p[:, u, i:i + 1]).then_inc(s_ex, 1)

            def turned(u):
                act.wait_ge(s_pt, u + 1)
                h, b = divmod(u, 4)
                if h >= 2:
                    act.wait_ge(s_full, MAIN_ATT + 2 * h - 2)
                act.activation(pT_hi[h % 2][:, :, b * 256:(b + 1) * 256],
                               ps[:, turn_banks[u % 3], :].rearrange("p (m n) -> p m n", m=2), ACT.Identity)\
                    .then_inc(s_pth, 1)

            def att(t):
                act.wait_ge(s_full, MAIN_ATT + t + 1)
                act.activation(b_hi[:, t, :], flat(att_pair[t]), ACT.Identity).then_inc(s_ath, 1)

            exps(0)
            exps(1)
            for u in range(4 * XHEADS):
                if u > 5 and u % 2 == 0:
                    att((u - 6) // 2)
                turned(u)
                if u + 2 < 4 * XHEADS:
                    exps(u + 2)
                if u < 2:
                    act.activation(xv_hi[:, u, :], xv[:, u, :], ACT.Identity).then_inc(s_kvh, 1)
            for t in range(KT - 3, KT):
                att(t)
            for t in range(KT):
                act.wait_ge(s_evac, MAIN_XO + t + 1)
                h_tile(col("g_ffn", t), x[:, t, :], a_hi[:, t, :], t, 2 * KT + t - 1 if t >= 2 else None,
                       flat(aux[t % 2]))
            root(2)

            def ffn_tile(g, j, f):
                act.wait_ge(s_cv, g * 2 + (j + 1))
                act.activation(conv[:, :], conv[:, :], ACT.Silu).then_inc(s_sl, 1)
                act.wait_ge(s_f, g * 2 + (j + 1))
                act.activation(f_hi[f][:, j, :], up[:, :], ACT.Identity).then_inc(s_fh, 1)

            with act.Fori(0, GROUPS // 2) as i:
                for f in range(2):
                    for j in range(GROUP):
                        ffn_tile(i * 2 + f, j, f)
            for j in range(GROUP):
                ffn_tile(GROUPS - 1, j, (GROUPS - 1) % 2)
            def final_root(half):
                act.wait_ge(s_ssq, 4 + half)
                act.activation(ssum[:, half * 4:half * 4 + 4], ps[:, half, 0:4], ACT.Sqrt, scale=1.0 / D,
                               bias=eps[:, 0:1]).then_inc(s_std, 1)

            for i, t, hs in pieces:
                act.wait_ge(s_oute, 8 * (GROUPS - 1) + i + 1)
                if t >= 1 and i >= 4:
                    act.wait_ge(s_facc, added(i - 4))
                out = fsq[:, i % 4, :] if t else facc[:, hs]
                act.activation(out, x[:, t, hs], ACT.Square).then_inc(s_fsq, 1)
                act.wait_ge(s_fsq, i + 1)
                act.activation(x[:, t, hs], x[:, t, hs], ACT.Identity, scale=col("g_final", t)).then_inc(s_xg, 1)
                if i == KT + 1:
                    final_root(0)
            final_root(1)
            done = 0
            for i, t, hs in pieces:
                if t >= by_pool[i // KT]:
                    done += 1
                    act.wait_ge(s_yf, done)
                    act.dma_start(yT[t, :, hs], x[:, t, hs]).then_inc(s_store, 16)

        @block.vector
        def _(dve):
            step = Steps(dve, s_dve)
            def h_rest(gain, xs, hi, lo, hhi, sq, where, into, first):
                dve.wait_ge(s_hhi, hhi)
                dve.scalar_tensor_tensor(lo, xs, gain, hi.bitcast(F32), ALU.mult, ALU.subtract).then_inc(s_h, 1)
                dve.wait_ge(s_sq, sq)
                if first:
                    dve.tensor_copy(into, where).then_inc(s_acc, 1)
                else:
                    dve.wait_ge(s_acc, sq - 1)
                    dve.tensor_tensor(into, where, into, ALU.add).then_inc(s_acc, 1)

            for t in range(KT):
                dve.wait_ge(s_x[t], 16)
                h_rest(col("g_mix", t), x[:, t, :], a_hi[:, t, :], a_lo[:, t, :], t + 1, t + 1,
                       flat(aux[t % 2]), acc[:, :], t == 0)

            def diagonal(k, out):
                dve.wait_ge(s_std, k + 1)
                step(dve.reciprocal(srec[:, :], ssum[:, :]))
                step.settle()
                dve.wait_ge(s_cst, 2)
                dve.tensor_tensor(out, ident[:, :].unsqueeze(1).to_broadcast([P, NC, P]),
                                  srec[:, :].unsqueeze(2).to_broadcast([P, NC, P]), ALU.mult).then_inc(s_dg, 1)

            def rstd_ready(k):
                dve.wait_ge(s_bc, k + 1)
                dve.tensor_copy(rstd[:, :], flat(aux[1])).then_inc(s_rstd, 1)
                dve.wait_ge(s_rstd, k + 1)

            diagonal(0, diag[:, :, :])
            rstd_ready(0)

            def scaled(out, u):
                dve.wait_ge(s_full, u + 1)
                dve.tensor_tensor(out, flat(main[u % 2]), rstd[:, :], ALU.mult).then_inc(s_evac, 1)

            def branch(t):
                b = lru[t % 2]
                scaled(b["xr"][:, :], 2 * t)
                dve.wait_ge(s_evac, 2 * t + 1)
                tap = [col("conv_lru_w", 4 * t + n) for n in range(4)]
                step(dve.tensor_scalar(b["xc"][:, :], b["xr"][:, :], tap[3], col("conv_lru_b", t),
                                       ALU.mult, ALU.add))
                for back in (1, 2, 3):
                    step.settle()
                    ins = dve.scalar_tensor_tensor(b["xc"][:, back:], b["xr"][:, 0:S - back], tap[3 - back],
                                                   b["xc"][:, back:], ALU.mult, ALU.add)
                    if back < 3:
                        step(ins)
                    else:
                        ins.then_inc(s_xc, 1)

            def recurrence(t):
                b = lru[t % 2]
                dve.wait_ge(s_rec, t + 1)
                step(dve.scalar_tensor_tensor(b["ts"][:, :], b["ra"][:, :], 1.0, b["ts"][:, :],
                                              ALU.add, ALU.mult))
                step(dve.tensor_tensor(b["ix"][:, :], b["ix"][:, :], b["xc"][:, :], ALU.mult))
                step.settle()
                step(dve.memset(b["ts"][:, 0:1], 1.0))
                step.settle()
                step(dve.tensor_tensor(b["ts"][:, :], b["ts"][:, :], b["ix"][:, :], ALU.mult))
                step.settle()
                step(dve.tensor_tensor_scan(b["xr"][:, :], b["ra"][:, :], b["ts"][:, :], 0.0,
                                            ALU.mult, ALU.add))
                step.settle()
                dve.wait_ge(s_gelu, t + 1)
                dve.tensor_tensor(b["gg"][:, :], b["gg"][:, :], b["xr"][:, :], ALU.mult).then_inc(s_y, 1)
                dve.wait_ge(s_yhi, t + 1)
                dve.wait_ge(s_y, t + 1)
                dve.tensor_tensor(b_lo[:, 4 + t, :], b["gg"][:, :], b_hi[:, 4 + t, :].bitcast(F32),
                                  ALU.subtract).then_inc(s_ylo, 1)

            def gelu_in(t):
                scaled(lru[t % 2]["gg"][:, :], 2 * t + 1)

            branch(0)
            gelu_in(0)
            sm = [small[:, n, :] for n in range(12)]
            dve.wait_ge(s_sp, 1)
            step(dve.tensor_scalar(sm[2], sm[1], 2.0, None, ALU.add))
            step.settle()
            step(dve.reciprocal(sm[3], sm[2]))
            step.settle()
            step(dve.tensor_tensor(sm[4], sm[1], sm[3], ALU.mult))
            step.settle()
            step(dve.tensor_tensor(sm[5], sm[4], sm[4], ALU.mult))
            step.settle()
            step(dve.tensor_scalar(sm[6], sm[5], 1.0 / 17, 1.0 / 15, ALU.mult, ALU.add))
            for d in (13, 11, 9, 7, 5, 3, 1):
                step.settle()
                step(dve.tensor_tensor(sm[6], sm[6], sm[5], ALU.mult))
                step.settle()
                step(dve.tensor_scalar(sm[6], sm[6], 1.0 / d, None, ALU.add))
            step(dve.tensor_scalar(sm[7], par[:, PARAMS["lru_lambda"]:PARAMS["lru_lambda"] + 4], -1.0, 0.0,
                                   ALU.mult, ALU.max))
            step.settle()
            step(dve.scalar_tensor_tensor(sm[8], sm[4], 2.0, sm[6], ALU.mult, ALU.mult))
            step.settle()
            step(dve.tensor_tensor(sm[9], sm[8], sm[7], ALU.add))
            step.settle()
            step(dve.tensor_scalar(sm[10], sm[9], 4.0, None, ALU.mult))
            step.settle()
            dve.tensor_scalar(sm[11], sm[9], -8.0, None, ALU.mult).then_inc(s_spd, 1)

            for t in range(LRU_TILES):
                if t + 1 < LRU_TILES:
                    branch(t + 1)
                else:
                    dve.wait_ge(s_full, SLOT_GK + 1)
                    dve.tensor_tensor(gk_lr[:, :], flat(main[SLOT_GK % 2])[0:GLA_LOWRANK, :],
                                      rstd[0:GLA_LOWRANK, :], ALU.mult).then_inc(s_evac, 1)
                recurrence(t)
                if t + 1 < LRU_TILES:
                    gelu_in(t + 1)
            for j in range(2):
                scaled(kk[:, j, :], SLOT_KQ + j)
                if j == 0:
                    dve.wait_ge(s_lse, 1)
                    for i in range(2):
                        step(dve.tensor_scalar(gk_b[:, i, :], flat(aux[i]), col("b_gk", i), 0.0,
                                               ALU.add, ALU.min))
                    step.settle()
                    step(dve.tensor_tensor(gk_b[:, :, :], gk_b[:, :, :], gk_a[:, :, :], ALU.subtract))
                    step.settle()
                    for i in range(2):
                        for c in range(NC):
                            cs = slice(c * CH, (c + 1) * CH)
                            dve.tensor_tensor_scan(bsum[:, i, cs], ones[:, :], gk_b[:, i, cs], 0.0,
                                                   ALU.mult, ALU.add).then_inc(s_b, 1)
            for j in range(2):
                u = SLOT_KQ + 2 + j
                dve.wait_ge(s_full, u + 1)
                dve.scalar_tensor_tensor(qq[:, j, :], flat(main[u % 2]), DK ** -0.5, rstd[:, :],
                                         ALU.mult, ALU.mult).then_inc(s_evac, 1)
            for h in range(4):
                scaled(v_feat[:, h, :], SLOT_VO + h)
            dve.wait_ge(s_mq, 1)
            dve.wait_ge(s_cst, 6 + 2 * len(LEVELS))
            dve.tensor_reduce(m_acc[:, :], ps[:, 4:8, :].rearrange("p b (k m) -> p m (b k)", m=N_MEM),
                              AX.X, ALU.add).then_inc(s_msq, 1)
            scaled(og[:, 0, :], SLOT_VO + 4)
            for k in range(KT):
                dve.wait_ge(s_mhi, k + 1)
                ins = dve.scalar_tensor_tensor(m_lo[:, k, :], mem_raw[:, k, :], col("g_mem", k),
                                               m_hi[:, k, :].bitcast(F32), ALU.mult, ALU.subtract)
                if k < KT - 1:
                    step(ins)
            ins.then_inc(s_mh, 1)
            scaled(og[:, 1, :], SLOT_VO + 5)
            step.settle()
            dve.wait_ge(s_mh, 1)
            dve.tensor_tensor(lev[2][:, :, :], qq[:, :, :], kk[:, :, :], ALU.mult).then_inc(s_qk, 1)
            dve.wait_ge(s_mstd, 1)
            step(dve.reciprocal(m_rec[:, :], m_std[:, :]))
            step.settle()
            scaled(og[:, 2, :], SLOT_VO + 6)
            scaled(og[:, 3, :], SLOT_VO + 7)

            def level(L):
                m = LEVELS[L]
                buf = lev[L % 3]
                sv, bv = (t[:, :, :].rearrange("p j (n h m) -> p (j n) h m", h=2, m=m) for t in (buf, bsum))
                n = 2 * S // (2 * m)
                ref = bv[:, :, 0, m - 1:m].to_broadcast([P, n, m])
                step(dve.tensor_tensor(sv[:, :, 0, :], ref, bv[:, :, 0, :], ALU.subtract))
                dve.tensor_tensor(sv[:, :, 1, :], bv[:, :, 1, :], ref, ALU.subtract).then_inc(s_ld, 1)

            def level_product(L):
                m = LEVELS[L]
                sv, kv, qv = (t[:, :, :].rearrange("p j (n h m) -> p (j n) h m", h=2, m=m)
                              for t in (lev[L % 3], kk, qq))
                dve.wait_ge(s_le, L + 1)
                step(dve.tensor_tensor(sv[:, :, 0, :], sv[:, :, 0, :], kv[:, :, 0, :], ALU.mult))
                step.settle()
                dve.tensor_tensor(sv[:, :, 1, :], sv[:, :, 1, :], qv[:, :, 1, :], ALU.mult).then_inc(s_lt, 1)

            dve.wait_ge(s_b, 2 * NC)
            level(0)

            def memory(half):
                dve.wait_ge(s_full, SLOT_MEM + 4 * half + 4)
                out = (xk_tok, xv_new)[half // 2][:, :, (half % 2) * HALF:(half % 2 + 1) * HALF]
                dve.tensor_tensor(out, main[(half + 1) % 2], m_rec[:, :].unsqueeze(2).to_broadcast([P, 2, HALF]),
                                  ALU.mult).then_inc(s_evac, 4)

            dve.wait_ge(s_qks, 1)
            level(1)
            got = ps[:, 7, 0:4 * NC].rearrange("p (n o) -> p o n", o=2)
            for odd in range(2):
                ins = dve.tensor_tensor(sT[:, odd, :, :, :].rearrange("p c j n -> p (c j) n"),
                                        ident[:, :].unsqueeze(1).to_broadcast([P, 2 * NC, P]),
                                        got[:, odd, :].unsqueeze(2).to_broadcast([P, 2 * NC, P]), ALU.mult)
                if odd == 0:
                    step(ins)
            ins.then_inc(s_lc, 1)
            step.settle()
            level_product(0)
            kd = lev[len(LEVELS) % 3]
            unit = 0
            for L in range(len(LEVELS)):
                m = LEVELS[L]
                if L + 1 < len(LEVELS):
                    level_product(L + 1)
                else:
                    dve.wait_ge(s_le, L + 2)
                    dve.wait_ge(s_ld, L + 2)
                    dve.tensor_tensor(kd[:, :, :], kd[:, :, :], kk[:, :, :], ALU.mult).then_inc(s_kd, 1)
                if L == len(LEVELS) - 1:
                    memory(3)
                for c in range(0, NC, 2):
                    for odd in range(2):
                        dve.wait_ge(s_lp, unit + 1)
                        dve.wait_ge(s_lc, max(1, unit - 6))
                        got = ps[:, 4 + unit % 4, :].rearrange("p (i n h m) -> p i n h m", i=4, h=2, m=m)
                        kept = sT[:, odd, c:c + 2, :, :].rearrange("p c j (n h m) -> p (c j) n h m", h=2, m=m)
                        mask = masks[:, L, :].bitcast(U32).rearrange("p (n m) -> p n m", m=m)
                        mask = mask.unsqueeze(1).to_broadcast([P, 4, CH // (2 * m), m])
                        dve.copy_predicated(kept[:, :, :, 1, :], mask, got[:, :, :, 1, :]).then_inc(s_lc, 1)
                        unit += 1
                    if c == 2 and L % 2 == 0 and L < len(LEVELS) - 1:
                        memory(L // 2)
                    if c == 4 and L + 2 < len(LEVELS):
                        if L:
                            dve.wait_ge(s_lp, 8 * L)
                        level(L + 2)
                    if c == 4 and L + 2 == len(LEVELS):
                        bv, kdv = (t[:, :, :].rearrange("p j (c i) -> p (j c) i", i=CH) for t in (bsum, kd))
                        dve.tensor_tensor(kdv, bv[:, :, CH - 1:CH].to_broadcast([P, 2 * NC, CH]), bv,
                                          ALU.subtract).then_inc(s_ld, 1)
                    if c == 2 and L in (3, 5):
                        j = (L - 3) // 2
                        if j == 0:
                            dve.wait_ge(s_ke, 1)
                        dve.tensor_tensor(qe[:, j, :], qe[:, j, :], qq[:, j, :], ALU.mult).then_inc(s_qe, 1)
            dve.wait_ge(s_dec, 1)
            for c in range(NC - 1):
                dve.wait_ge(s_delta, c // 2 + 1)
                got = ps[:, c // 2, (c % 2) * 256:(c % 2) * 256 + 256].rearrange("p (j n) -> p j n", j=2)
                if c == 0:
                    dve.tensor_copy(states[:, 1, :, :], got).then_inc(s_st, 1)
                    continue
                dve.wait_ge(s_st, c)
                step(dve.scalar_tensor_tensor(states[:, c + 1, 0, :], states[:, c, 0, :], dec[:, 0, c:c + 1],
                                              got[:, 0, :], ALU.mult, ALU.add))
                dve.scalar_tensor_tensor(states[:, c + 1, 1, :], states[:, c, 1, :], dec[:, 1, c:c + 1],
                                         got[:, 1, :], ALU.mult, ALU.add).then_inc(s_st, 1)
            for c in range(NC + 2):
                if c < NC:
                    dve.wait_ge(s_ostd, c + 1)
                    step(dve.reciprocal(o_rec[:, c, :], o_std[:, c, :]))
                    step.settle()
                    if c >= 2:
                        dve.wait_ge(s_obc, c - 1)
                    dve.tensor_tensor(o_dg[c % 2][:, :, :], ident[:, :].unsqueeze(1).to_broadcast([P, 4, P]),
                                      o_rec[:, c, :].unsqueeze(2).to_broadcast([P, 4, P]), ALU.mult)\
                        .then_inc(s_odg, 1)
                if c >= 1 and c <= NC:
                    d = c - 1
                    dve.wait_ge(s_obc, d + 1)
                    o = o_sb[d % 4]
                    step(dve.tensor_tensor(o[:, :], ps[:, d % 2, :], o[:, :], ALU.mult))
                    step.settle()
                    ov = o[:, :].rearrange("p (h n) -> p h n", h=4)
                    dve.wait_ge(s_silu, 4)
                    dve.scalar_tensor_tensor(ov, ov, col("g_head"), og[:, :, d * CH:(d + 1) * CH],
                                             ALU.mult, ALU.mult).then_inc(s_oy, 1)
                if c >= 2:
                    d = c - 2
                    dve.wait_ge(s_oyhi, d + 1)
                    cs = slice(d * CH, (d + 1) * CH)
                    dve.tensor_tensor(b_lo[:, 0:4, cs], o_sb[d % 4][:, :].rearrange("p (h n) -> p h n", h=4),
                                      b_hi[:, 0:4, cs].bitcast(F32), ALU.subtract).then_inc(s_oylo, 1)

            def residual(t, u, gain, k):
                dve.wait_ge(s_full, u + 1)
                dve.tensor_tensor(x[:, t, :], flat(main[u % 2]), x[:, t, :], ALU.add).then_inc(s_evac, 1)
                h_rest(col(gain, t), x[:, t, :], a_hi[:, t, :], a_lo[:, t, :], KT * k + t + 1,
                       KT * k + t + 1, flat(aux[t % 2]), acc[:, :], t == 0)

            for t in range(KT):
                dve.wait_ge(s_xr[t], 16)
                residual(t, SLOT_MIX + t, "g_xattn", 1)
            diagonal(1, diag[:, :, :])
            rstd_ready(1)
            def query_scaled(i, j):
                u = SLOT_XQ + j
                dve.wait_ge(s_full, i * 2 + (u + 1))
                if not isinstance(i, int) or i + j:
                    dve.wait_ge(s_xq, i * 2 + j)
                dve.scalar_tensor_tensor(tmp[:, :], flat(main[u % 2]), XHEAD_DIM ** -0.5, rstd[:, :],
                                         ALU.mult, ALU.mult).then_inc(s_evac, 1)

            def query_rest(i, j):
                dve.wait_ge(s_xqh, i * 2 + (j + 1))
                dve.wait_ge(s_evac, i * 2 + (SLOT_XQ + j + 1))
                hi, lo = (z[:, bass.ds(i * 2 + j, 1), :].rearrange("p o n -> p (o n)")
                          for z in (b_hi, b_lo))
                dve.tensor_tensor(lo, tmp[:, :], hi.bitcast(F32), ALU.subtract).then_inc(s_xq, 1)

            def query(i, j):
                query_scaled(i, j)
                query_rest(i, j)

            query(0, 0)
            query(0, 1)
            with dve.Fori(1, KT // 2 - 1) as i:
                query(i, 0)
                query(i, 1)
            query(KT // 2 - 1, 0)

            def key_rest(part, tiles):
                dve.wait_ge(s_kvh, part + 1)
                dve.tensor_tensor(xk_lo[:, tiles, :], xk[:, tiles, :], xk_hi[:, tiles, :].bitcast(F32),
                                  ALU.subtract).then_inc(s_kv, 1)

            key_rest(0, slice(0, 2))
            query_scaled(KT // 2 - 1, 1)

            def maxima(u):
                dve.wait_ge(s_sc, u + 1)
                dve.tensor_reduce(nmax[:, u, :], ps[:, score_banks[u % 3], :].rearrange("p (i m) -> p i m", i=2),
                                  AX.X, ALU.max, negate=True).then_inc(s_mx, 1)

            def normalise(u):
                dve.wait_ge(s_ex, 2 * u + 2)
                step(dve.reciprocal(prec[:, u, :], psum_p[:, u, :]))
                step.settle()
                dve.tensor_tensor(pr[u % 4][:, :, :], pr[u % 4][:, :, :],
                                  prec[:, u, :].unsqueeze(2).to_broadcast([P, 2, N_MEM]), ALU.mult)\
                    .then_inc(s_pn, 1)

            def turned_rest(u):
                dve.wait_ge(s_pth, u + 1)
                h, b = divmod(u, 4)
                ts = slice(b * 256, (b + 1) * 256)
                dve.tensor_tensor(pT_lo[h % 2][:, :, ts], ps[:, turn_banks[u % 3], :].rearrange("p (m n) -> p m n", m=2),
                                  pT_hi[h % 2][:, :, ts].bitcast(F32), ALU.subtract).then_inc(s_ptl, 1)

            def att_rest(t):
                dve.wait_ge(s_ath, t + 1)
                dve.tensor_tensor(b_lo[:, t, :], flat(att_pair[t]), b_hi[:, t, :].bitcast(F32),
                                  ALU.subtract).then_inc(s_evac, 1)

            units = 4 * XHEADS
            for u in range(3):
                maxima(u)
            normalise(0)
            key_rest(1, slice(2, KT))
            for u in range(units):
                if u + 1 < units:
                    normalise(u + 1)
                if u > 5 and u % 2 == 0:
                    att_rest((u - 6) // 2)
                turned_rest(u)
                if u + 3 < units:
                    maxima(u + 3)
                if u == 1:
                    query_rest(KT // 2 - 1, 1)
                if 2 <= u < 4:
                    dve.wait_ge(s_kvh, u + 1)
                    dve.tensor_tensor(xv_lo[:, u - 2, :], xv[:, u - 2, :], xv_hi[:, u - 2, :].bitcast(F32),
                                      ALU.subtract).then_inc(s_kv, 1)
            for t in range(KT - 3, KT):
                att_rest(t)
            for t in range(KT):
                residual(t, MAIN_XO + t, "g_ffn", 2)
            diagonal(2, diag[:, :, :])
            rstd_ready(2)

            def ffn_tile(g, j, f, n):
                t = g * 2 + j
                dve.wait_ge(s_gu, g * 4 + (2 * j + 1))
                dve.tensor_tensor(gate[:, :], flat(main[1]), rstd[:, :], ALU.mult).then_inc(s_gue, 1)
                dve.wait_ge(s_gue, g * 4 + (2 * j + 1))
                tap = [par[:, bass.ds(g * 6 + (3 * j + k + PARAMS["conv_ffn_w"]), 1)] if not isinstance(g, int)
                       else col("conv_ffn_w", 3 * t + k) for k in range(3)]
                bias = (par[:, bass.ds(g * 2 + (j + PARAMS["conv_ffn_b"]), 1)] if not isinstance(g, int)
                        else col("conv_ffn_b", t))
                dve.tensor_scalar(conv[:, :], gate[:, :], tap[2], bias, ALU.mult, ALU.add).then_inc(s_dve, 1)
                dve.wait_ge(s_dve, n + 1)
                dve.scalar_tensor_tensor(conv[:, 1:], gate[:, 0:S - 1], tap[1], conv[:, 1:], ALU.mult,
                                         ALU.add).then_inc(s_dve, 1)
                dve.wait_ge(s_dve, n + 2)
                dve.scalar_tensor_tensor(conv[:, 2:], gate[:, 0:S - 2], tap[0], conv[:, 2:], ALU.mult,
                                         ALU.add).then_inc(s_cv, 1)
                dve.wait_ge(s_gu, g * 4 + (2 * j + 2))
                dve.tensor_tensor(up[:, :], flat(main[0]), rstd[:, :], ALU.mult).then_inc(s_gue, 1)
                dve.wait_ge(s_gue, g * 4 + (2 * j + 2))
                dve.wait_ge(s_sl, g * 2 + (j + 1))
                dve.tensor_tensor(up[:, :], up[:, :], conv[:, :], ALU.mult).then_inc(s_f, 1)

            def ffn_rest(g, j, f):
                dve.wait_ge(s_fh, g * 2 + (j + 1))
                dve.tensor_tensor(f_lo[f][:, j, :], up[:, :], f_hi[f][:, j, :].bitcast(F32),
                                  ALU.subtract).then_inc(s_fr, 1)

            def add_out(g, t):
                dve.wait_ge(s_out, g * 8 + (t - 7))
                dve.tensor_tensor(x[:, t, :], flat(aux[t % 2]), x[:, t, :], ALU.add).then_inc(s_oute, 1)

            per_group = 4

            def group(g, f, n0):
                for j in range(2):
                    ffn_tile(g, j, f, n0 + 2 * j)
                    add_out(g, 4 * j)
                    ffn_rest(g, j, f)
                    for t in range(4 * j + 1, 4 * j + 4):
                        add_out(g, t)

            before = step.n
            for j in range(GROUP):
                ffn_tile(0, j, 0, before + 2 * j)
                ffn_rest(0, j, 0)
            group(1, 1, before + per_group)
            group(2, 0, before + 2 * per_group)
            with dve.Fori(1, GROUPS // 2) as i:
                for j in range(2):
                    group(i * 2 + (1 + j), (1 + j) % 2, i * (2 * per_group) + (before + (1 + j) * per_group))
            step.n = before + GROUPS * per_group

            def add_piece(i, t, hs):
                dve.wait_ge(s_out, 8 * (GROUPS - 1) + i + 1)
                dve.tensor_tensor(x[:, t, hs], ps[:, 4 + i % 4, :], x[:, t, hs], ALU.add).then_inc(s_oute, 1)

            def add_squares(i, t, hs):
                dve.wait_ge(s_fsq, i + 1)
                if t >= 2:
                    dve.wait_ge(s_facc, added(i - 1))
                dve.tensor_tensor(facc[:, hs], fsq[:, i % 4, :], facc[:, hs], ALU.add).then_inc(s_facc, 1)

            def final_diagonal(half):
                part = slice(half * 4, half * 4 + 4)
                dve.wait_ge(s_std, 4 + half)
                step(dve.reciprocal(srec[:, part], ssum[:, part]))
                step.settle()
                dve.tensor_tensor(fdiag[:, part, :], ident[:, :].unsqueeze(1).to_broadcast([P, 4, P]),
                                  srec[:, part].unsqueeze(2).to_broadcast([P, 4, P]), ALU.mult).then_inc(s_dg, 1)

            def final_rstd(half):
                dve.wait_ge(s_bc, 4 + half)
                dve.tensor_copy(frs[:, half * HALF:(half + 1) * HALF], ps[:, 2 + half, :]).then_inc(s_rstd, 1)

            def final_scale(half, tiles):
                dve.wait_ge(s_rstd, 4 + half)
                hs = slice(half * HALF, (half + 1) * HALF)
                for t in tiles:
                    dve.wait_ge(s_xg, half * KT + t + 1)
                    dve.tensor_tensor(x[:, t, hs], x[:, t, hs], frs[:, hs], ALU.mult).then_inc(s_yf, 1)

            for i, t, hs in pieces:
                add_piece(i, t, hs)
                if i and (i - 1) % KT:
                    add_squares(*pieces[i - 1])
                if i == KT + 4:
                    final_diagonal(0)
                if i == KT + 7:
                    final_rstd(0)
            add_squares(*pieces[-1])
            own = [list(range(by_pool[half], KT)) for half in range(2)]
            final_scale(0, own[0][:2])
            final_diagonal(1)
            final_scale(0, own[0][2:])
            final_rstd(1)
            final_scale(1, own[1])


def kernel(x, mem, g_mix, w_in, w_gk, b_gk, g_gla_head, conv_lru_w, conv_lru_b, w_rg_a, b_rg_a, w_rg_x,
           b_rg_x, lru_lambda, w_mix_out, g_xattn, g_mem, w_xq, w_xkv, w_xo, g_ffn, w_ffn_in, conv_ffn_w,
           conv_ffn_b, w_ffn_out, g_final):
    import numpy as np
    import concourse.bacc as bacc
    from concourse.bass_utils import run_bass_kernel_spmd as run

    def slots(w):
        w = np.asarray(w)
        n = w.shape[1] // P
        return w.reshape(KT, P, n, P).transpose(2, 1, 0, 3).reshape(n, P, KT * P)

    def cols(v):
        v = np.asarray(v)
        return v.reshape(-1, P).T if v.ndim == 1 else v.reshape(v.shape[0], -1, P).transpose(2, 1, 0).reshape(P, -1)

    w = np.asarray(w_in)[0]
    at = np.cumsum([0, 256, 256, 512, 512, GLA_LOWRANK, 512, 512])
    q, k, v, og, gk, xr, xg = (w[:, at[n]:at[n + 1]] for n in range(7))
    gk_pad = np.zeros((D, P), w.dtype)
    gk_pad[:, :GLA_LOWRANK] = gk
    lru = np.stack([slots(xr), slots(xg)], 1).reshape(2 * LRU_TILES, P, D)
    ffn_in = slots(np.asarray(w_ffn_in)[0])
    out = np.asarray(w_ffn_out)[0].reshape(GROUPS, GROUP, P, 2, HALF).transpose(0, 3, 2, 1, 4)
    out = out.reshape(GROUPS, 2, P, GROUP * HALF)
    ffn = [ffn_in[0], ffn_in[FF_TILES], ffn_in[1], ffn_in[FF_TILES + 1]]
    for g in range(1, GROUPS):
        for half in range(2):
            t = GROUP * g + half
            ffn += [ffn_in[t], ffn_in[FF_TILES + t], out[g - 1, half]]
    ffn += [out[GROUPS - 1, 0], out[GROUPS - 1, 1]]
    xkv = np.asarray(w_xkv)[0].reshape(4, 2, P, 4, HALF).transpose(3, 0, 2, 1, 4).reshape(16, P, D)
    stream = np.concatenate([lru, slots(gk_pad), slots(k), slots(q), slots(v), slots(og),
                             xkv, slots(np.asarray(w_mix_out)[0]),
                             slots(np.asarray(w_xq)[0]), slots(np.asarray(w_xo)[0]), np.stack(ffn)])
    blocks = {"g_mix": g_mix, "g_xattn": g_xattn, "g_mem": g_mem, "g_ffn": g_ffn, "g_final": [g_final],
              "b_gk": b_gk, "g_head": g_gla_head, "conv_lru_w": conv_lru_w, "conv_lru_b": conv_lru_b,
              "b_rg_a": b_rg_a, "b_rg_x": b_rg_x, "lru_lambda": lru_lambda, "conv_ffn_w": conv_ffn_w,
              "conv_ffn_b": conv_ffn_b}
    params = np.concatenate([cols(np.asarray(blocks[n][0])) for n in PARAMS], 1)
    arrays = {
        "xT": np.asarray(x)[0].T.reshape(KT, P, S),
        "memT": np.asarray(mem)[0].T.reshape(KT, P, N_MEM).transpose(1, 0, 2),
        "wstream": stream,
        "params": params,
        "w_gk": np.asarray(w_gk)[0],
        "w_rg_a": np.asarray(w_rg_a)[0].reshape(LRU_TILES, 2, LRU_BLOCK, LRU_BLOCK).transpose(1, 2, 0, 3),
        "w_rg_x": np.asarray(w_rg_x)[0].reshape(LRU_TILES, 2, LRU_BLOCK, LRU_BLOCK).transpose(1, 2, 0, 3),
    }
    arrays = {n: np.ascontiguousarray(a) for n, a in arrays.items()}
    nc = bacc.Bacc("TRN2", target_bir_lowering=False, num_devices=1, dynamic_dma_scratch_size=1024)
    ins = [nc.dram_tensor(n, a.shape, mybir.dt.from_np(a.dtype), kind="ExternalInput").ap()
           for n, a in arrays.items()]
    yT = nc.dram_tensor("yT", (KT, P, S), F32, kind="ExternalOutput").ap()
    build(nc, *ins, yT)
    got = run(nc, [arrays], core_ids=[0]).results[0]["yT"]
    return np.ascontiguousarray(got.reshape(D, S).T)[None]
```

```python
from contextlib import ExitStack

import concourse.bass as bass
import concourse.mybir as mybir

P = 128
D = 1024
S = 1024
N_MEM = 256
KT = D // P
HALF = 512
EPS = 1e-6

GLA_HEADS = 4
DK = 64
GLA_LOWRANK = 16
GK_REST = 32
GK_ROWS = GK_REST + GLA_LOWRANK
GATE_NORM = 16.0
CH = 128
NC = S // CH

LRU_TILES = 4
LRU_BLOCK = 64
XHEADS = 4
XHEAD_DIM = D // XHEADS

D_FF = 2816
FF_TILES = D_FF // P
GROUP = 2
GROUPS = FF_TILES // GROUP

F32 = mybir.dt.float32
F32R = mybir.dt.float32r
U32 = mybir.dt.uint32
ACT = mybir.ActivationFunctionType
ALU = mybir.AluOpType
AX = mybir.AxisListType

KIB = 1024
RING = 2

SLOT_LRU = 0
SLOT_GK = 2 * LRU_TILES
SLOT_KQ = SLOT_GK + 1
SLOT_VO = SLOT_KQ + 4
SLOT_MEM = SLOT_VO + 8
SLOT_MIX = SLOT_MEM + 16
SLOT_XQ = SLOT_MIX + KT
SLOT_XO = SLOT_XQ + KT
SLOT_FFN = SLOT_XO + KT
N_SLOTS = SLOT_FFN + 6 * GROUPS

MAIN_ATT = SLOT_XO
MAIN_XO = MAIN_ATT + KT
MAIN_END = MAIN_XO + KT

PARAMS = {}
_col = 0
for _name, _n in (("g_mix", KT), ("g_xattn", KT), ("g_mem", KT), ("g_ffn", KT), ("g_final", KT),
                  ("b_gk", 2), ("g_head", 1), ("conv_lru_w", 4 * LRU_TILES), ("conv_lru_b", LRU_TILES),
                  ("b_rg_a", LRU_TILES), ("b_rg_x", LRU_TILES), ("lru_lambda", LRU_TILES),
                  ("conv_ffn_w", 3 * FF_TILES), ("conv_ffn_b", FF_TILES)):
    PARAMS[_name] = _col
    _col += _n
N_PARAMS = _col

LEVELS = [64, 32, 16, 8, 4, 2, 1]


class Steps:

    def __init__(self, engine, sem):
        self.engine, self.sem, self.n = engine, sem, 0

    def __call__(self, instruction):
        instruction.then_inc(self.sem, 1)
        self.n = self.n + 1
        return self.n

    def settle(self):
        self.engine.wait_ge(self.sem, self.n)


def build(nc, xT, memT, wstream, params, w_gk, w_rg_a, w_rg_x, yT):
    ctx = ExitStack()
    with ctx:
        base = (nc.sbuf_base + 31) // 32 * 32

        RAW, WHI, WLO = base, base + RING * 4 * KIB, base + 2 * RING * 4 * KIB
        A_HI = WLO + RING * 4 * KIB
        A_LO = A_HI + 32 * KIB
        B_HI = A_LO + 32 * KIB
        B_LO = B_HI + 32 * KIB
        X = B_LO + 32 * KIB
        KV = X + 32 * KIB
        RS = KV + 16 * KIB
        TMP = RS + 4 * KIB
        CONST = TMP + 4 * KIB
        top = [CONST]

        def at(name, shape, dt, offset):
            return nc.alloc_sbuf_tensor_at(name, shape, dt, offset=offset)

        def const(name, shape, dt=F32):
            n = 4
            for s in shape[1:]:
                n *= s
            t = at(name, shape, dt, top[0])
            top[0] += (n + 31) // 32 * 32
            assert top[0] <= nc.sbuf_usable_end, (name, top[0])
            return t

        raw = at("raw", [P, RING, 1024], F32, RAW)
        w_hi = at("w_hi", [P, RING, 1024], F32R, WHI)
        w_lo = at("w_lo", [P, RING, 1024], F32R, WLO)
        a_hi = at("a_hi", [P, KT, S], F32R, A_HI)
        a_lo = at("a_lo", [P, KT, S], F32R, A_LO)
        b_hi = at("b_hi", [P, KT, S], F32R, B_HI)
        b_lo = at("b_lo", [P, KT, S], F32R, B_LO)
        x = at("x", [P, KT, S], F32, X)
        rstd = at("rstd", [P, S], F32, RS)
        acc = at("acc", [P, S], F32, RS)
        diag = at("diag", [P, NC, P], F32, RS)
        tmp = at("tmp", [P, S], F32, TMP)
        masks = at("masks", [P, len(LEVELS) - 1, CH // 2], F32, TMP)

        names = ["xr", "xc", "ra", "ts", "ix", "gg"]
        places = [[B_HI + 4 * KIB * n for n in range(4)] + [KV, KV + 4 * KIB],
                  [B_LO + 4 * KIB * n for n in range(4)] + [KV + 8 * KIB, KV + 12 * KIB]]
        lru = [{n: at(f"lru_{n}{s}", [P, S], F32, places[s][i]) for i, n in enumerate(names)}
               for s in range(2)]
        og = at("og", [P, GLA_HEADS, S], F32, B_HI)
        kk = at("kk", [P, 2, S], F32, B_LO)
        qq = at("qq", [P, 2, S], F32, B_LO + 8 * KIB)
        v_tok = at("v_tok", [P, NC, 512], F32, X)
        bsum = at("bsum", [P, 2, S], F32, X + 16 * KIB)
        states = at("states", [P, NC, 2, P], F32, X + 24 * KIB)
        mem_raw = at("mem_raw", [P, KT, N_MEM], F32, X + 24 * KIB)
        gk_a = at("gk_a", [P, 2, S], F32, X)
        gk_b = at("gk_b", [P, 2, S], F32, X + 8 * KIB)
        gk_lr = at("gk_lr", [GK_ROWS, S], F32, X + 24 * KIB)
        v_feat = at("v_feat", [P, 4, S], F32, B_HI)
        m_hi = at("m_hi", [P, KT, N_MEM], F32R, KV)
        m_lo = at("m_lo", [P, KT, N_MEM], F32R, KV + 8 * KIB)
        xk_new = at("xk_new", [P, KT, N_MEM], F32, A_HI)
        xk_tok = at("xk_tok", [P, 2, D], F32, A_LO + 24 * KIB)
        xv_new = at("xv_new", [P, 2, D], F32, A_HI + 8 * KIB)
        lev = [at(f"lev{n}", [P, 2, S], F32, place)
               for n, place in enumerate((A_HI + 16 * KIB, A_HI + 24 * KIB, X + 24 * KIB))]
        sT = at("sT", [P, 2, NC, 2, P], F32, A_LO)
        m_acc = at("m_acc", [P, N_MEM], F32, TMP + 2 * KIB)
        qe = at("qe", [P, 2, S], F32, A_LO + 16 * KIB)
        kd_tok = at("kd_tok", [P, NC, 2 * P], F32, A_LO + 24 * KIB)
        o_tok = [at(f"o_tok{n}", [P, 512], F32, A_HI + (16 + 2 * n) * KIB) for n in range(4)]
        o_y = [at(f"o_y{n}", [P, 512], F32, A_HI + (24 + 2 * n) * KIB) for n in range(2)]
        o_sq = [at(f"o_sq{n}", [P, 512], F32, A_HI + (28 + 2 * n) * KIB) for n in range(2)]
        xk = at("xk", [P, KT, N_MEM], F32, KV)
        xv = at("xv", [P, 2, D], F32, KV + 8 * KIB)
        xk_hi = at("xk_hi", [P, KT, N_MEM], F32R, A_HI)
        xk_lo = at("xk_lo", [P, KT, N_MEM], F32R, A_HI + 8 * KIB)
        xv_hi = at("xv_hi", [P, 2, D], F32R, A_HI + 16 * KIB)
        xv_lo = at("xv_lo", [P, 2, D], F32R, A_HI + 24 * KIB)
        pr = [at(f"pr{n}", [P, 2, N_MEM], F32, A_LO + 2 * n * KIB) for n in range(4)]
        pT_hi = [at(f"pT_hi{n}", [P, 2, S], F32R, (A_LO + 8 * KIB, KV)[n]) for n in range(2)]
        pT_lo = [at(f"pT_lo{n}", [P, 2, S], F32R, (A_LO + 16 * KIB, KV + 8 * KIB)[n]) for n in range(2)]
        f_hi = [at(f"f_hi{n}", [P, GROUP, S], F32R, B_HI + 8 * n * KIB) for n in range(2)]
        f_lo = [at(f"f_lo{n}", [P, GROUP, S], F32R, B_HI + (16 + 8 * n) * KIB) for n in range(2)]
        gate = at("gate", [P, S], F32, B_LO)
        conv = at("conv", [P, S], F32, B_LO + 4 * KIB)
        up = at("up", [P, S], F32, B_LO + 8 * KIB)
        facc = at("facc", [P, S], F32, B_LO + 12 * KIB)
        frs = at("frs", [P, S], F32, B_LO + 16 * KIB)
        fdiag = at("fdiag", [P, NC, P], F32, B_LO + 16 * KIB)
        fsq = at("fsq", [P, 4, HALF], F32, B_LO)

        ident = const("ident", [P, P])
        ones = const("ones", [P, P])
        par = const("par", [P, N_PARAMS])
        wgk = const("wgk", [GK_ROWS, 2 * P])
        bd = const("bd", [P, 2, LRU_TILES, P])
        eps = const("eps", [P, 1])
        xk0_hi = const("xk0_hi", [P, 2, N_MEM], F32R)
        xk0_lo = const("xk0_lo", [P, 2, N_MEM], F32R)
        table = const("table", [P, 1])
        small = const("small", [P, 12, LRU_TILES])
        dec = const("dec", [P, 2, NC])
        ssum = const("ssum", [P, NC])
        srec = const("srec", [P, NC])
        m_std = const("m_std", [P, 2])
        m_rec = const("m_rec", [P, 2])
        sel = const("sel", [P, 2])
        o_ss = const("o_ss", [P, NC, GLA_HEADS])
        o_std = const("o_std", [P, NC, GLA_HEADS])
        o_rec = const("o_rec", [P, NC, GLA_HEADS])
        nmax = const("nmax", [P, 16, 2])
        psum_p = const("psum_p", [P, 16, 2])
        prec = const("prec", [P, 16, 2])

        def col(name, i=0):
            return par[:, PARAMS[name] + i:PARAMS[name] + i + 1]

        ps = ctx.enter_context(nc.psum_tensor("ps", [P, 8, HALF], F32))
        main = [ps[:, 0:2, :], ps[:, 2:4, :]]
        aux = [ps[:, 4:6, :], ps[:, 6:8, :]]

        score_banks = (4, 5, 2)
        turn_banks = (6, 7, 3)
        att_pair = [main[1] if t == KT - 2 else main[0] for t in range(KT)]

        turned_o_banks = (0, 1, 0, 1, 0, 1, 4, 6)
        kd_banks = (2, 3, 0, 1)

        def flat(pair):
            return pair.rearrange("p b n -> p (b n)")

        def sem(name):
            return ctx.enter_context(nc.semaphore(name))

        s_raw = [sem(f"raw_loaded{n}") for n in range(RING)]
        s_taken = sem("slot_taken")
        s_whi = sem("w_hi_done")
        s_split = sem("w_split")
        s_par = sem("params_loaded")
        s_x = [sem(f"x_loaded{n}") for n in range(KT)]
        s_xr = [sem(f"x_reloaded{n}") for n in range(KT)]
        s_mem = sem("mem_loaded")
        s_bd = sem("gate_weights_loaded")
        s_cst = sem("constants_made")
        s_bd0 = sem("gate_weights_zeroed")
        s_ones = sem("ones_made")
        s_full = sem("main_full")
        s_evac = sem("main_evacuated")
        s_dve = sem("dve_steps")
        s_act = sem("act_steps")
        s_hhi = sem("h_hi_done")
        s_sq = sem("squares_done")
        s_h = sem("h_ready")
        s_acc = sem("squares_summed")
        s_ssq = sem("ssq_ready")
        s_std = sem("std_ready")
        s_rstd = sem("rstd_ready")
        s_dg = sem("diag_ready")
        s_bc = sem("rstd_broadcast")
        s_xc = sem("xc_ready")
        s_gate = sem("gates_ready")
        s_sig = sem("sigmoids_done")
        s_rec = sem("lru_factors_ready")
        s_gelu = sem("gelu_done")
        s_y = sem("y_lru_ready")
        s_yhi = sem("y_lru_hi_done")
        s_ylo = sem("y_mix_lru_ready")
        s_sp = sem("softplus_exp")
        s_spd = sem("softplus_ready")
        s_z = sem("gate_logits_ready")
        s_lse = sem("log1p_exp_ready")
        s_b = sem("log_gates_summed")
        s_silu = sem("silu_done")
        s_vt = sem("v_turned")
        s_vtok = sem("v_token_ready")
        s_mhi = sem("mem_hi_done")
        s_mh = sem("mem_ready")
        s_wgk = sem("w_gk_loaded")
        s_gkw = sem("w_gk_rest_done")
        s_mq = sem("mem_squares")
        s_msq = sem("mem_squares_summed")
        s_mssq = sem("mem_ssq")
        s_mstd = sem("mem_std")
        s_ld = sem("level_exponents")
        s_le = sem("level_exps")
        s_lt = sem("level_ready")
        s_lp = sem("level_scores")
        s_lc = sem("level_scores_kept")
        s_qk = sem("q_times_k")
        s_qks = sem("q_dot_k")
        s_qe = sem("q_decayed")
        s_xkt = sem("memory_keys_turned")
        s_xkc = sem("memory_keys_copied")
        s_kvc = sem("memory_moved")
        s_ke = sem("k_exps")
        s_kd = sem("k_decayed")
        s_kt = sem("k_turned")
        s_ktok = sem("k_token_ready")
        s_dec = sem("chunk_decay")
        s_delta = sem("state_products")
        s_st = sem("states_ready")
        s_o = sem("o_ready")
        s_oc = sem("o_squared")
        s_on = sem("o_normalised")
        s_ot = sem("o_turned")
        s_ostd = sem("o_std")
        s_oy = sem("y_gla_ready")
        s_oyhi = sem("y_gla_hi")
        s_oylo = sem("y_mix_gla_ready")
        s_xqh = sem("xq_hi")
        s_xq = sem("xq_ready")
        s_kvh = sem("kv_hi")
        s_kv = sem("keys_ready")
        s_vlo = sem("values_ready")
        s_sc = sem("scores_ready")
        s_mx = sem("max_ready")
        s_ex = sem("exps_ready")
        s_pn = sem("p_normalised")
        s_pt = sem("p_turned")
        s_pth = sem("p_turned_hi")
        s_ptl = sem("p_turned_ready")
        s_ath = sem("att_hi")
        s_gu = sem("gate_up_full")
        s_gue = sem("gate_up_evacuated")
        s_cv = sem("conv_ready")
        s_sl = sem("ffn_silu_done")
        s_f = sem("f_product")
        s_fh = sem("f_hi")
        s_fr = sem("f_ready")
        s_out = sem("out_full")
        s_oute = sem("out_added")
        s_fsq = sem("final_squares")
        s_facc = sem("final_summed")
        s_xg = sem("x_times_gain_final")
        s_yf = sem("y_final_ready")
        s_yfp = sem("y_final_ready_pool")
        s_store = sem("y_stored")

        pieces = [(i, i % KT, slice(i // KT * HALF, (i // KT + 1) * HALF)) for i in range(2 * KT)]
        by_pool = (5, 3)

        def added(i):
            return i - i // KT

        block = ctx.enter_context(nc.Block())

        @block.sync
        def _(sp):
            sp.dma_start(raw[:, 0, :], wstream[0, :, :]).then_inc(s_raw[0], 16)
            sp.dma_start(par[:, :], params).then_inc(s_par, 16)
            sp.dma_start(x[:, 0, :], xT[0, :, :]).then_inc(s_x[0], 16)
            sp.dma_start(x[:, 1, :], xT[1, :, :]).then_inc(s_x[1], 16)
            sp.dma_start(raw[:, 1, :], wstream[1, :, :]).then_inc(s_raw[1], 16)
            for t in range(2, KT):
                sp.dma_start(x[:, t, :], xT[t, :, :]).then_inc(s_x[t], 16)
            sp.wait_ge(s_bd0, 2)
            for row in (0, GK_REST):
                sp.dma_start(wgk[row:row + GLA_LOWRANK, :], w_gk).then_inc(s_wgk, 16)
            for g, w in enumerate((w_rg_a, w_rg_x)):
                for h in range(2):
                    rows = slice(h * LRU_BLOCK, (h + 1) * LRU_BLOCK)
                    sp.dma_start(bd[rows, g, :, rows], w[h, :, :, :]).then_inc(s_bd, 16)
            assert N_SLOTS % 2 == 1
            with sp.Fori(1, N_SLOTS // 2) as i:
                for j in range(RING):
                    sp.wait_ge(s_split, i * 2 + (j - 1))
                    sp.dma_start(raw[:, j, :], wstream[i * 2 + j, :, :]).then_inc(s_raw[j], 16)
            sp.wait_ge(s_split, N_SLOTS - 2)
            sp.dma_start(raw[:, 0, :], wstream[N_SLOTS - 1, :, :]).then_inc(s_raw[0], 16)
            done = 0
            for i, t, hs in pieces:
                if t < by_pool[i // KT]:
                    done += 1
                    sp.wait_ge(s_yfp, done)
                    sp.dma_start(yT[t, :, hs], x[:, t, hs]).then_inc(s_store, 16)
            sp.wait_ge(s_store, 16 * len(pieces))

        @block.gpsimd
        def _(pool):
            made = 0
            pool.memset(bd[:, :, :, :], 0.0).then_inc(s_bd0, 1)
            pool.memset(wgk[:, :], 0.0).then_inc(s_bd0, 1)
            pool.memset(ones[:, :], 1.0).then_inc(s_ones, 1)
            pool.memset(eps[:, :], EPS).then_inc(s_ones, 1)
            pool.memset(ident[:, :], 0.0).then_inc(s_cst, 1)
            pool.wait_ge(s_cst, 1)
            pool.affine_select(out=ident[:, :], in_=ident[:, :], compare_op=ALU.not_equal, fill=1.0,
                               base=0, pattern=[[-1, P]], channel_multiplier=1).then_inc(s_cst, 1)
            made = 2

            def split(use, slot_of, freed=None):
                pool.wait_ge(s_raw[slot_of], use * 16 + 16)
                if freed is not None:
                    pool.wait_ge(*freed)
                pool.sem_inc(s_taken, 1)
                pool.tensor_scalar(w_hi[:, slot_of, :], raw[:, slot_of, :], 1.0, 1.0, ALU.mult,
                                   ALU.mult).then_inc(s_whi, 1)

            def rest(slot_of, count):
                pool.wait_ge(s_whi, count)
                pool.tensor_tensor(w_lo[:, slot_of, :], raw[:, slot_of, :],
                                   w_hi[:, slot_of, :].bitcast(F32), ALU.subtract).then_inc(s_split, 1)

            def slot(n, freed=None):
                split(n // RING, n % RING, freed)
                rest(n % RING, n + 1)

            slot(0)
            slot(1)
            pool.memset(masks[:, :, :], 1.0).then_inc(s_cst, 1)
            pool.memset(sel[:, :], 0.0).then_inc(s_cst, 1)
            pool.wait_ge(s_cst, made + 2)
            pool.memset(sel[0:DK, 0:1], 1.0).then_inc(s_cst, 1)
            pool.memset(sel[DK:P, 1:2], 1.0).then_inc(s_cst, 1)
            made += 4
            pool.wait_ge(s_cst, made)
            for i, m in enumerate(LEVELS[1:]):
                mask = masks[:, i, :].rearrange("p (n m) -> p n m", m=m)
                pool.affine_select(out=mask, in_=mask, compare_op=ALU.is_ge, fill=0.0, base=0,
                                   pattern=[[-2 * m, CH // (2 * m)], [0, m]], channel_multiplier=1)\
                    .then_inc(s_cst, 1)
                pool.wait_ge(s_cst, made + 1)
                pool.affine_select(out=mask, in_=mask, compare_op=ALU.is_ge, fill=0.0, base=m - 1,
                                   pattern=[[2 * m, CH // (2 * m)], [0, m]], channel_multiplier=-1)\
                    .then_inc(s_cst, 1)
                made += 2
                pool.wait_ge(s_cst, made)
            last_xq = SLOT_XO - 1
            def pairs(first, end):
                with pool.Fori(first // 2, end // 2) as i:
                    for j in range(RING):
                        split(i, j, (s_full, i * 2 + (j - 1)))
                        rest(j, i * 2 + (j + 1))

            pairs(2, SLOT_GK)
            place = SLOT_GK % RING
            split(SLOT_GK // RING, place, (s_full, SLOT_GK - 1))
            pool.wait_ge(s_whi, SLOT_GK + 1)
            pool.tensor_tensor(w_lo[:, place, :], raw[:, place, :], w_hi[:, place, :].bitcast(F32),
                               ALU.subtract).then_inc(s_gkw, 1)
            pool.wait_ge(s_gkw, 1)
            hi, lo = (w[:, place, :].rearrange("p (k n) -> p k n", k=KT)[:, :, GK_REST:GK_ROWS]
                      for w in (w_hi, w_lo))
            pool.tensor_scalar(hi, lo.bitcast(F32), 1.0, 1.0, ALU.mult, ALU.mult).then_inc(s_split, 1)
            slot(SLOT_GK + 1, (s_full, SLOT_GK))
            pairs(SLOT_GK + 2, (last_xq + 1) // 2 * 2)
            for n in range((last_xq + 1) // 2 * 2, SLOT_FFN + 2):
                if n == SLOT_XO + 2:
                    for mt in range(2):
                        pool.wait_ge(s_kvh, 3 + mt)
                        pool.tensor_tensor(xv_lo[:, mt, :], xv[:, mt, :], xv_hi[:, mt, :].bitcast(F32),
                                           ALU.subtract).then_inc(s_vlo, 1)
                used = n - 2 + 1
                if n - 2 >= SLOT_XO:
                    used += KT
                slot(n, (s_full, used))
            slot(SLOT_FFN + 2, (s_gu, 1))
            slot(SLOT_FFN + 3, (s_gu, 2))
            first = SLOT_FFN + 4
            for n, freed in enumerate(((s_gu, 3), (s_gu, 4), (s_gu, 5), (s_gu, 6), (s_out, 4), (s_gu, 7))):
                slot(first + n, freed)
            with pool.Fori(2, GROUPS) as g:
                for n in range(6):
                    freed = ((s_gu, g * 4), (s_out, g * 8 - 8), (s_gu, g * 4 + 1), (s_gu, g * 4 + 2),
                             (s_out, g * 8 - 4), (s_gu, g * 4 + 3))[n]
                    start = first - 6 + n
                    place = start % RING
                    split(g * 3 + start // 2, place, freed)
                    rest(place, g * 6 + (start + 1))
            slot(N_SLOTS - 2, (s_gu, 4 * GROUPS))
            slot(N_SLOTS - 1, (s_out, 8 * (GROUPS - 1)))
            for i, t, hs in pieces:
                if t < by_pool[i // KT]:
                    pool.wait_ge(s_xg, i + 1)
                    pool.wait_ge(s_rstd, 4 + i // KT)
                    pool.tensor_tensor(x[:, t, hs], x[:, t, hs], frs[:, hs], ALU.mult).then_inc(s_yfp, 1)

        @block.tensor
        def _(pe):
            def step_of(ring, out, k, hi, lo, first, last, halves=(0, 1)):
                ws = slice(k * P, (k + 1) * P)
                for m, (w, h) in enumerate(((w_hi, hi), (w_hi, lo), (w_lo, hi))):
                    for b in halves:
                        mm = pe.matmul(out[:, b, :], w[:, ring, ws], h[:, k, b * HALF:(b + 1) * HALF],
                                       start=first and m == 0, stop=last and m == 2)
                return mm

            def project(ring, out, hi, lo, order=range(KT), before=None):
                for n, k in enumerate(order):
                    if before:
                        before(k)
                    mm = step_of(ring, out, k, hi, lo, n == 0, n == len(order) - 1)
                return mm

            def ssq(src, out, n):
                for c in range(n):
                    mm = pe.matmul(out[:, c:c + 1], src[:, c * P:(c + 1) * P], ones[:, 0:1],
                                   start=True, stop=True)
                return mm

            def spread(dg, out, n):
                for c in range(0, n, 4):
                    w = min(4, n - c)
                    mm = pe.matmul(out[:, c // 4, 0:w * P], ones[:, :],
                                   dg[:, c:c + w, :].rearrange("p c n -> p (c n)"), start=True, stop=True)
                return mm

            def ready(n):
                pe.wait_ge(s_split, n + 1)
                if n >= 2:
                    u = n if n < SLOT_XO else n + KT
                    pe.wait_ge(s_evac, u - 1)

            def norm_sums(k, half):
                if half == 0:
                    pe.wait_ge(s_acc, KT * (k + 1))
                mm = ssq(acc[:, half * HALF:(half + 1) * HALF], aux[0][:, 0, half * 4:half * 4 + 4], NC // 2)
                if half:
                    mm.then_inc(s_ssq, 1)

            def norm_spread(k):
                pe.wait_ge(s_dg, k + 1)
                spread(diag, aux[1], NC).then_inc(s_bc, 1)

            def tile_ready(k):
                return lambda q: pe.wait_ge(s_h, KT * k + q + 1)

            def norm_within(k):
                return lambda q: norm_sums(k, q) if q < 2 else norm_spread(k) if q == KT // 2 else None

            def gates(t):
                pe.wait_ge(s_xc, t + 1)
                if t:
                    pe.wait_ge(s_sig, 2 * t)
                for g in range(2):
                    for h in range(2):
                        mm = pe.matmul(aux[g][:, h, :], bd[:, g, t, :],
                                       lru[t % 2]["xc"][:, h * HALF:(h + 1) * HALF], start=True, stop=True)
                mm.then_inc(s_gate, 1)

            pe.wait_ge(s_ones, 2)
            for k in range(KT):
                pe.wait_ge(s_h, k + 1)
                for n in range(2):
                    ready(n)
                    if k == KT - 2:
                        norm_sums(0, n)
                    if k == KT - 1 and n == 1:
                        norm_spread(0)
                    mm = step_of(n, main[n], k, a_hi, a_lo, k == 0, k == KT - 1)
                    if k == KT - 1:
                        mm.then_inc(s_full, 1)
            for n in range(2, 2 * LRU_TILES):
                ready(n)
                project(n % RING, main[n % 2], a_hi, a_lo).then_inc(s_full, 1)
                if n % 2 == 0:
                    if n == 2:
                        pe.wait_ge(s_bd, 64)
                        pe.wait_ge(s_rstd, 1)
                    gates(n // 2 - 1)
            n = SLOT_GK
            ready(n)
            for k in range(KT):
                for h in (a_hi, a_lo):
                    for b in range(2):
                        mm = pe.matmul(main[n % 2][0:GK_ROWS, b, :], w_hi[:, n % RING, k * P:k * P + GK_ROWS],
                                       h[:, k, b * HALF:(b + 1) * HALF], start=(k == 0 and h is a_hi),
                                       stop=(k == KT - 1 and h is a_lo))
            mm.then_inc(s_full, 1)
            gates(LRU_TILES - 1)
            for n in range(SLOT_KQ, SLOT_KQ + 4):
                ready(n)
                project(n % RING, main[n % 2], a_hi, a_lo).then_inc(s_full, 1)
                if n == SLOT_KQ:
                    pe.wait_ge(s_evac, SLOT_GK + 1)
                    pe.wait_ge(s_wgk, 32)
                    pe.wait_ge(s_sig, 2 * LRU_TILES)
                    for j in range(2):
                        for h in range(2):
                            mm = pe.matmul(aux[j][:, h, :], wgk[:, j * P:(j + 1) * P],
                                           gk_lr[:, h * HALF:(h + 1) * HALF], start=True, stop=True)
                    mm.then_inc(s_z, 1)
            assert SLOT_VO % 2 == 1
            with pe.Fori(0, 2) as i:
                for j in range(2):
                    n = SLOT_VO + j
                    pe.wait_ge(s_split, i * 2 + (n + 1))
                    pe.wait_ge(s_evac, i * 2 + (n - 1))
                    project(n % RING, main[n % 2], a_hi, a_lo).then_inc(s_full, 1)
            for n in range(SLOT_VO + 4, SLOT_VO + 8):
                ready(n)
                project(n % RING, main[n % 2], a_hi, a_lo).then_inc(s_full, 1)
                if n == SLOT_VO + 4:
                    pe.wait_ge(s_b, 2 * NC)
                    pe.wait_ge(s_evac, SLOT_VO + 4)
                    for c in range(NC):
                        if c >= 4:
                            pe.wait_ge(s_vtok, c - 3)
                        for h in range(4):
                            mm = pe.transpose(ps[:, 4 + c % 4, h * P:(h + 1) * P],
                                              v_feat[:, h, c * P:(c + 1) * P], ident[:, :])
                        mm.then_inc(s_vt, 1)
                if n == SLOT_VO + 6:
                    pe.wait_ge(s_msq, 1)
                    ssq(m_acc, ps[:, 4, :], 2).then_inc(s_mssq, 1)

            def memory(i):
                n = SLOT_MEM + i
                half, part = divmod(i, 4)
                out = main[(half + 1) % 2]
                pe.wait_ge(s_split, n + 1)
                if i == 0:
                    pe.wait_ge(s_mh, 1)
                if part == 0:
                    pe.wait_ge(s_evac, SLOT_MEM - 1 + half if half < 2 else SLOT_MEM + 4 * (half - 1))
                if i == 12:
                    pe.wait_ge(s_xkc, 2)
                for mt in range(2):
                    for k in range(2):
                        ms = slice(mt * P, (mt + 1) * P)
                        ws = slice(k * HALF, (k + 1) * HALF)
                        for p, (m, w) in enumerate(((m_hi, w_hi), (m_hi, w_lo), (m_lo, w_hi))):
                            mm = pe.matmul(out[:, mt, :], m[:, 2 * part + k, ms], w[:, n % RING, ws],
                                           start=(part == 0 and k == 0 and p == 0),
                                           stop=(part == 3 and k == 1 and p == 2))
                mm.then_inc(s_full, 1)

            def turn_keys(part):
                if part == 0:
                    pe.wait_ge(s_evac, SLOT_MEM + 8)
                else:
                    pe.wait_ge(s_xkc, part)
                for t in range(4):
                    for mt in range(2):
                        at_ = (t % 2) * 2 + mt
                        mm = pe.transpose(main[0][:, t // 2, at_ * P:(at_ + 1) * P],
                                          xk_tok[:, mt, (4 * part + t) * P:(4 * part + t + 1) * P], ident[:, :])
                mm.then_inc(s_xkt, 1)

            memory(0)
            pe.wait_ge(s_qk, 1)
            for c in range(NC):
                for j in range(2):
                    at_ = (c * 2 + j) * 2
                    mm = pe.matmul(ps[:, 7, at_:at_ + 2], lev[2][:, j, c * CH:(c + 1) * CH], sel[:, :],
                                   start=True, stop=True)
            mm.then_inc(s_qks, 1)
            memory(1)
            kd = lev[len(LEVELS) % 3]
            unit = 0
            for L in range(len(LEVELS)):
                if L < len(LEVELS) - 1:
                    memory(2 * L + 2)
                else:
                    memory(14)
                    memory(15)
                    pe.wait_ge(s_kd, 1)
                    for b in range(4):
                        if b == 2:
                            pe.wait_ge(s_evac, SLOT_MIX)
                        for c in range(2 * b, 2 * b + 2):
                            for j in range(2):
                                mm = pe.transpose(ps[:, kd_banks[b], ((c % 2) * 2 + j) * P:((c % 2) * 2 + j + 1) * P],
                                                  kd[:, j, c * CH:(c + 1) * CH], ident[:, :])
                        mm.then_inc(s_kt, 1)
                if L in (3, 4):
                    turn_keys(L - 3)
                pe.wait_ge(s_lt, L + 1)
                if L == 0:
                    pe.wait_ge(s_lc, 1)
                    pe.wait_ge(s_mstd, 1)
                src = lev[L % 3]
                for c in range(0, NC, 2):
                    if c == NC // 2 and L < len(LEVELS) - 1:
                        memory(2 * L + 3)
                    for odd in range(2):
                        if unit + odd >= 4:
                            pe.wait_ge(s_lc, unit + odd - 2)
                    for i in range(4):
                        cs = slice((c + i // 2) * CH, (c + i // 2 + 1) * CH)
                        for odd in range(2):
                            rows = slice(DK * odd, DK * odd + DK)
                            bank = 4 + (unit + odd) % 4
                            if L == 0:
                                to = slice(i * CH // 2, (i + 1) * CH // 2)
                                mm = pe.matmul(ps[0:CH // 2, bank, to], src[rows, i % 2, cs][:, 0:CH // 2],
                                               src[rows, i % 2, cs][:, CH // 2:], start=True, stop=True)
                            else:
                                mm = pe.matmul(ps[:, bank, i * P:(i + 1) * P], src[rows, i % 2, cs],
                                               src[rows, i % 2, cs], start=True, stop=True)
                            if i == 3:
                                mm.then_inc(s_lp, 1)
                    unit += 2
            for c in range(NC - 1):
                if c % 2 == 0:
                    pe.wait_ge(s_ktok, 4)
                for h in range(GLA_HEADS):
                    rows = slice(DK * (h % 2), DK * (h % 2) + DK)
                    at_ = (c % 2) * 2 + h // 2
                    mm = pe.matmul(ps[rows, c // 2, at_ * P:(at_ + 1) * P],
                                   kd_tok[:, c, h * DK:(h + 1) * DK], v_tok[:, c, h * P:(h + 1) * P],
                                   start=True, stop=True)
                if c % 2 or c == NC - 2:
                    mm.then_inc(s_delta, 1)
            pe.wait_ge(s_lc, 1 + unit)
            pe.wait_ge(s_qe, 2)
            n = SLOT_MIX
            lru_half, gla_half = range(4, 8), range(4)
            for c in range(NC + 2):
                if c < NC:
                    if c >= 1:
                        pe.wait_ge(s_st, c)
                    if c >= 2:
                        pe.wait_ge(s_on, c - 1)
                    out = ps[:, 4 + c % 2 * 2:6 + c % 2 * 2, :]
                    for h in range(GLA_HEADS):
                        rows, j = slice(DK * (h % 2), DK * (h % 2) + DK), h // 2
                        hs, js = slice(h * P, (h + 1) * P), slice(j * P, (j + 1) * P)
                        if c:
                            pe.matmul(out[:, h % 2, js], qe[rows, j, c * CH:(c + 1) * CH], states[rows, c, j, :],
                                      start=True, stop=False)
                        mm = pe.matmul(out[:, h % 2, js], sT[:, h % 2, c, j, :], v_tok[:, c, hs],
                                       start=(c == 0), stop=True)
                    mm.then_inc(s_o, 1)
                if c == 2:
                    pe.wait_ge(s_st, NC - 1)
                    pe.wait_ge(s_split, n + 1)
                    pe.wait_ge(s_ylo, LRU_TILES)
                if 2 <= c < 6:
                    step_of(n % RING, main[n % 2], lru_half[c - 2], b_hi, b_lo, c == 2, False)
                if c >= 2:
                    d = c - 2
                    pe.wait_ge(s_on, d + 1)
                    if d == 6:
                        ready(n + 1)
                        pe.wait_ge(s_oy, 6)
                        for k in lru_half[0:2]:
                            step_of((n + 1) % RING, main[(n + 1) % 2], k, b_hi, b_lo, k == 4, False)
                    if 2 <= d < 6:
                        pe.wait_ge(s_oy, d - 1)
                    for h in range(GLA_HEADS):
                        hs = slice(h * P, (h + 1) * P)
                        mm = pe.transpose(ps[:, turned_o_banks[d], hs], o_tok[d % 4][:, hs], ident[:, :])
                    mm.then_inc(s_ot, 1)

            order = list(lru_half) + list(gla_half)
            for k in lru_half[2:4]:
                step_of((n + 1) % RING, main[(n + 1) % 2], k, b_hi, b_lo, False, False)
            for i, halves, chunks in ((0, (0,), NC // 2), (0, (1,), NC), (1, (0, 1), NC)):
                pe.wait_ge(s_oylo, chunks)
                for k in gla_half:
                    mm = step_of((n + i) % RING, main[(n + i) % 2], k, b_hi, b_lo, False, k == 3, halves)
                if 1 in halves:
                    mm.then_inc(s_full, 1)
            with pe.Fori(1, KT // 2) as i:
                for j in range(2):
                    pe.wait_ge(s_split, i * 2 + (n + j + 1))
                    pe.wait_ge(s_evac, i * 2 + (n + j - 1))
                    project((n + j) % RING, main[(n + j) % 2], b_hi, b_lo, order=order).then_inc(s_full, 1)

            def after_norm(first, k, tiles):
                for n in range(first, first + 2):
                    ready(n)
                    before = tile_ready(k) if n == first else norm_within(k)
                    project(n % RING, main[n % 2], a_hi, a_lo, before=before).then_inc(s_full, 1)
                with pe.Fori(1, tiles // 2) as i:
                    for j in range(2):
                        pe.wait_ge(s_split, i * 2 + (first + j + 1))
                        pe.wait_ge(s_evac, i * 2 + (first + j - 1))
                        project((first + j) % RING, main[(first + j) % 2], a_hi, a_lo).then_inc(s_full, 1)
                if tiles % 2:
                    n = first + tiles - 1
                    ready(n)
                    project(n % RING, main[n % 2], a_hi, a_lo).then_inc(s_full, 1)

            UNITS = XHEADS * 4

            def scores(u):
                h, b = divmod(u, 4)
                if b == 0:
                    pe.wait_ge(s_kv, 2 if h else 1)
                    pe.wait_ge(s_xq, 2 * h + 2)
                if u == 2:
                    pe.wait_ge(s_evac, SLOT_XO - 1)
                if u >= 3:
                    pe.wait_ge(s_ex, 2 * (u - 2))
                khi, klo = (xk_hi, xk_lo) if h else (xk0_hi, xk0_lo)
                for i in range(2):
                    ts = slice((2 * b + i) * P, (2 * b + i + 1) * P)
                    for d in range(2):
                        t = 2 * h + d
                        for p, (q, k) in enumerate(((b_hi, khi), (b_hi, klo), (b_lo, khi))):
                            mm = pe.matmul(ps[:, score_banks[u % 3], i * N_MEM:(i + 1) * N_MEM], q[:, t, ts],
                                           k[:, t, :], start=(d == 0 and p == 0), stop=(d == 1 and p == 2))
                mm.then_inc(s_sc, 1)

            after_norm(SLOT_XQ, 1, KT - 1)
            scores(0)
            scores(1)
            n = SLOT_XO - 1
            ready(n)
            project(n % RING, main[n % 2], a_hi, a_lo).then_inc(s_full, 1)
            scores(2)

            def turn(u):
                pe.wait_ge(s_pn, u + 1)
                if u >= 3:
                    pe.wait_ge(s_ptl, u - 2)
                for m in range(2):
                    for i in range(2):
                        mm = pe.transpose(ps[:, turn_banks[u % 3], (2 * m + i) * P:(2 * m + i + 1) * P],
                                          pr[u % 4][:, i, m * P:(m + 1) * P], ident[:, :])
                mm.then_inc(s_pt, 1)

            def values(t):
                h = t // 2
                pe.wait_ge(s_vlo, 2)
                pe.wait_ge(s_ptl, 4 * h + 4)
                if t != KT - 2:
                    pe.wait_ge(s_evac, MAIN_ATT + min(t, KT - 2))
                for m in range(2):
                    ws = slice(t * P, (t + 1) * P)
                    for p, (w, q) in enumerate(((xv_hi, pT_hi[h % 2]), (xv_hi, pT_lo[h % 2]),
                                                (xv_lo, pT_hi[h % 2]))):
                        for b in range(2):
                            mm = pe.matmul(att_pair[t][:, b, :], w[:, m, ws],
                                           q[:, m, b * HALF:(b + 1) * HALF],
                                           start=(m == 0 and p == 0), stop=(m == 1 and p == 2))
                mm.then_inc(s_full, 1)

            for u in range(UNITS):
                turn(u)
                if u + 3 < UNITS:
                    scores(u + 3)
                if u > 4 and u % 2:
                    values((u - 5) // 2)
            values(KT - 2)
            values(KT - 1)

            n = SLOT_XO
            ready(n)
            project(n % RING, main[(n + KT) % 2], b_hi, b_lo,
                    before=lambda k: pe.wait_ge(s_evac, MAIN_ATT + k + 1)).then_inc(s_full, 1)
            ready(n + 1)
            project((n + 1) % RING, main[(n + 1) % 2], b_hi, b_lo).then_inc(s_full, 1)
            with pe.Fori(1, KT // 2) as i:
                for j in range(2):
                    pe.wait_ge(s_split, i * 2 + (n + j + 1))
                    pe.wait_ge(s_evac, i * 2 + (n + KT + j - 1))
                    project((n + j) % RING, main[(n + j) % 2], b_hi, b_lo).then_inc(s_full, 1)

            def out_part(ring, f, waits):
                for m in range(4):
                    if waits[m] is not None:
                        pe.wait_ge(s_oute, waits[m])
                    for k in range(GROUP):
                        ws = slice(k * HALF + m * P, k * HALF + (m + 1) * P)
                        for p, (w, q) in enumerate(((w_hi, f_hi[f]), (w_hi, f_lo[f]), (w_lo, f_hi[f]))):
                            for b in range(2):
                                mm = pe.matmul(aux[m % 2][:, b, :], w[:, ring, ws],
                                               q[:, k, b * HALF:(b + 1) * HALF],
                                               start=(k == 0 and p == 0), stop=(k == GROUP - 1 and p == 2))
                    mm.then_inc(s_out, 1)

            for q in range(4):
                n = SLOT_FFN + q
                pe.wait_ge(s_split, n + 1)
                pe.wait_ge(*((s_evac, MAIN_END - 1 + q) if q < 2 else (s_gue, q - 1)))
                before = (tile_ready(2), norm_within(2), None, None)[q]
                project(n % RING, main[(q + 1) % 2], a_hi, a_lo, before=before).then_inc(s_gu, 1)

            def group(g, f, first):
                start = SLOT_FFN - 2
                for part in range(2):
                    for q in range(2):
                        n = start + 3 * part + q
                        pe.wait_ge(s_split, g * 6 + (n + 1))
                        pe.wait_ge(s_gue, g * 4 + (2 * part + q - 1))
                        project(n % RING, main[1 - q], a_hi, a_lo).then_inc(s_gu, 1)
                    n = start + 3 * part + 2
                    pe.wait_ge(s_split, g * 6 + (n + 1))
                    if part == 0:
                        pe.wait_ge(s_fr, g * 2)
                    waits = [g * 8 + (4 * part + m - 9) for m in range(4)]
                    if first and part == 0:
                        waits[0:2] = [None, None]
                    out_part(n % RING, f, waits)

            def final_sums(half):
                if half == 0:
                    pe.wait_ge(s_gue, 4 * GROUPS)
                pe.wait_ge(s_facc, added((half + 1) * KT - 1))
                ssq(facc[:, half * HALF:(half + 1) * HALF], ps[:, half, :], NC // 2).then_inc(s_ssq, 1)

            def final_spread(half):
                pe.wait_ge(s_dg, 4 + half)
                spread(fdiag[:, half * 4:half * 4 + 4, :], ps[:, 2 + half:3 + half, :], NC // 2).then_inc(s_bc, 1)

            pe.wait_ge(s_rstd, 3)
            group(1, 0, True)
            assert GROUPS % 2 == 1
            group(2, 1, False)
            with pe.Fori(1, GROUPS // 2) as i:
                for j in range(2):
                    group(i * 2 + (1 + j), j, False)
            f = (GROUPS - 1) % 2
            pe.wait_ge(s_fr, 2 * GROUPS)
            for i, t, hs in pieces:
                if i in (0, 4):
                    pe.wait_ge(s_split, N_SLOTS - 1 + i // 4)
                if i < 4:
                    pe.wait_ge(s_oute, 8 * (GROUPS - 1) - 1 + i // 2)
                else:
                    pe.wait_ge(s_oute, 8 * (GROUPS - 1) + i - 3)
                for k in range(GROUP):
                    ring = (N_SLOTS - 2 + t // 4) % RING
                    ws = slice(k * HALF + t % 4 * P, k * HALF + (t % 4 + 1) * P)
                    for p, (w, q) in enumerate(((w_hi, f_hi[f]), (w_hi, f_lo[f]), (w_lo, f_hi[f]))):
                        mm = pe.matmul(ps[:, 4 + i % 4, :], w[:, ring, ws], q[:, k, hs],
                                       start=(k == 0 and p == 0), stop=(k == GROUP - 1 and p == 2))
                mm.then_inc(s_out, 1)
                if i == KT + 1:
                    final_sums(0)
                if i == KT + 5:
                    final_spread(0)
            final_sums(1)
            final_spread(1)

        @block.scalar
        def _(act):
            step = Steps(act, s_act)

            act.wait_ge(s_ones, 2)
            step(act.activation(table[:, :], eps[:, :], ACT.Square))
            act.wait_ge(s_par, 16)
            def h_tile(gain, xs, hi, acc_done, where):
                act.activation(hi, xs, ACT.Identity, scale=gain).then_inc(s_hhi, 1)
                if acc_done is not None:
                    act.wait_ge(s_acc, acc_done)
                act.activation(where, xs, ACT.Square).then_inc(s_sq, 1)

            for t in range(KT):
                act.wait_ge(s_x[t], 16)
                h_tile(col("g_mix", t), x[:, t, :], a_hi[:, t, :], t - 1 if t >= 2 else None,
                       flat(aux[t % 2]))

            def root(k):
                act.wait_ge(s_ssq, k + 1)
                act.activation(ssum[:, :], aux[0][:, 0, 0:NC], ACT.Sqrt, scale=1.0 / D,
                               bias=eps[:, 0:1]).then_inc(s_std, 1)

            root(0)
            step(act.activation(small[:, 0, :], par[:, PARAMS["lru_lambda"]:PARAMS["lru_lambda"] + 4], ACT.Abs))
            step.settle()
            act.activation(small[:, 1, :], small[:, 0, :], ACT.Exp, scale=-1.0).then_inc(s_sp, 1)

            def lru_tile(t):
                b = lru[t % 2]
                act.wait_ge(s_gate, t + 1)
                if t == 0:
                    act.wait_ge(s_spd, 1)
                if t >= 2:
                    act.wait_ge(s_ylo, t - 1)
                act.activation(b["ra"][:, :], flat(aux[0]), ACT.Sigmoid, bias=col("b_rg_a", t)).then_inc(s_sig, 1)
                act.activation(b["ix"][:, :], flat(aux[1]), ACT.Sigmoid, bias=col("b_rg_x", t)).then_inc(s_sig, 1)
                act.wait_ge(s_sig, 2 * t + 1)
                step(act.activation(b["ts"][:, :], b["ra"][:, :], ACT.Tanh, scale=small[:, 10, t:t + 1]))
                step(act.activation(b["ra"][:, :], b["ra"][:, :], ACT.Exp, scale=small[:, 11, t:t + 1]))
                step.settle()
                act.activation(b["ts"][:, :], b["ts"][:, :], ACT.Sqrt).then_inc(s_rec, 1)
                act.wait_ge(s_evac, 2 * t + 2)
                act.activation(b["gg"][:, :], b["gg"][:, :], ACT.Gelu_apprx_tanh).then_inc(s_gelu, 1)
                act.wait_ge(s_y, t + 1)
                act.activation(b_hi[:, 4 + t, :], b["gg"][:, :], ACT.Identity).then_inc(s_yhi, 1)

            for t in range(LRU_TILES):
                lru_tile(t)
            act.wait_ge(s_z, 1)
            act.dma_start(mem_raw[:, :, :], memT).then_inc(s_mem, 16)
            for j in range(2):
                step(act.activation(gk_a[:, j, :], flat(aux[j]), ACT.Abs, bias=col("b_gk", j)))
            step.settle()
            step(act.activation(gk_a[:, :, :], gk_a[:, :, :], ACT.Exp, scale=-1.0))
            step.settle()
            act.activation(gk_a[:, :, :], gk_a[:, :, :], ACT.Ln, bias=1.0).then_inc(s_lse, 1)
            for c in range(NC):
                act.wait_ge(s_vt, c + 1)
                act.activation(v_tok[:, c, :], ps[:, 4 + c % 4, :], ACT.Identity).then_inc(s_vtok, 1)
            act.wait_ge(s_mem, 16)
            act.wait_ge(s_vtok, NC)
            act.activation(ps[:, 4:8, :].rearrange("p b n -> p (b n)"),
                           mem_raw[:, :, :].rearrange("p k m -> p (k m)"), ACT.Square).then_inc(s_mq, 1)
            for k in range(KT):
                act.activation(m_hi[:, k, :], mem_raw[:, k, :], ACT.Identity,
                               scale=col("g_mem", k)).then_inc(s_mhi, 1)
            act.wait_ge(s_mssq, 1)
            act.activation(m_std[:, :], ps[:, 4, 0:2], ACT.Sqrt, scale=1.0 / D, bias=eps[:, 0:1])\
                .then_inc(s_mstd, 1)
            def output_gate(h):
                act.wait_ge(s_evac, SLOT_VO + 4 + h + 1)
                act.activation(og[:, h, :], og[:, h, :], ACT.Silu).then_inc(s_silu, 1)

            for h in range(3):
                output_gate(h)
            ends = bsum[:, :, :].rearrange("p j (c i) -> p j c i", i=CH)[:, :, :, CH - 1]
            act.activation(dec[:, :, :], ends, ACT.Exp, scale=1.0 / GATE_NORM).then_inc(s_dec, 1)
            for L in range(len(LEVELS) + 1):
                act.wait_ge(s_ld, L + 1)
                act.activation(lev[L % 3][:, :, :], lev[L % 3][:, :, :], ACT.Exp,
                               scale=1.0 / GATE_NORM).then_inc(s_le, 1)
                if L in (4, 5):
                    act.wait_ge(s_xkt, L - 3)
                    act.activation(xk_new[:, 4 * (L - 4):4 * (L - 3), :].rearrange("p t m -> p (t m)"),
                                   flat(main[0]), ACT.Identity).then_inc(s_xkc, 1)
                if L == 1:
                    act.activation(qe[:, :, :], bsum[:, :, :], ACT.Exp, scale=1.0 / GATE_NORM).then_inc(s_ke, 1)
            for b in range(4):
                act.wait_ge(s_kt, b + 1)
                act.activation(kd_tok[:, 2 * b:2 * b + 2, :],
                               ps[:, kd_banks[b], :].rearrange("p (c n) -> p c n", c=2), ACT.Identity)\
                    .then_inc(s_ktok, 1)
            act.wait_ge(s_evac, SLOT_MIX)
            act.activation(xk[:, :, :], xk_new[:, :, :], ACT.Identity).then_inc(s_kvc, 1)
            act.activation(xv[:, :, :], xv_new[:, :, :], ACT.Identity).then_inc(s_kvc, 1)
            output_gate(3)
            step(act.activation(table[:, :], eps[:, :], ACT.Sqrt))
            for c in range(NC + 3):
                if c < NC:
                    act.wait_ge(s_o, c + 1)
                    if c >= 2:
                        act.wait_ge(s_oc, 4 * (c - 1))
                    for h in range(GLA_HEADS):
                        act.activation(o_sq[c % 2][:, h * P:(h + 1) * P],
                                       ps[:, 4 + c % 2 * 2 + h % 2, h // 2 * P:(h // 2 + 1) * P], ACT.Square,
                                       accum_out=o_ss[:, c, h:h + 1]).then_inc(s_oc, 1)
                    act.wait_ge(s_oc, 4 * (c + 1))
                    act.activation(o_std[:, c, :], o_ss[:, c, :], ACT.Sqrt, scale=1.0 / P,
                                   bias=eps[:, 0:1]).then_inc(s_ostd, 1)
                if c >= 3:
                    act.wait_ge(s_oy, c - 2)
                    d = c - 3
                    act.activation(b_hi[:, 0:4, d * CH:(d + 1) * CH],
                                   o_y[d % 2][:, :].rearrange("p (h n) -> p h n", h=4), ACT.Identity)\
                        .then_inc(s_oyhi, 1)
            act.wait_ge(s_o, NC)
            act.wait_ge(s_oylo, NC)
            for t in range(KT):
                act.dma_start(x[:, t, :], xT[t, :, :]).then_inc(s_xr[t], 16)
            for t in range(KT):
                act.wait_ge(s_evac, SLOT_MIX + t + 1)
                h_tile(col("g_xattn", t), x[:, t, :], a_hi[:, t, :], KT + t - 1 if t >= 2 else None,
                       flat(aux[t % 2]))
            root(1)
            act.wait_ge(s_kvc, 2)
            act.activation(xk0_hi[:, :, :], xk[:, 0:2, :], ACT.Identity).then_inc(s_kvh, 1)
            with act.Fori(0, KT - 1) as t:
                act.wait_ge(s_evac, t + (SLOT_XQ + 1))
                act.activation(b_hi[:, bass.ds(t, 1), :].rearrange("p o n -> p (o n)"), tmp[:, :],
                               ACT.Identity).then_inc(s_xqh, 1)
            step(act.activation(table[:, :], eps[:, :], ACT.Exp))
            act.wait_ge(s_full, SLOT_XO)

            def exps(u):
                act.wait_ge(s_mx, u + 1)
                if u >= 4:
                    act.wait_ge(s_pt, u - 3)
                for i in range(2):
                    act.activation(pr[u % 4][:, i, :], ps[:, score_banks[u % 3], i * N_MEM:(i + 1) * N_MEM], ACT.Exp,
                                   bias=nmax[:, u, i:i + 1], accum_out=psum_p[:, u, i:i + 1]).then_inc(s_ex, 1)

            def turned(u):
                act.wait_ge(s_pt, u + 1)
                h, b = divmod(u, 4)
                if h >= 2:
                    act.wait_ge(s_full, MAIN_ATT + 2 * h - 2)
                act.activation(pT_hi[h % 2][:, :, b * 256:(b + 1) * 256],
                               ps[:, turn_banks[u % 3], :].rearrange("p (m n) -> p m n", m=2), ACT.Identity)\
                    .then_inc(s_pth, 1)

            def att(t):
                act.wait_ge(s_full, MAIN_ATT + t + 1)
                act.activation(b_hi[:, t, :], flat(att_pair[t]), ACT.Identity).then_inc(s_ath, 1)

            exps(0)
            act.activation(xk_hi[:, 2:, :], xk[:, 2:, :], ACT.Identity).then_inc(s_kvh, 1)
            exps(1)
            for u in range(4 * XHEADS):
                if u > 5 and u % 2 == 0:
                    att((u - 6) // 2)
                turned(u)
                if u + 2 < 4 * XHEADS:
                    exps(u + 2)
                if u == 0:
                    act.wait_ge(s_evac, SLOT_XO)
                    act.activation(b_hi[:, KT - 1, :], tmp[:, :], ACT.Identity).then_inc(s_xqh, 1)
                if u < 2:
                    act.activation(xv_hi[:, u, :], xv[:, u, :], ACT.Identity).then_inc(s_kvh, 1)
            for t in range(KT - 3, KT):
                att(t)
            for t in range(KT):
                act.wait_ge(s_evac, MAIN_XO + t + 1)
                h_tile(col("g_ffn", t), x[:, t, :], a_hi[:, t, :], 2 * KT + t - 1 if t >= 2 else None,
                       flat(aux[t % 2]))
            root(2)

            def ffn_tile(g, j, f):
                act.wait_ge(s_cv, g * 2 + (j + 1))
                act.activation(conv[:, :], conv[:, :], ACT.Silu).then_inc(s_sl, 1)
                act.wait_ge(s_f, g * 2 + (j + 1))
                act.activation(f_hi[f][:, j, :], up[:, :], ACT.Identity).then_inc(s_fh, 1)

            with act.Fori(0, GROUPS // 2) as i:
                for f in range(2):
                    for j in range(GROUP):
                        ffn_tile(i * 2 + f, j, f)
            for j in range(GROUP):
                ffn_tile(GROUPS - 1, j, (GROUPS - 1) % 2)
            def final_root(half):
                act.wait_ge(s_ssq, 4 + half)
                act.activation(ssum[:, half * 4:half * 4 + 4], ps[:, half, 0:4], ACT.Sqrt, scale=1.0 / D,
                               bias=eps[:, 0:1]).then_inc(s_std, 1)

            for i, t, hs in pieces:
                act.wait_ge(s_oute, 8 * (GROUPS - 1) + i + 1)
                if t >= 1 and i >= 4:
                    act.wait_ge(s_facc, added(i - 4))
                out = fsq[:, i % 4, :] if t else facc[:, hs]
                act.activation(out, x[:, t, hs], ACT.Square).then_inc(s_fsq, 1)
                act.wait_ge(s_fsq, i + 1)
                act.activation(x[:, t, hs], x[:, t, hs], ACT.Identity, scale=col("g_final", t)).then_inc(s_xg, 1)
                if i == KT + 1:
                    final_root(0)
            final_root(1)
            done = 0
            for i, t, hs in pieces:
                if t >= by_pool[i // KT]:
                    done += 1
                    act.wait_ge(s_yf, done)
                    act.dma_start(yT[t, :, hs], x[:, t, hs]).then_inc(s_store, 16)

        @block.vector
        def _(dve):
            step = Steps(dve, s_dve)
            def h_rest(gain, xs, hi, lo, hhi, sq, where, into, first):
                dve.wait_ge(s_hhi, hhi)
                dve.scalar_tensor_tensor(lo, xs, gain, hi.bitcast(F32), ALU.mult, ALU.subtract).then_inc(s_h, 1)
                dve.wait_ge(s_sq, sq)
                if first:
                    dve.tensor_copy(into, where).then_inc(s_acc, 1)
                else:
                    dve.wait_ge(s_acc, sq - 1)
                    dve.tensor_tensor(into, where, into, ALU.add).then_inc(s_acc, 1)

            for t in range(KT):
                dve.wait_ge(s_x[t], 16)
                h_rest(col("g_mix", t), x[:, t, :], a_hi[:, t, :], a_lo[:, t, :], t + 1, t + 1,
                       flat(aux[t % 2]), acc[:, :], t == 0)

            def diagonal(k, out):
                dve.wait_ge(s_std, k + 1)
                step(dve.reciprocal(srec[:, :], ssum[:, :]))
                step.settle()
                dve.wait_ge(s_cst, 2)
                dve.tensor_tensor(out, ident[:, :].unsqueeze(1).to_broadcast([P, NC, P]),
                                  srec[:, :].unsqueeze(2).to_broadcast([P, NC, P]), ALU.mult).then_inc(s_dg, 1)

            def rstd_ready(k):
                dve.wait_ge(s_bc, k + 1)
                dve.tensor_copy(rstd[:, :], flat(aux[1])).then_inc(s_rstd, 1)
                dve.wait_ge(s_rstd, k + 1)

            diagonal(0, diag[:, :, :])
            rstd_ready(0)

            def scaled(out, u):
                dve.wait_ge(s_full, u + 1)
                dve.tensor_tensor(out, flat(main[u % 2]), rstd[:, :], ALU.mult).then_inc(s_evac, 1)

            def branch(t):
                b = lru[t % 2]
                scaled(b["xr"][:, :], 2 * t)
                dve.wait_ge(s_evac, 2 * t + 1)
                tap = [col("conv_lru_w", 4 * t + n) for n in range(4)]
                step(dve.tensor_scalar(b["xc"][:, :], b["xr"][:, :], tap[3], col("conv_lru_b", t),
                                       ALU.mult, ALU.add))
                for back in (1, 2, 3):
                    step.settle()
                    ins = dve.scalar_tensor_tensor(b["xc"][:, back:], b["xr"][:, 0:S - back], tap[3 - back],
                                                   b["xc"][:, back:], ALU.mult, ALU.add)
                    if back < 3:
                        step(ins)
                    else:
                        ins.then_inc(s_xc, 1)

            def recurrence(t):
                b = lru[t % 2]
                dve.wait_ge(s_rec, t + 1)
                step(dve.scalar_tensor_tensor(b["ts"][:, :], b["ra"][:, :], 1.0, b["ts"][:, :],
                                              ALU.add, ALU.mult))
                step(dve.tensor_tensor(b["ix"][:, :], b["ix"][:, :], b["xc"][:, :], ALU.mult))
                step.settle()
                step(dve.memset(b["ts"][:, 0:1], 1.0))
                step.settle()
                step(dve.tensor_tensor(b["ts"][:, :], b["ts"][:, :], b["ix"][:, :], ALU.mult))
                step.settle()
                step(dve.tensor_tensor_scan(b["xr"][:, :], b["ra"][:, :], b["ts"][:, :], 0.0,
                                            ALU.mult, ALU.add))
                step.settle()
                dve.wait_ge(s_gelu, t + 1)
                dve.tensor_tensor(b["gg"][:, :], b["gg"][:, :], b["xr"][:, :], ALU.mult).then_inc(s_y, 1)
                dve.wait_ge(s_yhi, t + 1)
                dve.wait_ge(s_y, t + 1)
                dve.tensor_tensor(b_lo[:, 4 + t, :], b["gg"][:, :], b_hi[:, 4 + t, :].bitcast(F32),
                                  ALU.subtract).then_inc(s_ylo, 1)

            def gelu_in(t):
                scaled(lru[t % 2]["gg"][:, :], 2 * t + 1)

            branch(0)
            gelu_in(0)
            sm = [small[:, n, :] for n in range(12)]
            dve.wait_ge(s_sp, 1)
            step(dve.tensor_scalar(sm[2], sm[1], 2.0, None, ALU.add))
            step.settle()
            step(dve.reciprocal(sm[3], sm[2]))
            step.settle()
            step(dve.tensor_tensor(sm[4], sm[1], sm[3], ALU.mult))
            step.settle()
            step(dve.tensor_tensor(sm[5], sm[4], sm[4], ALU.mult))
            step.settle()
            step(dve.tensor_scalar(sm[6], sm[5], 1.0 / 17, 1.0 / 15, ALU.mult, ALU.add))
            for d in (13, 11, 9, 7, 5, 3, 1):
                step.settle()
                step(dve.tensor_tensor(sm[6], sm[6], sm[5], ALU.mult))
                step.settle()
                step(dve.tensor_scalar(sm[6], sm[6], 1.0 / d, None, ALU.add))
            step(dve.tensor_scalar(sm[7], par[:, PARAMS["lru_lambda"]:PARAMS["lru_lambda"] + 4], -1.0, 0.0,
                                   ALU.mult, ALU.max))
            step.settle()
            step(dve.scalar_tensor_tensor(sm[8], sm[4], 2.0, sm[6], ALU.mult, ALU.mult))
            step.settle()
            step(dve.tensor_tensor(sm[9], sm[8], sm[7], ALU.add))
            step.settle()
            step(dve.tensor_scalar(sm[10], sm[9], 4.0, None, ALU.mult))
            step.settle()
            dve.tensor_scalar(sm[11], sm[9], -8.0, None, ALU.mult).then_inc(s_spd, 1)

            for t in range(LRU_TILES):
                if t + 1 < LRU_TILES:
                    branch(t + 1)
                else:
                    dve.wait_ge(s_full, SLOT_GK + 1)
                    dve.tensor_tensor(gk_lr[:, :], flat(main[SLOT_GK % 2])[0:GK_ROWS, :],
                                      rstd[0:GK_ROWS, :], ALU.mult).then_inc(s_evac, 1)
                recurrence(t)
                if t + 1 < LRU_TILES:
                    gelu_in(t + 1)
            for j in range(2):
                scaled(kk[:, j, :], SLOT_KQ + j)
                if j == 0:
                    dve.wait_ge(s_lse, 1)
                    for i in range(2):
                        step(dve.tensor_scalar(gk_b[:, i, :], flat(aux[i]), col("b_gk", i), 0.0,
                                               ALU.add, ALU.min))
                    step.settle()
                    step(dve.tensor_tensor(gk_b[:, :, :], gk_b[:, :, :], gk_a[:, :, :], ALU.subtract))
                    step.settle()
                    for i in range(2):
                        for c in range(NC):
                            cs = slice(c * CH, (c + 1) * CH)
                            dve.tensor_tensor_scan(bsum[:, i, cs], ones[:, :], gk_b[:, i, cs], 0.0,
                                                   ALU.mult, ALU.add).then_inc(s_b, 1)
            for j in range(2):
                u = SLOT_KQ + 2 + j
                dve.wait_ge(s_full, u + 1)
                dve.scalar_tensor_tensor(qq[:, j, :], flat(main[u % 2]), DK ** -0.5, rstd[:, :],
                                         ALU.mult, ALU.mult).then_inc(s_evac, 1)
            for h in range(4):
                scaled(v_feat[:, h, :], SLOT_VO + h)
            dve.wait_ge(s_mq, 1)
            dve.wait_ge(s_cst, 6 + 2 * (len(LEVELS) - 1))
            dve.tensor_reduce(m_acc[:, :], ps[:, 4:8, :].rearrange("p b (k m) -> p m (b k)", m=N_MEM),
                              AX.X, ALU.add).then_inc(s_msq, 1)
            scaled(og[:, 0, :], SLOT_VO + 4)
            for k in range(KT):
                dve.wait_ge(s_mhi, k + 1)
                ins = dve.scalar_tensor_tensor(m_lo[:, k, :], mem_raw[:, k, :], col("g_mem", k),
                                               m_hi[:, k, :].bitcast(F32), ALU.mult, ALU.subtract)
                if k < KT - 1:
                    step(ins)
            ins.then_inc(s_mh, 1)
            scaled(og[:, 1, :], SLOT_VO + 5)
            step.settle()
            dve.wait_ge(s_mh, 1)
            dve.tensor_tensor(lev[2][:, :, :], qq[:, :, :], kk[:, :, :], ALU.mult).then_inc(s_qk, 1)
            dve.wait_ge(s_mstd, 1)
            step(dve.reciprocal(m_rec[:, :], m_std[:, :]))
            step.settle()
            scaled(og[:, 2, :], SLOT_VO + 6)

            def level(L):
                m = LEVELS[L]
                buf = lev[L % 3]
                sv, bv = (t[:, :, :].rearrange("p j (n h m) -> p (j n) h m", h=2, m=m) for t in (buf, bsum))
                n = 2 * S // (2 * m)
                ref = bv[:, :, 0, m - 1:m].to_broadcast([P, n, m])
                step(dve.tensor_tensor(sv[:, :, 0, :], ref, bv[:, :, 0, :], ALU.subtract))
                dve.tensor_tensor(sv[:, :, 1, :], bv[:, :, 1, :], ref, ALU.subtract).then_inc(s_ld, 1)

            def level_product(L):
                m = LEVELS[L]
                sv, kv, qv = (t[:, :, :].rearrange("p j (n h m) -> p (j n) h m", h=2, m=m)
                              for t in (lev[L % 3], kk, qq))
                dve.wait_ge(s_le, L + 1)
                step(dve.tensor_tensor(sv[:, :, 0, :], sv[:, :, 0, :], kv[:, :, 0, :], ALU.mult))
                step.settle()
                dve.tensor_tensor(sv[:, :, 1, :], sv[:, :, 1, :], qv[:, :, 1, :], ALU.mult).then_inc(s_lt, 1)

            dve.wait_ge(s_b, 2 * NC)
            dve.wait_ge(s_full, SLOT_VO + 8)
            level(0)
            level(1)
            level_product(0)
            scaled(og[:, 3, :], SLOT_VO + 7)

            def memory(half):
                dve.wait_ge(s_full, SLOT_MEM + 4 * half + 4)
                out = (xk_tok, xv_new)[half // 2][:, :, (half % 2) * HALF:(half % 2 + 1) * HALF]
                dve.tensor_tensor(out, main[(half + 1) % 2], m_rec[:, :].unsqueeze(2).to_broadcast([P, 2, HALF]),
                                  ALU.mult).then_inc(s_evac, 4)

            dve.wait_ge(s_qks, 1)
            got = ps[:, 7, 0:4 * NC].rearrange("p (n o) -> p o n", o=2)
            for odd in range(2):
                ins = dve.tensor_tensor(sT[:, odd, :, :, :].rearrange("p c j n -> p (c j) n"),
                                        ident[:, :].unsqueeze(1).to_broadcast([P, 2 * NC, P]),
                                        got[:, odd, :].unsqueeze(2).to_broadcast([P, 2 * NC, P]), ALU.mult)
                if odd == 0:
                    step(ins)
            ins.then_inc(s_lc, 1)
            step.settle()
            kd = lev[len(LEVELS) % 3]
            unit = 0
            for L in range(len(LEVELS)):
                m = LEVELS[L]
                if L + 1 < len(LEVELS):
                    level_product(L + 1)
                else:
                    dve.wait_ge(s_le, L + 2)
                    dve.wait_ge(s_ld, L + 2)
                    dve.tensor_tensor(kd[:, :, :], kd[:, :, :], kk[:, :, :], ALU.mult).then_inc(s_kd, 1)
                if L == len(LEVELS) - 1:
                    memory(3)
                for c in range(0, NC, 2):
                    for odd in range(2):
                        dve.wait_ge(s_lp, unit + 1)
                        dve.wait_ge(s_lc, max(1, unit - 6))
                        bank = ps[:, 4 + unit % 4, :]
                        kept = sT[:, odd, c:c + 2, :, :].rearrange("p c j (n h m) -> p (c j) n h m", h=2, m=m)
                        if L == 0:
                            ins = dve.tensor_copy(kept[0:CH // 2, :, 0, 1, :],
                                                  bank[0:CH // 2, 0:2 * CH].rearrange("p (i n) -> p i n", i=4))
                        else:
                            got = bank.rearrange("p (i n h m) -> p i n h m", i=4, h=2, m=m)
                            mask = masks[:, L - 1, :].bitcast(U32).rearrange("p (n m) -> p n m", m=m)
                            mask = mask.unsqueeze(1).to_broadcast([P, 4, CH // (2 * m), m])
                            ins = dve.copy_predicated(kept[:, :, :, 1, :], mask, got[:, :, :, 1, :])
                        ins.then_inc(s_lc, 1)
                        unit += 1
                    if c == 2 and L % 2 == 0 and L < len(LEVELS) - 1:
                        memory(L // 2)
                    if c == 0 and L + 2 < len(LEVELS):
                        if L:
                            dve.wait_ge(s_lp, 8 * L)
                        level(L + 2)
                    if c == 0 and L + 2 == len(LEVELS):
                        bv, kdv = (t[:, :, :].rearrange("p j (c i) -> p (j c) i", i=CH) for t in (bsum, kd))
                        dve.tensor_tensor(kdv, bv[:, :, CH - 1:CH].to_broadcast([P, 2 * NC, CH]), bv,
                                          ALU.subtract).then_inc(s_ld, 1)
                    if c == 2 and L in (3, 5):
                        j = (L - 3) // 2
                        if j == 0:
                            dve.wait_ge(s_ke, 1)
                        dve.tensor_tensor(qe[:, j, :], qe[:, j, :], qq[:, j, :], ALU.mult).then_inc(s_qe, 1)
            dve.wait_ge(s_dec, 1)
            for c in range(NC - 1):
                dve.wait_ge(s_delta, c // 2 + 1)
                got = ps[:, c // 2, (c % 2) * 256:(c % 2) * 256 + 256].rearrange("p (j n) -> p j n", j=2)
                if c == 0:
                    dve.tensor_copy(states[:, 1, :, :], got).then_inc(s_st, 1)
                    continue
                dve.wait_ge(s_st, c)
                step(dve.scalar_tensor_tensor(states[:, c + 1, 0, :], states[:, c, 0, :], dec[:, 0, c:c + 1],
                                              got[:, 0, :], ALU.mult, ALU.add))
                dve.scalar_tensor_tensor(states[:, c + 1, 1, :], states[:, c, 1, :], dec[:, 1, c:c + 1],
                                         got[:, 1, :], ALU.mult, ALU.add).then_inc(s_st, 1)
            for c in range(NC + 3):
                if 2 <= c < NC + 2:
                    d = c - 2
                    dve.wait_ge(s_ot, d + 1)
                    if d == 0:
                        dve.wait_ge(s_silu, 4)
                    if d >= 2:
                        dve.wait_ge(s_oylo, d - 1)
                    dve.scalar_tensor_tensor(o_y[d % 2][:, :].rearrange("p (h n) -> p h n", h=4),
                                             ps[:, turned_o_banks[d], :].rearrange("p (h n) -> p h n", h=4),
                                             col("g_head"), og[:, :, d * CH:(d + 1) * CH], ALU.mult, ALU.mult).then_inc(s_oy, 1)
                if c < NC:
                    dve.wait_ge(s_ostd, c + 1)
                    step(dve.reciprocal(o_rec[:, c, :], o_std[:, c, :]))
                    step.settle()
                    if c >= 4:
                        dve.wait_ge(s_ot, c - 3)
                    out = ps[:, 4 + c % 2 * 2:6 + c % 2 * 2, 0:256].rearrange("p o (j n) -> p o j n", j=2)
                    rec = o_rec[:, c, :].rearrange("p (j o) -> p o j", o=2).unsqueeze(3)
                    dve.tensor_tensor(o_tok[c % 4][:, :].rearrange("p (j o n) -> p o j n", j=2, o=2), out,
                                      rec.to_broadcast([P, 2, 2, P]), ALU.mult).then_inc(s_on, 1)
                if c >= 3:
                    d = c - 3
                    dve.wait_ge(s_oyhi, d + 1)
                    cs = slice(d * CH, (d + 1) * CH)
                    dve.tensor_tensor(b_lo[:, 0:4, cs], o_y[d % 2][:, :].rearrange("p (h n) -> p h n", h=4),
                                      b_hi[:, 0:4, cs].bitcast(F32), ALU.subtract).then_inc(s_oylo, 1)

            def residual(t, u, gain, k):
                dve.wait_ge(s_full, u + 1)
                dve.tensor_tensor(x[:, t, :], flat(main[u % 2]), x[:, t, :], ALU.add).then_inc(s_evac, 1)
                h_rest(col(gain, t), x[:, t, :], a_hi[:, t, :], a_lo[:, t, :], KT * k + t + 1,
                       KT * k + t + 1, flat(aux[t % 2]), acc[:, :], t == 0)

            for t in range(KT):
                dve.wait_ge(s_xr[t], 16)
                residual(t, SLOT_MIX + t, "g_xattn", 1)
            diagonal(1, diag[:, :, :])
            rstd_ready(1)
            def query_scaled(i, j):
                u = SLOT_XQ + j
                dve.wait_ge(s_full, i * 2 + (u + 1))
                if not isinstance(i, int) or i + j:
                    dve.wait_ge(s_xq, i * 2 + j)
                dve.scalar_tensor_tensor(tmp[:, :], flat(main[u % 2]), XHEAD_DIM ** -0.5, rstd[:, :],
                                         ALU.mult, ALU.mult).then_inc(s_evac, 1)

            def query_rest(i, j):
                dve.wait_ge(s_xqh, i * 2 + (j + 1))
                dve.wait_ge(s_evac, i * 2 + (SLOT_XQ + j + 1))
                hi, lo = (z[:, bass.ds(i * 2 + j, 1), :].rearrange("p o n -> p (o n)")
                          for z in (b_hi, b_lo))
                dve.tensor_tensor(lo, tmp[:, :], hi.bitcast(F32), ALU.subtract).then_inc(s_xq, 1)

            def query(i, j):
                query_scaled(i, j)
                query_rest(i, j)

            query(0, 0)
            query(0, 1)
            dve.wait_ge(s_kvh, 1)
            dve.tensor_tensor(xk0_lo[:, :, :], xk[:, 0:2, :], xk0_hi[:, :, :].bitcast(F32), ALU.subtract)\
                .then_inc(s_kv, 1)
            with dve.Fori(1, KT // 2 - 1) as i:
                query(i, 0)
                query(i, 1)
            query(KT // 2 - 1, 0)

            def maxima(u):
                dve.wait_ge(s_sc, u + 1)
                dve.tensor_reduce(nmax[:, u, :], ps[:, score_banks[u % 3], :].rearrange("p (i m) -> p i m", i=2),
                                  AX.X, ALU.max, negate=True).then_inc(s_mx, 1)

            def normalise(u):
                dve.wait_ge(s_ex, 2 * u + 2)
                step(dve.reciprocal(prec[:, u, :], psum_p[:, u, :]))
                step.settle()
                dve.tensor_tensor(pr[u % 4][:, :, :], pr[u % 4][:, :, :],
                                  prec[:, u, :].unsqueeze(2).to_broadcast([P, 2, N_MEM]), ALU.mult)\
                    .then_inc(s_pn, 1)

            def turned_rest(u):
                if u == 4:
                    dve.wait_ge(s_vlo, 2)
                dve.wait_ge(s_pth, u + 1)
                h, b = divmod(u, 4)
                ts = slice(b * 256, (b + 1) * 256)
                dve.tensor_tensor(pT_lo[h % 2][:, :, ts],
                                  ps[:, turn_banks[u % 3], :].rearrange("p (m n) -> p m n", m=2),
                                  pT_hi[h % 2][:, :, ts].bitcast(F32), ALU.subtract).then_inc(s_ptl, 1)

            def att_rest(t):
                dve.wait_ge(s_ath, t + 1)
                dve.tensor_tensor(b_lo[:, t, :], flat(att_pair[t]), b_hi[:, t, :].bitcast(F32),
                                  ALU.subtract).then_inc(s_evac, 1)

            units = 4 * XHEADS
            maxima(0)
            maxima(1)
            query_scaled(KT // 2 - 1, 1)
            normalise(0)
            maxima(2)
            dve.wait_ge(s_kvh, 2)
            dve.tensor_tensor(xk_lo[:, 2:, :], xk[:, 2:, :], xk_hi[:, 2:, :].bitcast(F32), ALU.subtract)\
                .then_inc(s_kv, 1)
            for u in range(units):
                if u + 1 < units:
                    normalise(u + 1)
                if u > 5 and u % 2 == 0:
                    att_rest((u - 6) // 2)
                turned_rest(u)
                if u + 3 < units:
                    maxima(u + 3)
                if u == 1:
                    query_rest(KT // 2 - 1, 1)
            for t in range(KT - 3, KT):
                att_rest(t)
            for t in range(KT):
                residual(t, MAIN_XO + t, "g_ffn", 2)
            diagonal(2, diag[:, :, :])
            rstd_ready(2)

            def ffn_tile(g, j, f, n):
                dve.wait_ge(s_gu, g * 4 + (2 * j + 1))
                dve.tensor_tensor(gate[:, :], flat(main[1]), rstd[:, :], ALU.mult).then_inc(s_gue, 1)
                dve.wait_ge(s_gue, g * 4 + (2 * j + 1))
                tap = [par[:, bass.ds(g * 6 + (3 * j + k + PARAMS["conv_ffn_w"]), 1)] for k in range(3)]
                bias = par[:, bass.ds(g * 2 + (j + PARAMS["conv_ffn_b"]), 1)]
                dve.tensor_scalar(conv[:, :], gate[:, :], tap[2], bias, ALU.mult, ALU.add).then_inc(s_dve, 1)
                dve.wait_ge(s_dve, n + 1)
                dve.scalar_tensor_tensor(conv[:, 1:], gate[:, 0:S - 1], tap[1], conv[:, 1:], ALU.mult,
                                         ALU.add).then_inc(s_dve, 1)
                dve.wait_ge(s_dve, n + 2)
                dve.scalar_tensor_tensor(conv[:, 2:], gate[:, 0:S - 2], tap[0], conv[:, 2:], ALU.mult,
                                         ALU.add).then_inc(s_cv, 1)
                dve.wait_ge(s_gu, g * 4 + (2 * j + 2))
                dve.tensor_tensor(up[:, :], flat(main[0]), rstd[:, :], ALU.mult).then_inc(s_gue, 1)
                dve.wait_ge(s_gue, g * 4 + (2 * j + 2))
                dve.wait_ge(s_sl, g * 2 + (j + 1))
                dve.tensor_tensor(up[:, :], up[:, :], conv[:, :], ALU.mult).then_inc(s_f, 1)

            def ffn_rest(g, j, f):
                dve.wait_ge(s_fh, g * 2 + (j + 1))
                dve.tensor_tensor(f_lo[f][:, j, :], up[:, :], f_hi[f][:, j, :].bitcast(F32),
                                  ALU.subtract).then_inc(s_fr, 1)

            def add_out(g, t):
                dve.wait_ge(s_out, g * 8 + (t - 7))
                dve.tensor_tensor(x[:, t, :], flat(aux[t % 2]), x[:, t, :], ALU.add).then_inc(s_oute, 1)

            per_group = 4

            def group(g, f, n0):
                for j in range(2):
                    ffn_tile(g, j, f, n0 + 2 * j)
                    add_out(g, 4 * j)
                    ffn_rest(g, j, f)
                    for t in range(4 * j + 1, 4 * j + 4):
                        add_out(g, t)

            before = step.n
            for j in range(GROUP):
                ffn_tile(0, j, 0, before + 2 * j)
                ffn_rest(0, j, 0)
            group(1, 1, before + per_group)
            group(2, 0, before + 2 * per_group)
            with dve.Fori(1, GROUPS // 2) as i:
                for j in range(2):
                    group(i * 2 + (1 + j), (1 + j) % 2, i * (2 * per_group) + (before + (1 + j) * per_group))
            step.n = before + GROUPS * per_group

            def add_piece(i, t, hs):
                dve.wait_ge(s_out, 8 * (GROUPS - 1) + i + 1)
                dve.tensor_tensor(x[:, t, hs], ps[:, 4 + i % 4, :], x[:, t, hs], ALU.add).then_inc(s_oute, 1)

            def add_squares(i, t, hs):
                dve.wait_ge(s_fsq, i + 1)
                if t >= 2:
                    dve.wait_ge(s_facc, added(i - 1))
                dve.tensor_tensor(facc[:, hs], fsq[:, i % 4, :], facc[:, hs], ALU.add).then_inc(s_facc, 1)

            def final_diagonal(half):
                part = slice(half * 4, half * 4 + 4)
                dve.wait_ge(s_std, 4 + half)
                step(dve.reciprocal(srec[:, part], ssum[:, part]))
                step.settle()
                dve.tensor_tensor(fdiag[:, part, :], ident[:, :].unsqueeze(1).to_broadcast([P, 4, P]),
                                  srec[:, part].unsqueeze(2).to_broadcast([P, 4, P]), ALU.mult).then_inc(s_dg, 1)

            def final_rstd(half):
                dve.wait_ge(s_bc, 4 + half)
                dve.tensor_copy(frs[:, half * HALF:(half + 1) * HALF], ps[:, 2 + half, :]).then_inc(s_rstd, 1)

            def final_scale(half, tiles):
                dve.wait_ge(s_rstd, 4 + half)
                hs = slice(half * HALF, (half + 1) * HALF)
                for t in tiles:
                    dve.wait_ge(s_xg, half * KT + t + 1)
                    dve.tensor_tensor(x[:, t, hs], x[:, t, hs], frs[:, hs], ALU.mult).then_inc(s_yf, 1)

            for i, t, hs in pieces:
                add_piece(i, t, hs)
                if i and (i - 1) % KT:
                    add_squares(*pieces[i - 1])
                if i == KT + 4:
                    final_diagonal(0)
                if i == KT + 7:
                    final_rstd(0)
            add_squares(*pieces[-1])
            own = [list(range(by_pool[half], KT)) for half in range(2)]
            final_scale(0, own[0][:2])
            final_diagonal(1)
            final_scale(0, own[0][2:])
            final_rstd(1)
            final_scale(1, own[1])


def kernel(x, mem, g_mix, w_in, w_gk, b_gk, g_gla_head, conv_lru_w, conv_lru_b, w_rg_a, b_rg_a, w_rg_x,
           b_rg_x, lru_lambda, w_mix_out, g_xattn, g_mem, w_xq, w_xkv, w_xo, g_ffn, w_ffn_in, conv_ffn_w,
           conv_ffn_b, w_ffn_out, g_final):
    import numpy as np
    import concourse.bacc as bacc
    from concourse.bass_utils import run_bass_kernel_spmd as run

    def slots(w):
        w = np.asarray(w)
        n = w.shape[1] // P
        return w.reshape(KT, P, n, P).transpose(2, 1, 0, 3).reshape(n, P, KT * P)

    def cols(v):
        v = np.asarray(v)
        return v.reshape(-1, P).T if v.ndim == 1 else v.reshape(v.shape[0], -1, P).transpose(2, 1, 0).reshape(P, -1)

    w = np.asarray(w_in)[0]
    at = np.cumsum([0, 256, 256, 512, 512, GLA_LOWRANK, 512, 512])
    q, k, v, og, gk, xr, xg = (w[:, at[n]:at[n + 1]] for n in range(7))
    gk_pad = np.zeros((D, P), w.dtype)
    gk_pad[:, :GLA_LOWRANK] = gk_pad[:, GK_REST:GK_ROWS] = gk
    lru = np.stack([slots(xr), slots(xg)], 1).reshape(2 * LRU_TILES, P, D)
    ffn_in = slots(np.asarray(w_ffn_in)[0])
    out = np.asarray(w_ffn_out)[0].reshape(GROUPS, GROUP, P, 2, HALF).transpose(0, 3, 2, 1, 4)
    out = out.reshape(GROUPS, 2, P, GROUP * HALF)
    ffn = [ffn_in[0], ffn_in[FF_TILES], ffn_in[1], ffn_in[FF_TILES + 1]]
    for g in range(1, GROUPS):
        for half in range(2):
            t = GROUP * g + half
            ffn += [ffn_in[t], ffn_in[FF_TILES + t], out[g - 1, half]]
    ffn += [out[GROUPS - 1, 0], out[GROUPS - 1, 1]]
    xkv = np.asarray(w_xkv)[0].reshape(4, 2, P, 4, HALF).transpose(3, 0, 2, 1, 4).reshape(16, P, D)
    stream = np.concatenate([lru, slots(gk_pad), slots(k), slots(q), slots(v), slots(og),
                             xkv, slots(np.asarray(w_mix_out)[0]),
                             slots(np.asarray(w_xq)[0]), slots(np.asarray(w_xo)[0]), np.stack(ffn)])
    blocks = {"g_mix": g_mix, "g_xattn": g_xattn, "g_mem": g_mem, "g_ffn": g_ffn, "g_final": [g_final],
              "b_gk": b_gk, "g_head": g_gla_head, "conv_lru_w": conv_lru_w, "conv_lru_b": conv_lru_b,
              "b_rg_a": b_rg_a, "b_rg_x": b_rg_x, "lru_lambda": lru_lambda, "conv_ffn_w": conv_ffn_w,
              "conv_ffn_b": conv_ffn_b}
    params = np.concatenate([cols(np.asarray(blocks[n][0])) for n in PARAMS], 1)
    arrays = {
        "xT": np.asarray(x)[0].T.reshape(KT, P, S),
        "memT": np.asarray(mem)[0].T.reshape(KT, P, N_MEM).transpose(1, 0, 2),
        "wstream": stream,
        "params": params,
        "w_gk": np.asarray(w_gk)[0],
        "w_rg_a": np.asarray(w_rg_a)[0].reshape(LRU_TILES, 2, LRU_BLOCK, LRU_BLOCK).transpose(1, 2, 0, 3),
        "w_rg_x": np.asarray(w_rg_x)[0].reshape(LRU_TILES, 2, LRU_BLOCK, LRU_BLOCK).transpose(1, 2, 0, 3),
    }
    arrays = {n: np.ascontiguousarray(a) for n, a in arrays.items()}
    nc = bacc.Bacc("TRN2", target_bir_lowering=False, num_devices=1, dynamic_dma_scratch_size=1024)
    ins = [nc.dram_tensor(n, a.shape, mybir.dt.from_np(a.dtype), kind="ExternalInput").ap()
           for n, a in arrays.items()]
    yT = nc.dram_tensor("yT", (KT, P, S), F32, kind="ExternalOutput").ap()
    build(nc, *ins, yT)
    got = run(nc, [arrays], core_ids=[0]).results[0]["yT"]
    return np.ascontiguousarray(got.reshape(D, S).T)[None]
```
